# Optimizing a Trainium2 kernel written in Bass

```python
import math
import jax, jax.numpy as jnp
from jax import lax
import numpy as np

D_MODEL = 1024
BATCH = 1
SEQ = 1024
DEPTH = 1

M_HEADS = 4
M_HEAD_DIM = 128
M_WIDTH = M_HEADS * M_HEAD_DIM
M_CONV = 4
M_CHUNK = 64
A_HEADS = 8
A_NOPE = 64
A_ROPE = 32
A_V = 64
A_QK = A_NOPE + A_ROPE
A_Q_RANK = 256
A_KV_RANK = 128
A_WIDTH = A_HEADS * A_V
ROPE_THETA = 10000.0
Q_BLOCK = 128
D_FF = ((8 * D_MODEL + 3 * 256 - 1) // (3 * 256)) * 256
NORM_EPS = 1e-6
IN_SIZES = (M_WIDTH, M_WIDTH, M_WIDTH, M_WIDTH, M_HEADS, M_HEADS,
            A_Q_RANK, A_KV_RANK, A_ROPE, D_MODEL, D_MODEL)
D_IN = sum(IN_SIZES)

kernel_name = "hybrid_mlstm_mla_gated_block"

def rmsnorm(x, g):
    xf = x.astype(jnp.float32)
    y = xf * lax.rsqrt(jnp.mean(xf * xf, axis=-1, keepdims=True) + NORM_EPS)
    return (y * g.astype(jnp.float32)).astype(x.dtype)

def split_cols(z, sizes):
    idx = [int(v) for v in np.cumsum(sizes)[:-1]]
    return jnp.split(z, idx, axis=-1)

def rope_tables(positions):
    inv_freq = ROPE_THETA ** (-jnp.arange(0, A_ROPE, 2, dtype=jnp.float32) / A_ROPE)
    ang = positions.astype(jnp.float32)[..., None] * inv_freq
    return jnp.cos(ang), jnp.sin(ang)

def apply_rope(x, cos, sin):
    x1, x2 = jnp.split(x.astype(jnp.float32), 2, axis=-1)
    out = jnp.concatenate([x1 * cos - x2 * sin, x2 * cos + x1 * sin], axis=-1)
    return out.astype(x.dtype)

def causal_conv(x, w, b):
    S = x.shape[1]
    xp = jnp.pad(x, ((0, 0), (M_CONV - 1, 0), (0, 0)))
    y = b
    for j in range(M_CONV):
        y = y + xp[:, j:j + S] * w[j]
    return y

def to_chunks(t):
    B, S, H = t.shape[:3]
    t = t.reshape((B, S // M_CHUNK, M_CHUNK, H) + t.shape[3:])
    return jnp.moveaxis(t, (1, 3), (0, 2))

def mlstm_chunkwise(q, k, v, ig, lf):
    B, S, H, d = q.shape
    qc, kc, vc = to_chunks(q), to_chunks(k), to_chunks(v)
    igc, lfc = to_chunks(ig), to_chunks(lf)
    causal = jnp.tril(jnp.ones((M_CHUNK, M_CHUNK), dtype=bool))

    def step(carry, inp):
        C, n, m = carry
        qq, kk, vv, ii, ff = inp
        b = jnp.cumsum(ff, axis=-1)
        dlog = b[..., :, None] - b[..., None, :] + ii[..., None, :]
        dlog = jnp.where(causal, dlog, -jnp.inf)
        inter_log = b + m[..., None]
        m_t = jnp.maximum(inter_log, jnp.max(dlog, axis=-1))
        dw = jnp.exp(dlog - m_t[..., None])
        inter_w = jnp.exp(inter_log - m_t)
        s = jnp.einsum('bhtd,bhsd->bhts', qq, kk) * dw
        num = jnp.einsum('bhts,bhse->bhte', s, vv) + inter_w[..., None] * jnp.einsum('bhtd,bhde->bhte', qq, C)
        den = jnp.sum(s, axis=-1) + inter_w * jnp.einsum('bhtd,bhd->bht', qq, n)
        h = num / jnp.maximum(jnp.abs(den), jnp.exp(-m_t))[..., None]
        b_end = b[..., -1]
        wlog = b_end[..., None] - b + ii
        m_new = jnp.maximum(b_end + m, jnp.max(wlog, axis=-1))
        w = jnp.exp(wlog - m_new[..., None])
        decay = jnp.exp(b_end + m - m_new)
        C_new = decay[..., None, None] * C + jnp.einsum('bhs,bhsd,bhse->bhde', w, kk, vv)
        n_new = decay[..., None] * n + jnp.einsum('bhs,bhsd->bhd', w, kk)
        return (C_new, n_new, m_new), h

    init = (jnp.zeros((B, H, d, d), jnp.float32), jnp.zeros((B, H, d), jnp.float32),
            jnp.zeros((B, H), jnp.float32))
    _, hc = lax.scan(step, init, (qc, kc, vc, igc, lfc))
    return jnp.moveaxis(hc, (0, 2), (1, 3)).reshape(B, S, H, d)

def mla_attention(q_nope, q_rope, k_nope, k_rope, v):
    S = q_nope.shape[1]
    scale = A_QK ** -0.5
    outs = []
    for start in range(0, S, Q_BLOCK):
        end = start + Q_BLOCK
        s = (jnp.einsum('bqhd,bkhd->bhqk', q_nope[:, start:end], k_nope[:, :end])
             + jnp.einsum('bqhr,bkr->bhqk', q_rope[:, start:end], k_rope[:, :end]))
        s = s.astype(jnp.float32) * scale
        qi = start + jnp.arange(Q_BLOCK)[:, None]
        ki = jnp.arange(end)[None, :]
        s = jnp.where(ki <= qi, s, -jnp.inf)
        p = jax.nn.softmax(s, axis=-1).astype(v.dtype)
        outs.append(jnp.einsum('bhqk,bkhd->bqhd', p, v[:, :end]))
    return jnp.concatenate(outs, axis=1)

def setup_inputs(seed: int = 0) -> dict:
    key = jax.random.key(seed)
    ks = jax.random.split(key, 24)
    f32 = jnp.float32
    nrm = lambda k, shape, s: jax.random.normal(k, shape, f32) * s
    gain = lambda k, shape: 1.0 + 0.02 * jax.random.normal(k, shape, f32)
    L = DEPTH
    x = jax.random.normal(ks[0], (BATCH, SEQ, D_MODEL), f32)
    c = jax.random.normal(ks[1], (BATCH, D_MODEL), f32)
    offs = jax.random.randint(ks[2], (BATCH, 1), 0, 1024, dtype=jnp.int32)
    positions = (offs + jnp.arange(SEQ, dtype=jnp.int32)[None, :]).astype(jnp.int32)
    return {
        "x": x,
        "c": c,
        "positions": positions,
        "w_ada": nrm(ks[3], (L, D_MODEL, 6 * D_MODEL), 0.5 * D_MODEL ** -0.5),
        "b_ada": nrm(ks[4], (L, 6 * D_MODEL), 0.02),
        "g_mix": gain(ks[5], (L, D_MODEL)),
        "w_in": nrm(ks[6], (L, D_MODEL, D_IN), D_MODEL ** -0.5),
        "conv_w": nrm(ks[7], (L, M_CONV, 2 * M_WIDTH), M_CONV ** -0.5),
        "conv_b": nrm(ks[8], (L, 2 * M_WIDTH), 0.02),
        "b_igate": nrm(ks[9], (L, M_HEADS), 0.1),
        "b_fgate": jnp.linspace(3.0, 6.0, M_HEADS, dtype=f32)[None, :] + nrm(ks[10], (L, M_HEADS), 0.1),
        "g_mhead": gain(ks[11], (L, M_WIDTH)),
        "g_q_lat": gain(ks[12], (L, A_Q_RANK)),
        "w_uq": nrm(ks[13], (L, A_Q_RANK, A_HEADS * A_QK), A_Q_RANK ** -0.5),
        "g_kv_lat": gain(ks[14], (L, A_KV_RANK)),
        "w_ukv": nrm(ks[15], (L, A_KV_RANK, A_HEADS * (A_NOPE + A_V)), A_KV_RANK ** -0.5),
        "w_branch_m": nrm(ks[16], (L, M_WIDTH, D_MODEL), M_WIDTH ** -0.5),
        "w_branch_a": nrm(ks[17], (L, A_WIDTH, D_MODEL), A_WIDTH ** -0.5),
        "w_out": nrm(ks[18], (L, D_MODEL, D_MODEL), D_MODEL ** -0.5),
        "g_ffn": gain(ks[19], (L, D_MODEL)),
        "w_ffn_in": nrm(ks[20], (L, D_MODEL, 2 * D_FF), D_MODEL ** -0.5),
        "w_ffn_out": nrm(ks[21], (L, D_FF, D_MODEL), D_FF ** -0.5),
        "g_final": gain(ks[22], (D_MODEL,)),
    }

def reference(x, c, positions, w_ada, b_ada, g_mix, w_in, conv_w, conv_b, b_igate, b_fgate,
              g_mhead, g_q_lat, w_uq, g_kv_lat, w_ukv, w_branch_m, w_branch_a, w_out,
              g_ffn, w_ffn_in, w_ffn_out, g_final):
    B, S, _ = x.shape
    cos, sin = rope_tables(positions)
    cos_q, sin_q = cos[:, :, None, :], sin[:, :, None, :]
    h = x
    for l in range(DEPTH):
        ada = jax.nn.silu(c) @ w_ada[l] + b_ada[l]
        sh1, sc1, gt1, sh2, sc2, gt2 = [a[:, None, :] for a in jnp.split(ada, 6, axis=-1)]

        u = rmsnorm(h, g_mix[l]) * (1.0 + sc1) + sh1
        z = u @ w_in[l]
        (qm, km, vm, om, ipre, fpre, q_lat, kv_lat, kr_raw,
         gate_m, gate_a) = split_cols(z, IN_SIZES)

        qk = jax.nn.silu(causal_conv(jnp.concatenate([qm, km], axis=-1), conv_w[l], conv_b[l]))
        qm, km = jnp.split(qk, 2, axis=-1)
        f32 = jnp.float32
        qh = qm.reshape(B, S, M_HEADS, M_HEAD_DIM).astype(f32) * (M_HEAD_DIM ** -0.5)
        kh = km.reshape(B, S, M_HEADS, M_HEAD_DIM).astype(f32)
        vh = vm.reshape(B, S, M_HEADS, M_HEAD_DIM).astype(f32)
        log_i = ipre.astype(f32) + b_igate[l].astype(f32)
        log_f = jax.nn.log_sigmoid(fpre.astype(f32) + b_fgate[l].astype(f32))
        hm = mlstm_chunkwise(qh, kh, vh, log_i, log_f)
        hm = hm * lax.rsqrt(jnp.mean(hm * hm, axis=-1, keepdims=True) + NORM_EPS)
        hm = hm * g_mhead[l].astype(f32).reshape(M_HEADS, M_HEAD_DIM)
        hm = (jax.nn.sigmoid(om.astype(f32)) * hm.reshape(B, S, M_WIDTH)).astype(x.dtype)
        y_m = hm @ w_branch_m[l]

        cq = rmsnorm(q_lat, g_q_lat[l])
        qa = (cq @ w_uq[l]).reshape(B, S, A_HEADS, A_QK)
        q_nope, q_rope = qa[..., :A_NOPE], apply_rope(qa[..., A_NOPE:], cos_q, sin_q)
        ckv = rmsnorm(kv_lat, g_kv_lat[l])
        kva = (ckv @ w_ukv[l]).reshape(B, S, A_HEADS, A_NOPE + A_V)
        k_nope, va = kva[..., :A_NOPE], kva[..., A_NOPE:]
        k_rope = apply_rope(kr_raw, cos, sin)
        oa = mla_attention(q_nope, q_rope, k_nope, k_rope, va).reshape(B, S, A_WIDTH)
        y_a = oa @ w_branch_a[l]

        y = jax.nn.sigmoid(gate_m) * y_m + jax.nn.sigmoid(gate_a) * y_a
        h = h + gt1 * (y @ w_out[l])

        u2 = rmsnorm(h, g_ffn[l]) * (1.0 + sc2) + sh2
        gu = u2 @ w_ffn_in[l]
        g_, up = gu[..., :D_FF], gu[..., D_FF:]
        h = h + gt2 * ((jax.nn.silu(g_) * up) @ w_ffn_out[l])
    return rmsnorm(h, g_final)


_drawn_inputs = setup_inputs


def setup_inputs(seed=0):
    import zlib

    import numpy as np

    out = dict(_drawn_inputs(seed))
    spreads = {}
    factors = {'b_ada': 3.092,
     'g_mix': 8.0,
     'conv_b': 193.711,
     'b_igate': 64.0,
     'g_mhead': 30.894,
     'g_q_lat': 8.0,
     'w_uq': 3.002,
     'g_kv_lat': 8.0,
     'g_ffn': 8.0,
     'g_final': 23.348}
    for name, (base, spread) in spreads.items():
        noise = np.random.default_rng([zlib.crc32(name.encode()), seed]).standard_normal(out[name].shape)
        drawn = base * np.exp(spread * noise) if base else spread * noise
        out[name] = __import__('jax').numpy.asarray(drawn.astype(out[name].dtype))
    for name, factor in factors.items():
        out[name] = (out[name] * factor).astype(out[name].dtype)
    return out
```

```python
from contextlib import ExitStack

import numpy as np

import concourse.bass as bass
from concourse import mybir

F32, F32R, I32 = mybir.dt.float32, mybir.dt.float32r, mybir.dt.int32
ALU, ACT, AX = mybir.AluOpType, mybir.ActivationFunctionType, mybir.AxisListType

P = 128
BANK = 512
S = 1024
D = 1024
TT = S // P
KT = D // P
MH, MD = 4, 128
MW = MH * MD
CONV = 4
VA = MD + 2
AH, NOPE, ROPE, AV = 8, 64, 32, 64
AQK = NOPE + ROPE
QR, KVR = 256, 128
AW = AH * AV
FF = ((8 * D + 3 * 256 - 1) // (3 * 256)) * 256
FT = FF // P
EPS = 1e-6
NEG = -1e30
PW = 256
PANEL = KT * PW

C_V, C_O, C_I, C_F = 2 * MW, 3 * MW, 4 * MW, 4 * MW + MH
C_QL = C_F + MH
C_KVL = C_QL + QR
C_KR = C_KVL + KVR
C_GATE = C_KR + ROPE

ROWS = {}
for _name, _n in (("c", KT), ("b_ada", 6 * KT), ("g_mix", KT), ("g_ffn", KT), ("conv_w", CONV * 2 * MH),
                  ("conv_b", 2 * MH), ("g_mhead", MH), ("g_q_lat", QR // P), ("g_kv_lat", KVR // P)):
    ROWS[_name] = (sum(n for _, n in ROWS.values()), _n)
NROWS = sum(n for _, n in ROWS.values())

K_ID, K_QMASK, K_TMASK, K_FOLD, K_SEL = 0, P, 2 * P, 3 * P, 4 * P
K_COL = K_SEL + MH * P
NCONST = K_COL + 3 + 2 * MH


def constants():
    t = np.zeros((P, NCONST), np.float32)
    r = np.arange(P)
    t[:, K_ID:K_ID + P] = np.eye(P)
    t[:, K_QMASK:K_QMASK + P] = np.where(r[None, :] <= r[:, None], 0, NEG)
    t[:, K_TMASK:K_TMASK + P] = np.where(r[:, None] <= r[None, :], 0, NEG)
    t[:, K_FOLD:K_FOLD + P] = (r[:, None] >= NOPE) & (r[None, :] >= NOPE) & ((r[:, None] - r[None, :]) % ROPE == 0)
    for h in range(MH):
        t[h, K_SEL + h * P:K_SEL + (h + 1) * P] = 1
    inv = np.float32(10000.0) ** (-np.arange(0, ROPE, 2, dtype=np.float32) / np.float32(ROPE))
    t[NOPE:, K_COL] = inv[r[NOPE:] % (ROPE // 2)]
    turns = np.zeros(P)
    turns[NOPE:NOPE + ROPE] = 0.25
    turns[NOPE + ROPE:NOPE + ROPE + ROPE // 2] = 0.5
    t[:, K_COL + 1] = turns
    t[:, K_COL + 2] = turns * 2 * np.pi
    t[:, K_COL + 3:K_COL + 3 + 2 * MH] = np.repeat([MD ** -0.5, 1.0], MH)
    return t


class Record:
    pass


class Count:

    def __init__(self, eng, sem):
        self.eng, self.sem, self.n, self.var, self.per = eng, sem, 0, None, 0

    def loop(self, var, per):
        self.start, self.var, self.per = self.n, var, per

    def end(self, iterations):
        assert self.n - self.start == self.per, (self.n - self.start, self.per)
        self.n, self.var = self.start + self.per * iterations, None

    def value(self):
        return self.n if self.var is None else self.var * self.per + self.n

    def then(self, ins):
        ins.then_inc(self.sem, 1)
        self.n += 1
        return ins

    def wait(self):
        self.eng.wait_ge(self.sem, self.value())


def col(m, name, n=0):
    return m.cols[:, bass.ds(ROWS[name][0] + n, 1)]



SPEC_PARTS = 5 * 16


def load_panel(sp, m, q, s, parts, first=False):
    if not first:
        sp.wait_ge(m.w_hi, q * 2 + (s - 1))
        sp.wait_ge(m.w_lo, q * 2 + (s - 1))
    for n, (dst, src) in enumerate(parts):
        sp.dma_start(dst, src).then_inc(m.parts_landed[s] if n else m.raw_landed[s], 16)


def split_hi(act, m, q, s, parts=None):
    act.wait_ge(m.raw_landed[s], q * 16 + 16)
    if parts is not None:
        act.wait_ge(m.parts_landed[s], parts)
    if not (s == 0 and isinstance(q, int) and q == 0):
        act.wait_ge(m.w_used, q * 2 + s)
    act.activation(m.whi[s][:, :], m.raw[:, s, :], ACT.Copy).then_inc(m.w_hi, 1)


def split_lo(dve, m, q, s):
    dve.wait_ge(m.w_hi, q * 2 + (s + 1))
    if not (s == 0 and isinstance(q, int) and q == 0):
        dve.wait_ge(m.w_used, q * 2 + s)
    dve.tensor_tensor(m.wlo[s][:, :], m.raw[:, s, :], m.whi[s][:, :], ALU.subtract).then_inc(m.w_lo, 1)


def ffn_parts(i, s):
    return i * 16 + (16 + SPEC_PARTS * s)


def panel_ready(pe, m, q, s):
    pe.wait_ge(m.w_hi, q * 2 + (s + 1))
    pe.wait_ge(m.w_lo, q * 2 + (s + 1))


def kn(ap, k=KT):
    return ap.rearrange("p (k n) -> p k n", k=k)


def cols_of(w, c0, n=PW):
    return w[:, bass.ds(c0, n)].rearrange("(k p) c -> p k c", p=P)


def passes(m, s, xhi, xlo):
    return (m.whi[s], xhi), (m.whi[s], xlo), (m.wlo[s], xhi)



NQK, NV, NO, NL, NG = 4, 2, 2, 2, 8
ADA1 = 2 * D
NZ = NQK + NV + NO + NL + NG
ACC = P
PIECES = 4 * D // ACC // NG


def stage_project(nc, m, io):
    with ExitStack() as ctx:
        alloc = lambda name, shape, dt=F32: ctx.enter_context(nc.sbuf_tensor(name, shape, dt))
        uhi, ulo = alloc("uhi", [P, KT, S], F32R), alloc("ulo", [P, KT, S], F32R)
        conv = alloc("conv", [P, 2, S + CONV])
        temp = conv[:, :, CONV:CONV + S]
        acc_raw = temp[:, 1, :].rearrange("p (a k n) -> p a k n", a=2, k=KT // 2)
        acc_sum = alloc("acc_sum", [P, 2, ACC])
        acc_landed, acc_stored = ([m.sem(f"{n}{i}") for i in range(2)] for n in ("accr_landed", "acc_stored"))
        acc_step = m.sem("acc_step")
        sem = m.sem
        rows_landed, const_landed, ones_ready = sem("rows_landed"), sem("const_landed"), sem("ones_ready")
        ada_landed, ada_used = [sem(f"ada_landed{i}") for i in range(4)], sem("ada_used")
        x_landed = [sem(f"x_landed{i}") for i in range(4)]
        rows_zeroed, cols_turned, cols_ready, c_sig = sem("rows_zeroed"), sem("cols_turned"), sem("cols_ready"), sem("c_sig")
        sq_done, rms_ready, x_normed = sem("sq_done"), sem("rms_ready"), sem("x_normed")
        ada_summed, ada_in_ps, ada1_ready = sem("ada_summed"), sem("ada_in_ps"), sem("ada1_ready")
        x_turned, u_ready, uhi_ready, ulo_ready = sem("x_turned"), sem("u_ready"), sem("uhi_ready"), sem("ulo_ready")
        tile_done, tile_drained = sem("z_tile_done"), sem("z_tile_drained")
        conv_acc, conv_sig, conv_out = sem("conv_acc"), sem("conv_sig"), sem("conv_out")
        gate_stored = sem("gate_stored")
        dve_own, pool_own, pool_first = sem("dve_own1"), sem("pool_own1"), sem("pool_first")
        w_in = io.w_in
        GQ = (NZ - NG) // 2

        block = ctx.enter_context(nc.Block("project"))

        @block.sync
        def _(sp):
            sp.wait_ge(rows_zeroed, 1)
            for name, src in io.rows:
                r, n = ROWS[name]
                sp.dma_start(m.rows[r:r + n, :], src).then_inc(rows_landed, 16)
            sp.dma_start(m.const[:, :], io.const).then_inc(const_landed, 16)
            sp.dma_start(m.bif[32:32 + MH, 0:1], io.b_igate).then_inc(const_landed, 16)
            sp.dma_start(m.bif[0:MH, 0:1], io.b_fgate).then_inc(const_landed, 16)
            for k in range(KT):
                if k >= 4:
                    sp.wait_ge(ada_used, k - 3)
                sp.dma_start(m.ada_raw[:, k % 4, :], io.w_ada[k * P:(k + 1) * P, 0:ADA1]).then_inc(ada_landed[k % 4], 16)
            panels = [[(kn(m.raw[:, n % 2, :]), cols_of(w_in, c))] for n, c in
                      enumerate([PW * i for i in range(NQK)] + [C_V, C_V + PW, C_O, C_O + PW, C_QL])]
            r, half = kn(m.raw[:, 1, :]), ROPE // 2
            panels.append([(r[:, :, a:a + n], cols_of(w_in, c, n)) for a, c, n in (
                (0, C_KVL, KVR), (P, C_F, MH), (P + 32, C_I, MH), (P + NOPE, C_KR, ROPE),
                (P + NOPE + ROPE, C_KR + half, half), (P + NOPE + ROPE + half, C_KR, half))])
            for n, parts in enumerate(panels):
                load_panel(sp, m, n // 2, n % 2, parts, first=n < 2)

            def gate_panel(q, s, c):
                load_panel(sp, m, q, s, [(kn(m.raw[:, s, :]), cols_of(w_in, c + (C_GATE + s * PW)))])

            def pieces(i, s):
                for n in range(PIECES * s, PIECES * (s + 1)):
                    for h in range(2):
                        sp.wait_ge(acc_step, i * (2 * PIECES * KT) + (KT * n + KT // 2 * (h + 1)))
                        sp.dma_start(acc_raw[:, h, :, :], io.w_ada[h * S // 2:(h + 1) * S // 2, bass.ds(i * (2 * PIECES * ACC) + (ADA1 + n * ACC), ACC)].rearrange(
                            "(k p) n -> p k n", p=P)).then_inc(acc_landed[h], 16)

            for s in range(2):
                gate_panel(GQ, s, 0)
            sp.wait_ge(conv_out, 2 * NQK)
            with sp.Fori(0, NG // 2 - 1) as i:
                for s in range(2):
                    gate_panel(i + (GQ + 1), s, i * (2 * PW) + 2 * PW)
                    pieces(i, s)
            for s in range(2):
                load_panel(sp, m, NZ // 2, s, io.branch_panel(m, 0, s))
                pieces(NG // 2 - 1, s)

        @block.gpsimd
        def _(pool):
            own = Count(pool, pool_own)
            pool.memset(m.rows[:, :], 0.0).then_inc(rows_zeroed, 1)
            pool.memset(m.ones[:, :], 1.0).then_inc(ones_ready, 1)
            own.then(pool.memset(m.neghalf[:, :], -0.5))
            pool.memset(conv[:, 0, 0:CONV], 0.0).then_inc(pool_first, 1)
            pool.wait_ge(sq_done, TT)
            own.then(pool.tensor_scalar(m.stat[:, 0:TT], m.stat[:, 0:TT], 1.0 / D, EPS, ALU.mult, ALU.add))
            own.wait()
            pool.tensor_tensor(m.stat[:, TT:2 * TT], m.stat[:, 0:TT], m.neghalf[:, 0:TT], ALU.pow).then_inc(rms_ready, 1)
            pool.wait_ge(tile_drained, 4)
            own.then(pool.memset(m.vaug[:, :, :, MD:VA], 1.0))

            with pool.Fori(0, NG // 2) as i:
                for n in range(2 * PIECES):
                    pool.wait_ge(acc_step, i * (2 * PIECES * KT) + KT * (n + 2))
                    pool.dma_start(io.ada_acc[:, bass.ds(i * (2 * PIECES * ACC) + n * ACC, ACC)], acc_sum[:, n % 2, :]).then_inc(acc_stored[n % 2], 16)
            for s in range(2):
                pool.wait_ge(acc_stored[s], 16 * PIECES * NG // 2)

        @block.scalar
        def _(act):
            for i in range(4):
                act.dma_start(m.xs[:, 2 * i:2 * i + 2, :], io.x[i * 2 * P:(i + 1) * 2 * P, :].rearrange("(t p) n -> p t n", p=P)).then_inc(x_landed[i], 16)
            act.wait_ge(cols_ready, 1)
            act.activation(m.csil[:, :], m.cols[:, 0:KT], ACT.Sigmoid).then_inc(c_sig, 1)
            for t in range(TT):
                act.wait_ge(x_landed[t // 2], 16)
                if t >= 2:
                    act.wait_ge(sq_done, t - 1)
                act.activation(uhi[:, t % 2, :], m.xs[:, t, :], ACT.Square, accum_out=m.stat[:, t:t + 1]).then_inc(sq_done, 1)
            split_hi(act, m, 0, 0)
            act.wait_ge(ada1_ready, 1)
            for k in range(KT):
                act.wait_ge(x_turned, k + 1)
                if k >= 2:
                    act.wait_ge(ulo_ready, k - 1)
                b = (4 + 2 * (k % 2)) * BANK
                act.activation(temp[:, k % 2, :], m.ps[:, b:b + S], ACT.Identity,
                               scale=m.aff[:, k:k + 1], bias=m.aff[:, KT + k:KT + k + 1]).then_inc(u_ready, 1)
            act.wait_ge(u_ready, KT)
            act.sem_inc(tile_drained, 2)
            act.wait_ge(ulo_ready, KT)
            act.wait_ge(pool_first, 1)

            def banks(n):
                return m.ps[:, 2 * n * BANK:2 * (n + 1) * BANK]

            with act.Fori(0, NQK // 2) as i:
                for s in range(2):
                    split_hi(act, m, i + s, 1 - s)
                    for t in range(2):
                        n = 2 * s + t
                        act.wait_ge(tile_done, i * 4 + (n + 1))
                        act.wait_ge(conv_acc, i * 4 + (n + 1))
                        act.activation(conv[:, 0, CONV - 1:CONV - 1 + S], banks(n), ACT.Copy).then_inc(tile_drained, 1)
                        act.wait_ge(conv_acc, i * 4 + (n + 2))
                        act.activation(temp[:, 1, :], m.qk[:, bass.ds(i * 4 + n, 1), :].rearrange("p a n -> p (a n)"),
                                       ACT.Sigmoid).then_inc(conv_sig, 1)
            for n in range(NQK, NZ - NG):
                split_hi(act, m, (n + 1) // 2, (n + 1) % 2, SPEC_PARTS if n + 1 == NZ - NG - 1 else None)
                for t in range(2):
                    act.wait_ge(tile_done, 2 * n + t + 1)
                    src, func = banks(2 * (n % 2) + t), ACT.Copy
                    if n < NQK + NV:
                        h = 2 * (n - NQK)
                        src = src.rearrange("p (t h e) -> p t h e", t=TT // 2, h=2)
                        dst = m.vaug[:, TT // 2 * t:TT // 2 * (t + 1), h:h + 2, 0:MD]
                    elif n < NQK + NV + NO:
                        dst, func = m.osig[:, 2 * (n - NQK - NV) + t, :], ACT.Sigmoid
                    else:
                        dst = m.lat[:, 2 * (n - NQK - NV - NO) + t, :]
                    act.activation(dst, src, func).then_inc(tile_drained, 1)
            act.wait_ge(conv_out, 2 * NQK)
            with act.Fori(0, NG // 2) as i:
                for s in range(2):
                    split_hi(act, m, i + (GQ + s), 1 - s)
                    for t in range(2):
                        n = 2 * s + t
                        act.wait_ge(tile_done, i * 4 + (4 * GQ + n + 1))
                        if n:
                            act.wait_ge(gate_stored, i * 64 + 16 * n)
                        act.activation(temp[:, 0, :], banks(n), ACT.Sigmoid).then_inc(tile_drained, 1)
                        act.wait_ge(tile_drained, i * 4 + (4 * GQ + n + 1 + 4))
                        act.dma_start(io.gates[bass.ds(i * 4 + n, 1), :, :].rearrange("a p n -> p (a n)"), temp[:, 0, :]).then_inc(gate_stored, 16)
                act.wait_ge(gate_stored, i * 64 + 64)

        @block.vector
        def _(dve):
            own = Count(dve, dve_own)
            dve.wait_ge(cols_turned, 1)
            dve.tensor_copy(m.cols[:, :], m.ps[:, 7 * BANK:7 * BANK + P]).then_inc(cols_ready, 1)
            dve.wait_ge(cols_ready, 1)
            dve.wait_ge(c_sig, 1)
            own.then(dve.tensor_tensor(m.csil[:, :], m.cols[:, 0:KT], m.csil[:, :], ALU.mult))
            for k in range(KT):
                dve.wait_ge(ada_landed[k % 4], 16 * (k // 4 + 1))
                own.wait()
                own.then(dve.tensor_scalar(m.ada_acc[:, :], m.ada_raw[:, 0, :], m.csil[:, 0:1], None, ALU.mult) if k == 0 else
                         dve.scalar_tensor_tensor(out=m.ada_acc[:, :], in0=m.ada_raw[:, k % 4, :], scalar=m.csil[:, k:k + 1],
                                                  in1=m.ada_acc[:, :], op0=ALU.mult, op1=ALU.add))
                own.wait()
                dve.sem_inc(ada_used, 1)
            dve.sem_inc(ada_summed, 1)
            split_lo(dve, m, 0, 0)
            dve.wait_ge(rms_ready, 1)
            for t in range(TT):
                dve.tensor_scalar(m.xs[:, t, :], m.xs[:, t, :], m.stat[:, TT + t:TT + t + 1], None, ALU.mult).then_inc(x_normed, 1)
            dve.wait_ge(ada_in_ps, 1)
            adac = m.ps[:, 0:2 * KT * P].rearrange("p (j n) -> p j n", n=P)[:, :, 0]
            r = ROWS["b_ada"][0]
            own.then(dve.tensor_tensor(m.aff[:, KT:2 * KT], adac[:, 0:KT], m.cols[:, r:r + KT], ALU.add))
            own.then(dve.tensor_tensor(m.aff[:, 0:KT], adac[:, KT:2 * KT], m.cols[:, r + KT:r + 2 * KT], ALU.add))
            own.wait()
            dve.sem_inc(tile_drained, 2)
            r = ROWS["g_mix"][0]
            dve.scalar_tensor_tensor(out=m.aff[:, 0:KT], in0=m.aff[:, 0:KT], scalar=1.0, in1=m.cols[:, r:r + KT],
                                     op0=ALU.add, op1=ALU.mult).then_inc(ada1_ready, 1)
            for k in range(KT):
                dve.wait_ge(u_ready, k + 1)
                dve.tensor_copy(uhi[:, k, :], temp[:, k % 2, :]).then_inc(uhi_ready, 1)
                dve.wait_ge(uhi_ready, k + 1)
                dve.tensor_tensor(ulo[:, k, :], temp[:, k % 2, :], uhi[:, k, :], ALU.subtract).then_inc(ulo_ready, 1)
            dve.sem_inc(conv_acc, 1)
            with dve.Fori(0, NQK // 2) as i:
                own.loop(i, 2 * 2 * CONV - 4)
                for s in range(2):
                    split_lo(dve, m, i + s, 1 - s)
                    for t in range(2):
                        n = 2 * s + t
                        acc = m.qk[:, bass.ds(i * 4 + n, 1), :].rearrange("p a n -> p (a n)")
                        dve.wait_ge(tile_drained, i * 4 + (n + 1 + 4))
                        own.then(dve.tensor_scalar(acc, conv[:, 0, 0:S], col(m, "conv_w", i * 4 + n), col(m, "conv_b", i * 4 + n),
                                                   ALU.mult, ALU.add))
                        for j in range(1, CONV):
                            own.wait()
                            ins = dve.scalar_tensor_tensor(out=acc, in0=conv[:, 0, j:j + S], scalar=col(m, "conv_w", i * 4 + (j * 2 * MH + n)),
                                                           in1=acc, op0=ALU.mult, op1=ALU.add)
                            if j < CONV - 1:
                                own.then(ins)
                            else:
                                ins.then_inc(conv_acc, 1)
                        dve.wait_ge(conv_sig, i * 4 + (n + 1))
                        dve.scalar_tensor_tensor(out=acc, in0=acc, scalar=m.const[:, bass.ds(i * 4 + (K_COL + 3 + n), 1)],
                                                 in1=temp[:, 1, :], op0=ALU.mult, op1=ALU.mult).then_inc(conv_out, 1)
                own.end(NQK // 2)
            for n in range(NQK, NZ - NG):
                split_lo(dve, m, (n + 1) // 2, (n + 1) % 2)
            dve.sem_inc(acc_step, KT)
            with dve.Fori(0, NG // 2) as i:
                for s in range(2):
                    split_lo(dve, m, i + (GQ + s), 1 - s)
                    for n in range(PIECES * s, PIECES * (s + 1)):
                        if n >= 2:
                            dve.wait_ge(acc_stored[n % 2], i * (16 * PIECES) + 16 * (n // 2))
                        for k in range(KT):
                            if k % (KT // 2) == 0:
                                dve.wait_ge(acc_landed[2 * k // KT], i * (32 * PIECES) + 16 * (n + 1))
                            dve.wait_ge(acc_step, i * (2 * PIECES * KT) + (KT * (n + 1) + k))
                            raw, out = acc_raw[:, 2 * k // KT, k % (KT // 2), :], acc_sum[:, n % 2, :]
                            (dve.tensor_scalar(out, raw, m.csil[:, 0:1], None, ALU.mult) if k == 0 else
                             dve.scalar_tensor_tensor(out=out, in0=raw, scalar=m.csil[:, k:k + 1], in1=out, op0=ALU.mult, op1=ALU.add)
                             ).then_inc(acc_step, 1)
                for n in range(2):
                    dve.wait_ge(acc_stored[n], i * (16 * PIECES) + 16 * PIECES)

        @block.tensor
        def _(pe):
            pe.sem_inc(m.w_used, 1)
            pe.wait_ge(rows_landed, 16 * len(io.rows))
            pe.wait_ge(const_landed, 48)
            pe.transpose(m.ps[:, 7 * BANK:7 * BANK + P], m.rows[:, :], m.ident).then_inc(cols_turned, 1)
            pe.wait_ge(ada_summed, 1)
            pe.wait_ge(ones_ready, 1)
            for j in range(2 * KT):
                mm = pe.matmul(m.ps[:, j * P:(j + 1) * P], m.ada_acc[:, j * P:(j + 1) * P], m.ones[:, :], start=True, stop=True)
            mm.then_inc(ada_in_ps, 1)
            pe.wait_ge(cols_ready, 1)
            for k in range(KT):
                if k >= 2:
                    pe.wait_ge(u_ready, k - 1)
                for t in range(TT):
                    if k == 0:
                        pe.wait_ge(x_normed, t + 1)
                    b = (4 + 2 * (k % 2)) * BANK + t * P
                    mm = pe.transpose(m.ps[:, b:b + P], m.xs[:, t, k * P:(k + 1) * P], m.ident)
                mm.then_inc(x_turned, 1)

            def feature_major(q):
                for s in range(2):
                    panel_ready(pe, m, q, s)
                    for t in range(2):
                        pe.wait_ge(tile_drained, q * 4 + (2 * s + t + 1))
                        for k in range(KT):
                            pe.wait_ge(ulo_ready, k + 1)
                            for g, (w, x) in enumerate(passes(m, s, uhi, ulo)):
                                for half in range(2):
                                    b = (4 * s + 2 * t + half) * BANK
                                    mm = pe.matmul(m.ps[:, b:b + BANK], kn(w[:, :])[:, k, t * P:(t + 1) * P],
                                                   x[:, k, half * BANK:(half + 1) * BANK],
                                                   start=(k == 0 and g == 0), stop=(k == KT - 1 and g == 2))
                        mm.then_inc(tile_done, 1)
                    pe.wait_ge(tile_done, q * 4 + (2 * s + 2))
                    pe.sem_inc(m.w_used, 1)

            with pe.Fori(0, NQK // 2) as i:
                feature_major(i)
            for n in range(NQK, NQK + NV):
                panel_ready(pe, m, n // 2, n % 2)
                for t in range(TT):
                    if t % 4 == 0:
                        pe.wait_ge(tile_drained, 2 * n + t // 4 + 1)
                    b = 4 * (n % 2) * BANK + t * PW
                    for k in range(KT):
                        for g, (w, x) in enumerate(passes(m, n % 2, uhi, ulo)):
                            mm = pe.matmul(m.ps[:, b:b + PW], x[:, k, t * P:(t + 1) * P], kn(w[:, :])[:, k, :],
                                           start=(k == 0 and g == 0), stop=(k == KT - 1 and g == 2))
                    if t % 4 == 3:
                        mm.then_inc(tile_done, 1)
                pe.wait_ge(tile_done, 2 * n + 2)
                pe.sem_inc(m.w_used, 1)
            with pe.Fori(0, (NZ - NQK - NV) // 2) as i:
                feature_major(i + (NQK + NV) // 2)



def stage_mlstm(nc, m, io):
    NC = TT
    with ExitStack() as ctx:
        alloc = lambda name, shape, dt=F32: ctx.enter_context(nc.sbuf_tensor(name, shape, dt))
        sem = m.sem
        g = alloc("gate_rows", [P, 6, S])
        x_, sp_, lf, b_, a_, cm = (g[0:MH, n, :] for n in range(6))
        turn = alloc("turn_rows", [P, S])
        mprev, mdec = alloc("mprev", [P, NC + 1]), alloc("mdec", [P, NC])
        acol = alloc("acol", [P, NC, MH])
        ecol = alloc("ecol", [P, NC, 3, MH])
        cmb = alloc("cmb", [P, MH, S])
        decay = alloc("decay", [P, MH, NC])
        state = alloc("state", [P, MH, VA])
        qkc = [alloc(f"qkc{i}", [P, 2 * MH, P]) for i in range(2)]
        kw = [alloc(f"kw{i}", [P, MH, P]) for i in range(2)]
        sw = [alloc(f"sw{i}", [P, MH, P]) for i in range(2)]
        arg, dmat = alloc("arg", [P, MH, P]), alloc("dmat", [P, MH, P])
        inter, num = alloc("inter", [P, MH, VA]), alloc("num", [P, MH, VA])
        sq, hs = alloc("sq", [P, P]), alloc("hs", [P, MH, P])
        den, ss, rt = alloc("den", [P, MH]), alloc("ss", [P, MH]), alloc("rt", [P, 4, MH])

        zeroed, x_ready, l_ready, lf_ready, cm_ready, turn_ready, turned = (
            sem("l_zeroed"), sem("lx_ready"), sem("l_ready"), sem("lf_ready"), sem("cm_ready"), sem("turn_ready"), sem("turned"))
        act_own, dve_own, cmb_ps, cols_done = sem("act_own2"), sem("dve_own2"), sem("cmb_ps"), sem("l_cols_done")
        kc_ready, kt_done, kw_ready, s_done, arg_ready, d_ready, sw_ready = (
            sem("kc_ready"), sem("kt_done"), sem("kw_ready"), sem("s_done"), sem("arg_ready"), sem("d_ready"), sem("sw_ready"))
        upd_done, inter_done, intra_done, state_ready, inter_ready, num_ready = (
            sem("upd_done"), sem("inter_done"), sem("intra_done"), sem("state_ready"), sem("inter_ready"), sem("num_ready"))
        ss_ready, var_ready, pow_ready, hs_ready, ht_done, hm_ready, pool_own = (
            sem("ss_ready"), sem("var_ready"), sem("pow_ready"), sem("hs_ready"), sem("ht_done"), sem("hm_ready"), sem("pool_own2"))

        B = lambda n, w=BANK: m.ps[:, n * BANK:n * BANK + w]
        heads = lambda ap: ap.rearrange("p (h n) -> p h n", h=MH)
        two = lambda n: m.ps[:, n * BANK:(n + 2) * BANK].rearrange("p (b n) -> p b n", b=2)[:, :, 0:2 * VA]
        slot = lambda n, h: m.ps[:, (n + h // 2) * BANK + (h % 2) * VA:(n + h // 2) * BANK + (h % 2 + 1) * VA]
        chunk = lambda ap, c: ap[:, :, bass.ds(c * P, P)]
        LOOPS = (NC - 3) // 2
        is_ = lambda c, n: isinstance(c, int) and c == n

        block = ctx.enter_context(nc.Block("mlstm"))

        def schedule(eng, step, own=None, per=0):
            step(0, 0)
            with eng.Fori(0, LOOPS) as i:
                if own:
                    own.loop(i, 2 * per)
                for k in (1, 2):
                    step(i * 2 + k, k % 2)
                if own:
                    own.end(LOOPS)
            for c in range(2 * LOOPS + 1, NC):
                step(c, c % 2)

        @block.gpsimd
        def _(pool):
            own = Count(pool, pool_own)
            own.then(pool.memset(turn[:, :], 0.0))
            own.then(pool.memset(mprev[:, :], 0.0))
            own.then(pool.memset(state[:, :, :], 0.0))
            own.wait()
            pool.sem_inc(zeroed, 1)

            def step(c, s):
                pool.wait_ge(var_ready, c + 1)
                pool.tensor_tensor(rt[:, 2, :], rt[:, 1, :], m.neghalf[:, 0:MH], ALU.pow).then_inc(pow_ready, 1)

            schedule(pool, step)

        @block.scalar
        def _(act):
            own = Count(act, act_own)
            act.wait_ge(x_ready, 1)
            own.then(act.activation(sp_, x_, ACT.Abs))
            own.wait()
            own.then(act.activation(sp_, sp_, ACT.Exp, scale=-1.0))
            own.wait()
            act.activation(sp_, sp_, ACT.Ln, bias=1.0).then_inc(l_ready, 1)
            act.wait_ge(cmb_ps, 1)
            act.activation(cmb[:, 0:2, :].rearrange("p h n -> p (h n)"), m.ps[:, 0:2 * S], ACT.Copy).then_inc(cols_done, 1)
            act.wait_ge(cmb_ps, 2)
            act.activation(cmb[:, 2:4, :].rearrange("p h n -> p (h n)"), m.ps[:, 2 * S:4 * S], ACT.Copy).then_inc(cols_done, 1)
            act.wait_ge(turned, 1)
            t = m.ps[:, 0:S].rearrange("p (c n) -> p c n", c=NC)
            act.activation(acol[:, :, :], t[:, :, 0:MH], ACT.Copy).then_inc(cols_done, 1)
            for n in range(3):
                act.activation(ecol[:, :, n, :], t[:, :, 32 * (n + 1):32 * (n + 1) + MH], ACT.Exp).then_inc(cols_done, 1)
            act.activation(decay[:, :, :], m.ps[:, 2 * BANK:2 * BANK + MH * NC].rearrange("p (h c) -> p h c", h=MH), ACT.Exp).then_inc(cols_done, 1)
            act.wait_ge(cols_done, 7)

            def copy(c, s):
                if not (isinstance(c, int) and c < 2):
                    act.wait_ge(s_done, c - 1)
                    act.wait_ge(kt_done, c - 1)
                    act.wait_ge(inter_done, c - 1)
                act.activation(qkc[s][:, :, :], chunk(m.qk[:, :, :], c), ACT.Copy).then_inc(kc_ready, 1)

            def weights(c, s):
                act.wait_ge(kt_done, c + 1)
                if not (isinstance(c, int) and c < 2):
                    act.wait_ge(upd_done, c - 1)
                for h in range(MH):
                    last = act.activation(kw[s][:, h, :], heads(B(0))[:, h, :], ACT.Copy,
                                          scale=ecol[:, bass.ds(c, 1), 2, h:h + 1].rearrange("p a n -> p (a n)"))
                last.then_inc(kw_ready, 1)
                act.wait_ge(arg_ready, c + 1)
                if not is_(c, 0):
                    act.wait_ge(sw_ready, c)
                act.activation(dmat[:, :, :], arg[:, :, :], ACT.Exp).then_inc(d_ready, 1)

            def step(c, s):
                if not is_(c, NC - 1):
                    weights(c + 1, 1 - s)
                act.wait_ge(inter_done, c + 1)
                if not is_(c, 0):
                    act.wait_ge(num_ready, c)
                for h in range(MH):
                    last = act.activation(inter[:, h, :], slot(4, h), ACT.Copy,
                                          scale=ecol[:, bass.ds(c, 1), 0, h:h + 1].rearrange("p a n -> p (a n)"))
                last.then_inc(inter_ready, 1)
                if not (isinstance(c, int) and c >= NC - 2):
                    copy(c + 2, s)
                act.wait_ge(num_ready, c + 1)
                if not is_(c, 0):
                    act.wait_ge(var_ready, c)
                for h in range(MH):
                    if h or not is_(c, 0):
                        act.wait_ge(ss_ready, c * MH + h)
                    act.activation(sq[:, :], num[:, h, 0:MD], ACT.Square, accum_out=ss[:, h:h + 1]).then_inc(ss_ready, 1)

            copy(0, 0)
            copy(1, 1)
            weights(0, 0)
            schedule(act, step)

        @block.vector
        def _(dve):
            own = Count(dve, dve_own)
            dve.wait_ge(zeroed, 1)
            dve.tensor_scalar(x_, m.lat[0:MH, 3, :], m.bif[0:MH, 0:1], None, ALU.add).then_inc(x_ready, 1)
            own.then(dve.tensor_scalar(cm, m.lat[32:32 + MH, 3, :], m.bif[32:32 + MH, 0:1], None, ALU.add))
            dve.wait_ge(x_ready, 1)
            own.then(dve.tensor_scalar(lf, x_, 0.0, None, ALU.min))
            own.wait()
            dve.wait_ge(l_ready, 1)
            own.then(dve.tensor_tensor(lf, lf, sp_, ALU.subtract))
            own.wait()
            for c in range(NC):
                r = slice(c * P, (c + 1) * P)
                own.then(dve.tensor_tensor_scan(b_[:, r], m.ones[0:MH, :], lf[:, r], 0.0, ALU.mult, ALU.add))
            own.wait()
            own.then(dve.tensor_tensor(a_, cm, b_, ALU.subtract))
            own.wait()
            for c in range(NC):
                r, e = slice(c * P, (c + 1) * P), slice((c + 1) * P - 1, (c + 1) * P)
                own.then(dve.tensor_tensor_scan(cm[:, r], a_[:, r], a_[:, r], mprev[0:MH, c:c + 1], ALU.max, ALU.max))
                own.wait()
                own.then(dve.tensor_tensor(mprev[0:MH, c + 1:c + 2], b_[:, e], cm[:, e], ALU.add))
                own.wait()
            dve.sem_inc(cm_ready, 1)
            cend = cm.rearrange("p (c n) -> p c n", c=NC)[:, :, P - 1:P]
            mp = mprev[0:MH, 0:NC].rearrange("p (c o) -> p c o", o=1)
            c3 = lambda ap: ap.rearrange("p (c n) -> p c n", c=NC)
            own.then(dve.tensor_copy(turn[0:MH, :], a_))
            own.then(dve.tensor_tensor(c3(turn[32:32 + MH, :]), mp.to_broadcast([MH, NC, P]), c3(cm), ALU.subtract))
            own.then(dve.scalar_tensor_tensor(out=turn[64:64 + MH, :], in0=b_, scalar=-1.0, in1=cm, op0=ALU.mult, op1=ALU.subtract))
            own.then(dve.tensor_tensor(c3(turn[96:96 + MH, :]), c3(a_), cend.to_broadcast([MH, NC, P]), ALU.subtract))
            own.then(dve.tensor_tensor(mdec[0:MH, :].rearrange("p (c o) -> p c o", o=1), mp, cend, ALU.subtract))
            own.wait()
            dve.sem_inc(turn_ready, 1)
            dve.wait_ge(cols_done, 7)

            def exponents(c):
                if not is_(c, 0):
                    dve.wait_ge(d_ready, c)
                for h in range(MH):
                    last = dve.scalar_tensor_tensor(out=arg[:, h, :], in0=m.const[:, K_TMASK:K_TMASK + P],
                                                    scalar=acol[:, bass.ds(c, 1), h:h + 1].rearrange("p a n -> p (a n)"),
                                                    in1=cmb[:, h, bass.ds(c * P, P)], op0=ALU.add, op1=ALU.subtract)
                last.then_inc(arg_ready, 1)

            def weights(c, s):
                dve.wait_ge(s_done, c + 1)
                dve.wait_ge(d_ready, c + 1)
                if not (isinstance(c, int) and c < 2):
                    dve.wait_ge(intra_done, c - 1)
                dve.tensor_tensor(sw[s][:, :, :], heads(B(1)), dmat[:, :, :], ALU.mult).then_inc(sw_ready, 1)

            def out(c):
                dve.wait_ge(ht_done, c + 1)
                for h in range(MH):
                    last = dve.scalar_tensor_tensor(out=m.qk[:, h, bass.ds(c * P, P)], in0=heads(B(0))[:, h, :], scalar=col(m, "g_mhead", h),
                                                    in1=m.osig[:, h, bass.ds(c * P, P)], op0=ALU.mult, op1=ALU.mult)
                last.then_inc(hm_ready, 1)

            def step(c, s):
                if not is_(c, NC - 1):
                    weights(c + 1, 1 - s)
                dve.wait_ge(upd_done, c + 1)
                dve.wait_ge(inter_done, c + 1)
                for h in range(MH):
                    last = dve.scalar_tensor_tensor(out=state[:, h, :], in0=state[:, h, :], scalar=decay[:, h, bass.ds(c, 1)],
                                                    in1=slot(6, h), op0=ALU.mult, op1=ALU.add)
                last.then_inc(state_ready, 1)
                dve.wait_ge(intra_done, c + 1)
                dve.wait_ge(inter_ready, c + 1)
                if not is_(c, 0):
                    dve.wait_ge(hs_ready, c)
                    dve.wait_ge(ss_ready, c * MH)
                dve.tensor_tensor(num[:, :, :].rearrange("p (b h) n -> p b (h n)", b=2), two(2),
                                  inter[:, :, :].rearrange("p (b h) n -> p b (h n)", b=2), ALU.add).then_inc(num_ready, 1)
                if not is_(c, 0):
                    out(c - 1)
                dve.wait_ge(num_ready, c + 1)
                d = num[:, :, MD]
                own.then(dve.scalar_tensor_tensor(out=den[:, :], in0=d, scalar=-1.0, in1=d, op0=ALU.mult, op1=ALU.max))
                own.wait()
                own.then(dve.tensor_tensor(den[:, :], den[:, :], ecol[:, bass.ds(c, 1), 1, :].rearrange("p a n -> p (a n)"), ALU.max))
                own.wait()
                own.then(dve.reciprocal(rt[:, 0, :], den[:, :]))
                own.wait()
                own.then(dve.tensor_tensor(rt[:, 3, :], rt[:, 0, :], rt[:, 0, :], ALU.mult))
                own.wait()
                dve.wait_ge(ss_ready, c * MH + MH)
                own.then(dve.tensor_tensor(rt[:, 1, :], ss[:, :], rt[:, 3, :], ALU.mult))
                own.wait()
                dve.tensor_scalar(rt[:, 1, :], rt[:, 1, :], 1.0 / MD, EPS, ALU.mult, ALU.add).then_inc(var_ready, 1)
                if not (isinstance(c, int) and c >= NC - 2):
                    exponents(c + 2)
                dve.wait_ge(pow_ready, c + 1)
                own.then(dve.tensor_tensor(rt[:, 3, :], rt[:, 0, :], rt[:, 2, :], ALU.mult))
                own.wait()
                if not is_(c, 0):
                    dve.wait_ge(ht_done, c)
                for h in range(MH):
                    last = dve.tensor_scalar(hs[:, h, :], num[:, h, 0:MD], rt[:, 3, h:h + 1], None, ALU.mult)
                last.then_inc(hs_ready, 1)

            exponents(0)
            weights(0, 0)
            exponents(1)
            schedule(dve, step, own, 6)
            out(NC - 1)

        @block.tensor
        def _(pe):
            sel = lambda h: m.const[0:MH, K_SEL + h * P:K_SEL + (h + 1) * P]
            pe.sem_inc(hm_ready, 1)
            pe.wait_ge(cm_ready, 1)
            for h in range(MH):
                for half in range(2):
                    mm = pe.matmul(B(2 * h + half), sel(h), cm[:, half * BANK:(half + 1) * BANK], start=True, stop=True)
                if h % 2:
                    mm.then_inc(cmb_ps, 1)
            pe.wait_ge(turn_ready, 1)
            pe.wait_ge(cols_done, 2)
            for c in range(NC):
                pe.transpose(m.ps[:, c * P:(c + 1) * P], turn[:, c * P:(c + 1) * P], m.ident)
            for h in range(MH):
                mm = pe.matmul(m.ps[:, 2 * BANK + h * NC:2 * BANK + (h + 1) * NC], sel(h), mdec[0:MH, :], start=True, stop=True)
            mm.then_inc(turned, 1)
            pe.wait_ge(cols_done, 7)

            def front(c, s):
                pe.wait_ge(kc_ready, c + 1)
                if not is_(c, 0):
                    pe.wait_ge(sw_ready, c)
                for h in range(MH):
                    mm = pe.matmul(heads(B(1))[:, h, :], qkc[s][:, MH + h, :], qkc[s][:, h, :], start=True, stop=True)
                mm.then_inc(s_done, 1)
                if not is_(c, 0):
                    pe.wait_ge(kw_ready, c)
                if not (isinstance(c, int) and c < 2):
                    pe.wait_ge(hm_ready, c - 1)
                for h in range(MH):
                    mm = pe.transpose(heads(B(0))[:, h, :], qkc[s][:, MH + h, :], m.ident)
                mm.then_inc(kt_done, 1)

            def tail(c):
                pe.wait_ge(hs_ready, c + 1)
                if isinstance(c, int):
                    pe.wait_ge(kw_ready, min(c + 3, NC))
                else:
                    pe.wait_ge(kw_ready, c + 3)
                if is_(c, NC - 1):
                    pe.wait_ge(hm_ready, c + 1)
                for h in range(MH):
                    mm = pe.transpose(heads(B(0))[:, h, :], hs[:, h, :], m.ident)
                mm.then_inc(ht_done, 1)

            def step(c, s):
                if not is_(c, NC - 1):
                    front(c + 1, 1 - s)
                pe.wait_ge(kw_ready, c + 1)
                if not is_(c, 0):
                    pe.wait_ge(state_ready, c)
                v = lambda h: m.vaug[:, bass.ds(c, 1), h, :].rearrange("p a n -> p (a n)")
                for h in range(MH):
                    mm = pe.matmul(slot(6, h), kw[s][:, h, :], v(h), start=True, stop=True)
                mm.then_inc(upd_done, 1)
                if not is_(c, 0):
                    pe.wait_ge(inter_ready, c)
                for h in range(MH):
                    mm = pe.matmul(slot(4, h), qkc[s][:, h, :], state[:, h, :], start=True, stop=True)
                mm.then_inc(inter_done, 1)
                pe.wait_ge(sw_ready, c + 1)
                if not is_(c, 0):
                    pe.wait_ge(num_ready, c)
                for h in range(MH):
                    mm = pe.matmul(slot(2, h), sw[s][:, h, :], v(h), start=True, stop=True)
                mm.then_inc(intra_done, 1)
                if not is_(c, 0):
                    tail(c - 1)

            front(0, 0)
            schedule(pe, step)
            tail(NC - 1)



SCALE = AQK ** -0.5
TURN = (6.28125, 1.93500518798828125e-3, 3.0192172958656e-7)
MAGIC = 1.5 * 2.0 ** 23
GROUPS = [0]
for _qb in range(TT):
    GROUPS.append(GROUPS[-1] + (_qb + 4) // 4)
NGRP, NPAIR = GROUPS[-1], TT // 2


def alloc_attention(nc, m, ctx):
    alloc = lambda name, shape, dt=F32: ctx.enter_context(nc.sbuf_tensor(name, shape, dt))
    m.cqhi, m.cqlo = alloc("cqhi", [P, 2, S], F32R), alloc("cqlo", [P, 2, S], F32R)
    m.ckhi, m.cklo = alloc("ckhi", [P, S], F32R), alloc("cklo", [P, S], F32R)
    m.wuq = alloc("wuq", [P, 2, AH, P])
    m.wkhi, m.wklo = alloc("wkhi", [P, AH * P], F32R), alloc("wklo", [P, AH * P], F32R)
    m.rot = alloc("rot", [P, S])
    m.q = [w[:, 0:S] for w in (m.whi[1], m.wlo[1])]
    m.k = [w[:, S:2 * S] for w in (m.whi[1], m.wlo[1])]
    m.vall = m.lat[:, :, :].rearrange("p a n -> p (a n)").rearrange("p (t n) -> p t n", t=TT)
    m.oa = m.qk[:, MH:2 * MH, :]


def stage_latents(nc, m, io):
    with ExitStack() as ctx:
        alloc = lambda name, shape, dt=F32: ctx.enter_context(nc.sbuf_tensor(name, shape, dt))
        sem = m.sem
        pos_i, pos = alloc("pos_i", [P, S], I32), alloc("pos", [P, S])
        ang, turns, sq = alloc("ang", [P, S]), alloc("turns", [P, S]), alloc("lat_sq", [P, 3, S])
        var, rinv, wkv = alloc("lat_var", [P, 2, S]), alloc("lat_rinv", [P, 2, S]), alloc("wkv", [P, AH * P])
        krt = alloc("krt", [P, S])
        log_ready = sem("lat_log_ready")
        pos_landed, wuq_landed, wkv_landed = sem("pos_landed"), sem("wuq_landed"), sem("wkv_landed")
        sq_ready, sum_done, var_ready, rinv_ready = sem("lat_sq_ready"), sem("lat_sum_done"), sem("lat_var_ready"), sem("lat_rinv_ready")
        lat_ready, lhi_ready, llo_ready = sem("lat_ready"), sem("lhi_ready"), sem("llo_ready")
        wk_hi, wk_lo, ang_ready, rot_ready, krt_ready, kr_done, krhi_ready = (
            sem("wk_hi"), sem("wk_lo"), sem("ang_ready"), sem("rot_ready"), sem("krt_ready"), sem("kr_done"), sem("krhi_ready"))
        v_done, v_ready, dve_own, pool_own = sem("v_done"), sem("v_ready"), sem("dve_own3"), sem("pool_own3")
        lo = slice(NOPE, P)
        block = ctx.enter_context(nc.Block("latents"))
        lats = [(m.lat[:, 0, :], ("g_q_lat", 0), 0, m.cqhi[:, 0, :], m.cqlo[:, 0, :]),
                (m.lat[:, 1, :], ("g_q_lat", 1), 0, m.cqhi[:, 1, :], m.cqlo[:, 1, :]),
                (m.lat[:, 2, :], ("g_kv_lat", 0), 1, m.ckhi[:, :], m.cklo[:, :])]

        @block.sync
        def _(sp):
            sp.dma_start(pos_i[lo, :], io.positions.partition_broadcast(P - NOPE)).then_inc(pos_landed, 16)
            sp.dma_start(wkv[:, :], io.w_ukv).then_inc(wkv_landed, 16)
            for k in range(2):
                sp.dma_start(m.wuq[:, k, :, 0:AQK], io.w_uq[k * P:(k + 1) * P, :].rearrange("p (h c) -> p h c", h=AH)).then_inc(wuq_landed, 16)

        @block.gpsimd
        def _(pool):
            pool.memset(m.rot[0:NOPE, :], 1.0).then_inc(pool_own, 1)
            half = ROPE // 2
            pool.wait_ge(wuq_landed, 32)
            for a, b in ((NOPE, NOPE + half), (NOPE + half, NOPE)):
                for k in range(2):
                    pool.tensor_copy(m.wuq[:, k, :, a + ROPE:a + ROPE + half], m.wuq[:, k, :, b:b + half]).then_inc(pool_own, 1)

        @block.scalar
        def _(act):
            for n in range(3):
                act.activation(sq[:, n, :], m.lat[:, n, :], ACT.Square).then_inc(sq_ready, 1)
            act.wait_ge(wkv_landed, 16)
            act.activation(m.wkhi[:, :], wkv[:, :], ACT.Copy).then_inc(wk_hi, 1)
            act.wait_ge(ang_ready, 1)
            act.activation(m.rot[lo, :], ang[lo, :], ACT.Sin).then_inc(rot_ready, 1)
            act.wait_ge(var_ready, 2)
            act.activation(var[:, :, :], var[:, :, :], ACT.Ln).then_inc(log_ready, 1)
            act.wait_ge(log_ready, 1)
            act.activation(rinv[:, :, :], var[:, :, :], ACT.Exp, scale=-0.5).then_inc(rinv_ready, 2)
            act.wait_ge(kr_done, 1)
            act.activation(m.k[0][lo, :], m.ps[lo, 4 * BANK:6 * BANK], ACT.Copy).then_inc(krhi_ready, 1)
            for n, (src, _, _, hi, _) in enumerate(lats):
                act.wait_ge(lat_ready, n + 1)
                act.activation(hi, src, ACT.Copy).then_inc(lhi_ready, 1)
            act.wait_ge(llo_ready, 3)
            for t in range(TT):
                act.wait_ge(v_done, t + 1)
                act.activation(m.vall[:, t, :], m.ps[:, (6 + t % 2) * BANK:(7 + t % 2) * BANK], ACT.Copy).then_inc(v_ready, 1)

        @block.vector
        def _(dve):
            own = Count(dve, dve_own)

            def step(ins):
                own.then(ins)
                own.wait()

            dve.wait_ge(wk_hi, 1)
            dve.tensor_tensor(m.wklo[:, :], wkv[:, :], m.wkhi[:, :], ALU.subtract).then_inc(wk_lo, 1)
            dve.wait_ge(pos_landed, 16)
            step(dve.tensor_copy(pos[lo, :], pos_i[lo, :]))
            c = lambda n: m.const[lo, K_COL + n:K_COL + n + 1]
            step(dve.tensor_scalar(ang[lo, :], pos[lo, :], c(0), None, ALU.mult))
            step(dve.tensor_scalar(turns[lo, :], ang[lo, :], 1 / (2 * np.pi), c(1), ALU.mult, ALU.add))
            step(dve.tensor_scalar(turns[lo, :], turns[lo, :], MAGIC, None, ALU.add))
            step(dve.tensor_scalar(turns[lo, :], turns[lo, :], MAGIC, None, ALU.subtract))
            for part in TURN:
                step(dve.scalar_tensor_tensor(out=ang[lo, :], in0=turns[lo, :], scalar=-part, in1=ang[lo, :], op0=ALU.mult, op1=ALU.add))
            step(dve.tensor_scalar(ang[lo, :], ang[lo, :], c(2), None, ALU.add))
            dve.tensor_scalar(ang[lo, :], ang[lo, :], 3.1415925, -3.1415925, ALU.min, ALU.max).then_inc(ang_ready, 1)
            for n, width in ((0, QR), (1, KVR)):
                dve.wait_ge(sum_done, n + 1)
                dve.tensor_scalar(var[:, n, :], m.ps[:, 2 * n * BANK:2 * (n + 1) * BANK], 1.0 / width, EPS, ALU.mult, ALU.add).then_inc(var_ready, 1)
            dve.wait_ge(rot_ready, 1)
            dve.tensor_tensor(krt[lo, :], m.lat[lo, 3, :], m.rot[lo, :], ALU.mult).then_inc(krt_ready, 1)
            dve.wait_ge(rinv_ready, 2)
            for src, g, n, _, _ in lats:
                dve.scalar_tensor_tensor(out=src, in0=src, scalar=col(m, *g), in1=rinv[:, n, :], op0=ALU.mult, op1=ALU.mult).then_inc(lat_ready, 1)
            dve.wait_ge(krhi_ready, 1)
            dve.tensor_tensor(m.k[1][lo, :], m.ps[lo, 4 * BANK:6 * BANK], m.k[0][lo, :], ALU.subtract).then_inc(dve_own, 1)
            for n, (src, _, _, hi, low) in enumerate(lats):
                dve.wait_ge(lhi_ready, n + 1)
                dve.tensor_tensor(low, src, hi, ALU.subtract).then_inc(llo_ready, 1)

        @block.tensor
        def _(pe):
            for n, ks in ((0, (0, 1)), (1, (2,))):
                pe.wait_ge(sq_ready, ks[-1] + 1)
                for half in range(2):
                    for k in ks:
                        mm = pe.matmul(m.ps[:, (2 * n + half) * BANK:(2 * n + half + 1) * BANK], m.ones[:, :],
                                       sq[:, k, half * BANK:(half + 1) * BANK], start=k == ks[0], stop=k == ks[-1])
                mm.then_inc(sum_done, 1)
            pe.wait_ge(krt_ready, 1)
            for half in range(2):
                mm = pe.matmul(m.ps[:, (4 + half) * BANK:(5 + half) * BANK], m.const[lo, K_FOLD:K_FOLD + P],
                               krt[lo, half * BANK:(half + 1) * BANK], start=True, stop=True)
            mm.then_inc(kr_done, 1)
            pe.wait_ge(wk_lo, 1)
            pe.wait_ge(llo_ready, 3)
            v = lambda w: w[:, :].rearrange("p (h n) -> p h n", h=AH)[:, :, NOPE:P]
            for t in range(TT):
                if t >= 2:
                    pe.wait_ge(v_ready, t - 1)
                for g, (x, w) in enumerate(((m.ckhi, m.wkhi), (m.ckhi, m.wklo), (m.cklo, m.wkhi))):
                    mm = pe.matmul(m.ps[:, (6 + t % 2) * BANK:(7 + t % 2) * BANK], x[:, t * P:(t + 1) * P], v(w),
                                   start=g == 0, stop=g == 2)
                mm.then_inc(v_done, 1)


def stage_attention(nc, m, io):
    with ExitStack() as ctx:
        alloc = lambda name, shape, dt=F32: ctx.enter_context(nc.sbuf_tensor(name, shape, dt))
        sem = m.sem
        sq = [alloc(f"stq{i}", [P, 2, P], F32R) for i in range(2)]
        sk = [alloc(f"stk{i}", [P, P], F32R) for i in range(2)]
        v = [alloc(f"vh{i}", [P, (TT + 1) * AV], F32R) for i in range(2)]
        qf = alloc("qf", [P, S])
        p = [alloc(f"prob{i}", [P, (TT // 2 + 1 + i) * P]) for i in range(4)]
        pt = [[alloc(f"probt{g}{i}", [P, TT - 2 + 2 * g, 2 * P], F32R) for i in range(2)] for g in range(2)]
        diag = alloc("diag", [P, 2, P])
        mx, nb, rs, rr = (alloc(n, [P, TT]) for n in ("mx", "nb", "rs", "rr"))
        init = sem("att_init")
        sq_hi, sq_lo, sk_ready, projq, projk = sem("sq_hi"), sem("sq_lo"), sem("sk_ready"), sem("projq"), sem("projk")
        qf_ready, q_hi, q_lo, k_hi, k_lo, v_hi, v_lo = (sem("qf_ready"), sem("q_hi"), sem("q_lo"), sem("k_hi"), sem("k_lo"), sem("vh_hi"), sem("vh_lo"))
        sc_done, masked, max_ready, nb_ready, e_ready, rr_ready, diag_ready = (
            sem("sc_done"), sem("masked"), sem("max_ready"), sem("nb_ready"), sem("e_ready"), sem("rr_ready"), sem("diag_ready"))
        t_done, th_ready, tl_ready, pv_done, oa_ready = sem("t_done"), sem("th_ready"), sem("tl_ready"), sem("pv_done"), sem("oa_ready")
        block = ctx.enter_context(nc.Block("attention"))
        B = lambda n, w=BANK: m.ps[:, n * BANK:n * BANK + w]

        def scores_of(qb):
            n = (qb + 1) * P
            b = 2 * (qb % 2)
            if n <= BANK:
                return B(b, n)
            return m.ps[:, b * BANK:(b + 2) * BANK].rearrange("p (a n) -> p a n", a=2)[:, :, 0:n // 2]

        def diagonal(qb):
            n = (qb + 1) * P
            end = 2 * (qb % 2) * BANK + (n if n <= BANK else BANK + n // 2)
            return m.ps[:, end - P:end]

        def prob(qb):
            n = (qb + 1) * P
            ap = p[qb % 4][:, 0:n]
            return ap if n <= BANK else ap.rearrange("p (a n) -> p a n", a=2)

        def groups(qb):
            return [(GROUPS[qb] + n, 4 * n, min(4, qb + 1 - 4 * n)) for n in range((qb + 4) // 4)]

        def turned(gi, nb_):
            return B(4 + gi % 2, nb_ * P).rearrange("p (j n) -> p j n", j=nb_)

        def pt_part(i, qb, j0, n):
            first = 2 * (qb // 2) + 2 - j0 - n
            return pt[(qb // 2) % 2][i][:, first:first + n, (qb % 2) * P:(qb % 2 + 1) * P]

        ORDER = dict(
            pe="S0 S1 X3 S2 T0 S3 T1 S4 T2 V0 S5 T3 S6 T4 V1 S7 T5 Q0 T6 K0 V2 T7",
            act="S0 S1 X3 S2 T0 S3 T1 W0 S4 T2 V0 S5 T3 S6 T4 V1 S7 T5 Q0 T6 K0 V2 T7",
            dve="S0 S1 H0 S2 H1 X3 T0 S3 H2 T1 W0 S4 H3 T2 S5 H4 T3 S6 H5 T4 S7 H6 T5 Q0 H7 T6 R0 K0 T7")

        def run(eng, order, start, parts):
            start()
            parts["X"] = parts["V"]

            def head(h, pair, odd):
                first, last = isinstance(h, int) and h == 0, isinstance(h, int) and h == AH - 1
                for o in ORDER[order].split():
                    if not (first and o[0] == "X" or last and o[0] in "WQRK"):
                        at = (h, pair, odd) if o[0] != "X" else (h - 1, pair if odd else pair - 1, 1 - odd)
                        parts[o[0]](*at, int(o[1]))

            head(0, 0, 0)
            with eng.Fori(0, (AH - 2) // 2) as i:
                head(i * 2 + 1, i, 1)
                head(i * 2 + 2, i + 1, 0)
            head(AH - 1, AH // 2 - 1, 1)
            parts["X"](AH - 1, AH // 2 - 1, 1, NPAIR - 1)

        @block.gpsimd
        def _(pool):
            for i in range(2):
                pool.memset(v[i][:, TT * AV:].bitcast(F32), 0.0).then_inc(init, 1)
                for g in range(2):
                    pool.memset(pt[g][i][:, 0, 0:P].bitcast(F32), 0.0).then_inc(init, 1)

        @block.scalar
        def _(act):
            def weights(h):
                act.activation(sq[0][:, :, :], m.wuq[:, :, bass.ds(h, 1), :].rearrange("p k a n -> p k (a n)"), ACT.Copy).then_inc(sq_hi, 1)
                for i, w in enumerate((m.wkhi, m.wklo)):
                    act.activation(sk[i][:, :], w[:, bass.ds(h * P, P)], ACT.Copy).then_inc(sk_ready, 1)

            def next_weights(h, pair, odd, _):
                act.wait_ge(projk, h + 1)
                weights(h + 1)

            def queries(h):
                act.wait_ge(qf_ready, h + 1)
                act.activation(m.q[0], qf[:, :], ACT.Copy).then_inc(q_hi, 1)

            def keys(h):
                act.wait_ge(projk, h + 1)
                act.activation(m.k[0][0:NOPE, :], m.ps[0:NOPE, 2 * BANK:4 * BANK], ACT.Copy).then_inc(k_hi, 1)

            def values(h):
                act.activation(v[0][:, 0:TT * AV].rearrange("p (t n) -> p t n", t=TT), m.vall[:, :, bass.ds(h * AV, AV)], ACT.Copy).then_inc(v_hi, 1)

            def start():
                weights(0)
                keys(0)
                queries(0)
                values(0)

            def exps(h, pair, odd, qb):
                act.wait_ge(nb_ready, h * TT + (qb + 1))
                act.wait_ge(t_done, h * NGRP + (GROUPS[qb - 3] + NGRP if qb >= 4 else GROUPS[qb + 5]))
                act.activation(prob(qb), scores_of(qb), ACT.Exp, bias=nb[:, qb:qb + 1], scale=SCALE,
                               accum_out=rs[:, qb:qb + 1]).then_inc(e_ready, 1)

            def hi(h, pair, odd, qb):
                if qb % 2 == 0:
                    act.wait_ge(pv_done, h * NPAIR + (qb // 2 - 1 + NPAIR))
                for gi, j0, n in groups(qb):
                    act.wait_ge(t_done, h * NGRP + (gi + 1 + NGRP))
                    act.activation(pt_part(0, qb, j0, n), turned(gi, n), ACT.Copy).then_inc(th_ready, 1)

            def out(h, pair, odd, g):
                act.wait_ge(pv_done, h * NPAIR + (g + 1 + NPAIR))
                dst = m.oa[odd * AV:(odd + 1) * AV, bass.ds(pair, 1), g * 2 * P:(g + 1) * 2 * P].rearrange("p a n -> p (a n)")
                act.activation(dst, m.ps[0:AV, (6 + g % 2) * BANK:(6 + g % 2) * BANK + 2 * P], ACT.Copy).then_inc(oa_ready, 1)
                if g == NPAIR - 1 and not (isinstance(h, int) and h == AH - 1):
                    values(h + 1)

            def q_next(h, pair, odd, _):
                act.wait_ge(sc_done, h * TT + TT)
                queries(h + 1)

            def k_next(h, pair, odd, _):
                act.wait_ge(sc_done, h * TT + TT)
                keys(h + 1)

            act.wait_ge(init, 6)
            act.sem_inc(th_ready, NGRP)
            act.sem_inc(oa_ready, NPAIR)
            run(act, "act", start, {"S": exps, "T": hi, "V": out, "W": next_weights, "Q": q_next, "K": k_next})

        @block.vector
        def _(dve):
            def weights(h):
                dve.wait_ge(sq_hi, h + 1)
                dve.tensor_tensor(sq[1][:, :, :], m.wuq[:, :, bass.ds(h, 1), :].rearrange("p k a n -> p k (a n)"), sq[0][:, :, :],
                                  ALU.subtract).then_inc(sq_lo, 1)

            def queries(h):
                dve.wait_ge(projq, h + 1)
                dve.tensor_tensor(qf[:, :], m.ps[:, 0:2 * BANK], m.rot[:, :], ALU.mult).then_inc(qf_ready, 1)

            def queries_lo(h):
                dve.wait_ge(q_hi, h + 1)
                dve.tensor_tensor(m.q[1], qf[:, :], m.q[0], ALU.subtract).then_inc(q_lo, 1)

            def keys(h):
                dve.wait_ge(k_hi, h + 1)
                dve.tensor_tensor(m.k[1][0:NOPE, :], m.ps[0:NOPE, 2 * BANK:4 * BANK], m.k[0][0:NOPE, :], ALU.subtract).then_inc(k_lo, 1)

            def values(h):
                dve.wait_ge(v_hi, h + 1)
                dve.tensor_tensor(v[1][:, 0:TT * AV].rearrange("p (t n) -> p t n", t=TT), m.vall[:, :, bass.ds(h * AV, AV)],
                                  v[0][:, 0:TT * AV].rearrange("p (t n) -> p t n", t=TT), ALU.subtract).then_inc(v_lo, 1)

            def maxima(h, pair, odd, qb):
                n = h * TT + (qb + 1)
                dve.wait_ge(sc_done, n)
                dve.tensor_tensor(diagonal(qb), diagonal(qb), m.const[:, K_QMASK:K_QMASK + P], ALU.add).then_inc(masked, 1)
                dve.wait_ge(masked, n)
                dve.tensor_reduce(mx[:, qb:qb + 1], scores_of(qb), AX.X if qb < 4 else AX.XY, ALU.max).then_inc(max_ready, 1)
                dve.wait_ge(max_ready, n)
                dve.tensor_scalar(nb[:, qb:qb + 1], mx[:, qb:qb + 1], -SCALE, None, ALU.mult).then_inc(nb_ready, 1)

            def shares(h, pair, odd, qb):
                dve.wait_ge(e_ready, h * TT + (qb + 1))
                dve.reciprocal(rr[:, qb:qb + 1], rs[:, qb:qb + 1]).then_inc(rr_ready, 1)
                dve.wait_ge(t_done, h * NGRP + (GROUPS[qb - 1] + NGRP if qb >= 2 else GROUPS[qb + 7]))
                dve.wait_ge(rr_ready, h * TT + (qb + 1))
                dve.tensor_scalar(diag[:, qb % 2, :], m.ident, rr[:, qb:qb + 1], None, ALU.mult).then_inc(diag_ready, 1)

            def lo(h, pair, odd, qb):
                for gi, j0, n in groups(qb):
                    dve.wait_ge(th_ready, h * NGRP + (gi + 1 + NGRP))
                    dve.tensor_tensor(pt_part(1, qb, j0, n), turned(gi, n), pt_part(0, qb, j0, n), ALU.subtract).then_inc(tl_ready, 1)

            def next_weights(h, pair, odd, _):
                dve.wait_ge(projq, h + 1)
                weights(h + 1)

            dve.sem_inc(tl_ready, NGRP)
            run(dve, "dve", lambda: (weights(0), queries(0), queries_lo(0), keys(0), values(0)),
                {"S": maxima, "H": shares, "T": lo, "V": lambda h, pair, odd, g: values(h + 1) if not isinstance(h, int) or h < AH - 1 else None,
                 "W": next_weights, "Q": lambda h, *_: queries(h + 1), "R": lambda h, *_: queries_lo(h + 1), "K": lambda h, *_: keys(h + 1)})

        @block.tensor
        def _(pe):
            def proj_q(h):
                pe.wait_ge(sq_lo, h + 1)
                for k in range(2):
                    for g, (w, x) in enumerate(((sq[0], m.cqhi), (sq[0], m.cqlo), (sq[1], m.cqhi))):
                        for half in range(2):
                            mm = pe.matmul(B(half), w[:, k, :], x[:, k, half * BANK:(half + 1) * BANK],
                                           start=(k == 0 and g == 0), stop=(k == 1 and g == 2))
                mm.then_inc(projq, 1)

            def proj_k(h):
                pe.wait_ge(sk_ready, h * 2 + 2)
                for g, (w, x) in enumerate(((sk[0], m.ckhi), (sk[0], m.cklo), (sk[1], m.ckhi))):
                    for half in range(2):
                        mm = pe.matmul(B(2 + half), w[:, :], x[:, half * BANK:(half + 1) * BANK], start=g == 0, stop=g == 2)
                mm.then_inc(projk, 1)

            def scores(h, pair, odd, qb):
                if qb < 2:
                    pe.wait_ge(q_lo, h + 1)
                    pe.wait_ge(k_lo, h + 1)
                else:
                    pe.wait_ge(e_ready, h * TT + (qb - 1))
                n = max((qb + 1) * P, 2 * P)
                pieces = [(0, n)] if n <= BANK else [(0, n // 2), (n // 2, n // 2)]
                for g, (a, b) in enumerate(((0, 0), (0, 1), (1, 0))):
                    for j, (c0, w) in enumerate(pieces):
                        mm = pe.matmul(B(2 * (qb % 2) + j, w), m.q[a][:, qb * P:(qb + 1) * P], m.k[b][:, c0:c0 + w],
                                       start=g == 0, stop=g == 2)
                mm.then_inc(sc_done, 1)

            def turn(h, pair, odd, qb):
                pe.wait_ge(diag_ready, h * TT + (qb + 1))
                for gi, j0, n in groups(qb):
                    pe.wait_ge(tl_ready, h * NGRP + (gi - 1 + NGRP))
                    for j in range(n):
                        mm = pe.matmul(B(4 + gi % 2)[:, (n - 1 - j) * P:(n - j) * P], p[qb % 4][:, (j0 + j) * P:(j0 + j + 1) * P],
                                       diag[:, qb % 2, :], start=True, stop=True)
                    mm.then_inc(t_done, 1)

            def values(h, pair, odd, g):
                pe.wait_ge(tl_ready, h * NGRP + (GROUPS[2 * g + 2] + NGRP))
                pe.wait_ge(v_lo, h + 1)
                pe.wait_ge(oa_ready, h * NPAIR + (g - 1 + NPAIR))
                nj = 2 * g + 2
                for j in range(nj):
                    for n, (a, b) in enumerate(((0, 0), (0, 1), (1, 0))):
                        mm = pe.matmul(B(6 + g % 2, 2 * P), v[a][:, j * AV:j * AV + P], pt[g % 2][b][:, nj - 1 - j, :],
                                       start=(j == 0 and n == 0), stop=(j == nj - 1 and n == 2))
                mm.then_inc(pv_done, 1)

            def q_next(h, pair, odd, _):
                pe.wait_ge(e_ready, h * TT + (TT - 1))
                proj_q(h + 1)

            def k_next(h, pair, odd, _):
                pe.wait_ge(e_ready, h * TT + TT)
                proj_k(h + 1)

            pe.sem_inc(t_done, NGRP)
            pe.sem_inc(pv_done, NPAIR)
            run(pe, "pe", lambda: (proj_q(0), proj_k(0)),
                {"S": scores, "T": turn, "V": values, "Q": q_next, "K": k_next})



Q_BRANCH = NZ // 2
Q_OUT = Q_BRANCH + 2
NOUT = D // PW
Q_FIN = Q_OUT + NOUT // 2
Q_FOUT = Q_FIN + FT // 2
HALF = S // 2


def stage_branches(nc, m, io):
    with ExitStack() as ctx:
        alloc = lambda name, shape, dt=F32, **kw: ctx.enter_context(nc.sbuf_tensor(name, shape, dt, **kw))
        sem = m.sem
        bhi, blo = alloc("bhi", [P, 2 * MH, S], F32R), alloc("blo", [P, 2 * MH, S], F32R)
        gate = alloc("gate", [P, 2, 2, S], side="right")
        b_hi, b_lo = sem("b_hi"), sem("b_lo")
        gate_landed = [[sem(f"gate_landed{s}{i}") for i in range(2)] for s in range(2)]
        b_done, b_drained, y_ready = sem("b_done"), sem("b_drained"), sem("y_ready")
        block = ctx.enter_context(nc.Block("branches"))
        pair = lambda t, s: m.ps[:, (4 * (t % 2) + 2 * s) * BANK:(4 * (t % 2) + 2 * s + 2) * BANK]

        @block.sync
        def _(sp):
            for s in range(2):
                load_panel(sp, m, Q_BRANCH + 1, s, io.branch_panel(m, 1, s))
            for s in range(2):
                load_panel(sp, m, Q_OUT, s, [(kn(m.raw[:, s, :]), cols_of(io.w_out, s * PW))])

        @block.gpsimd
        def _(pool):
            with pool.Fori(0, 2) as j:
                for t in range(4):
                    pool.wait_ge(y_ready, j * 4 + (t + 1))
                    for s in range(2):
                        pool.dma_start(gate[:, s, t % 2, :], io.gates[bass.ds(j * 4 + (s * KT + t), 1), :, :].rearrange(
                            "a p n -> p (a n)")).then_inc(gate_landed[s][t % 2], 16)

        @block.scalar
        def _(act):
            for k in range(2 * MH):
                act.activation(bhi[:, k, :], m.qk[:, k, :], ACT.Copy).then_inc(b_hi, 1)
                if k == MH - 1:
                    split_hi(act, m, Q_BRANCH, 1)
            for s in range(2):
                split_hi(act, m, Q_BRANCH + 1, s)

        @block.vector
        def _(dve):
            dve.sem_inc(b_drained, 4)
            dve.sem_inc(y_ready, 2)
            for k in range(2 * MH):
                dve.wait_ge(b_hi, k + 1)
                dve.tensor_tensor(blo[:, k, :], m.qk[:, k, :], bhi[:, k, :], ALU.subtract).then_inc(b_lo, 1)
                if k == MH - 1:
                    split_lo(dve, m, Q_BRANCH, 1)

            def merged(j, t):
                for s in range(2):
                    dve.wait_ge(b_done, j * 8 + (2 * t + s + 1))
                    dve.wait_ge(gate_landed[s][t % 2], j * 32 + 16 * (t // 2 + 1))
                    g = gate[:, s, t % 2, :]
                    dve.tensor_tensor(g, pair(t, s), g, ALU.mult).then_inc(b_drained, 1)
                dve.wait_ge(b_drained, j * 8 + (2 * t + 2 + 4))
                dve.tensor_tensor(m.y[:, bass.ds(j * 4 + t, 1), :].rearrange("p a n -> p (a n)"), gate[:, 0, t % 2, :],
                                  gate[:, 1, t % 2, :], ALU.add).then_inc(y_ready, 1)

            for t in range(4):
                merged(0, t)
            for s in range(2):
                split_lo(dve, m, Q_BRANCH + 1, s)
            for t in range(4):
                merged(1, t)

        @block.tensor
        def _(pe):
            with pe.Fori(0, 2) as j:
                for t in range(4):
                    for s in range(2):
                        if t == 0:
                            panel_ready(pe, m, j + Q_BRANCH, s)
                        pe.wait_ge(b_drained, j * 8 + (2 * t + s + 1))
                        for k in range(MH):
                            if t == 0:
                                pe.wait_ge(b_lo, MH * s + k + 1)
                            for g, (w, x) in enumerate(passes(m, s, bhi, blo)):
                                for half in range(2):
                                    mm = pe.matmul(pair(t, s)[:, half * BANK:(half + 1) * BANK], kn(w[:, :], MH)[:, k, t * P:(t + 1) * P],
                                                   x[:, MH * s + k, half * BANK:(half + 1) * BANK],
                                                   start=(k == 0 and g == 0), stop=(k == MH - 1 and g == 2))
                        mm.then_inc(b_done, 1)
                pe.wait_ge(b_done, j * 8 + 8)
                pe.sem_inc(m.w_used, 2)



def stage_out(nc, m, io):
    with ExitStack() as ctx:
        alloc = lambda name, shape, dt=F32, **kw: ctx.enter_context(nc.sbuf_tensor(name, shape, dt, **kw))
        sem = m.sem
        yhi, ylo = alloc("yhi", [P, KT, S], F32R), alloc("ylo", [P, KT, S], F32R)
        acc, gt1, tmp = alloc("ada_acc2", [P, 3 * D]), alloc("gt1", [P, D]), alloc("out_tmp", [P, 4, PW])
        acc_landed, gt1_landed, xr_landed = sem("acc_landed"), sem("b_gt1_landed"), [sem(f"xr_landed{i}") for i in range(4)]
        y_hi, y_lo, gt_done, gt1_ready, c_done = sem("y_hi"), sem("y_lo"), sem("gt1_done"), sem("gt1_ready"), sem("c2_done")
        o_done, o_drained, h_ready, dve_own = sem("o_done"), sem("o_drained"), sem("h_ready"), sem("dve_own5")
        block = ctx.enter_context(nc.Block("out"))
        quad = lambda n, a: m.ps[:, (4 * (n % 2) + 2 * a) * BANK:(4 * (n % 2) + 2 * a + 2) * BANK]

        @block.sync
        def _(sp):
            for s in range(2):
                load_panel(sp, m, Q_OUT + 1, s, [(kn(m.raw[:, s, :]), cols_of(io.w_out, (2 + s) * PW))])
            for s in range(2):
                load_panel(sp, m, Q_FIN, s, io.ffn_panel(m, s, s))

        @block.gpsimd
        def _(pool):
            pool.dma_start(acc[:, :], io.ada_acc[:, 0:3 * D]).then_inc(acc_landed, 16)
            pool.dma_start(gt1[:, :], io.b_ada[:, 2 * D:3 * D].partition_broadcast(P)).then_inc(gt1_landed, 16)
            for i in range(4):
                pool.wait_ge(y_lo, 2 * i + 2)
                pool.dma_start(m.y[:, 2 * i:2 * i + 2, :], io.x[i * 2 * P:(i + 1) * 2 * P, :].rearrange("(t p) n -> p t n", p=P)).then_inc(xr_landed[i], 16)

        @block.scalar
        def _(act):
            split_hi(act, m, Q_OUT, 0)
            for k in range(KT):
                act.activation(yhi[:, k, :], m.y[:, k, :], ACT.Copy).then_inc(y_hi, 1)
            for n in range(1, NOUT):
                split_hi(act, m, Q_OUT + n // 2, n % 2)

        @block.vector
        def _(dve):
            own = Count(dve, dve_own)
            split_lo(dve, m, Q_OUT, 0)
            for k in range(KT):
                dve.wait_ge(y_hi, k + 1)
                dve.tensor_tensor(ylo[:, k, :], m.y[:, k, :], yhi[:, k, :], ALU.subtract).then_inc(y_lo, 1)
            dve.wait_ge(gt_done, 1)
            dve.wait_ge(gt1_landed, 16)
            dve.tensor_tensor(gt1[:, :], m.ps[:, 4 * BANK:6 * BANK], gt1[:, :], ALU.add).then_inc(gt1_ready, 1)
            for i in range(4):
                dve.wait_ge(xr_landed[i], 16)
            for n in range(NOUT):
                if n + 1 < NOUT:
                    split_lo(dve, m, Q_OUT + (n + 1) // 2, (n + 1) % 2)
                dve.wait_ge(gt1_ready, 1)
                g = gt1[:, n * PW:(n + 1) * PW].rearrange("p (o n) -> p o n", o=1).to_broadcast([P, 4, PW])
                for a in range(2):
                    dve.wait_ge(o_done, 2 * n + a + 1)
                    own.wait()
                    dve.tensor_tensor(tmp[:, :, :], quad(n, a).rearrange("p (t n) -> p t n", t=4), g, ALU.mult).then_inc(o_drained, 1)
                    dve.wait_ge(o_drained, 2 * n + a + 1)
                    h = m.y[:, 4 * a:4 * a + 4, n * PW:(n + 1) * PW]
                    own.then(dve.tensor_tensor(h, h, tmp[:, :, :], ALU.add))
            dve.wait_ge(c_done, 1)
            adac = m.ps[:, 0:2 * KT * P].rearrange("p (j n) -> p j n", n=P)[:, :, 0]
            r = ROWS["b_ada"][0] + 3 * KT
            own.then(dve.tensor_tensor(m.aff[:, KT:2 * KT], adac[:, 0:KT], m.cols[:, r:r + KT], ALU.add))
            own.then(dve.tensor_tensor(m.aff[:, 0:KT], adac[:, KT:2 * KT], m.cols[:, r + KT:r + 2 * KT], ALU.add))
            own.wait()
            r = ROWS["g_ffn"][0]
            own.then(dve.scalar_tensor_tensor(out=m.aff[:, 0:KT], in0=m.aff[:, 0:KT], scalar=1.0, in1=m.cols[:, r:r + KT],
                                              op0=ALU.add, op1=ALU.mult))

        @block.tensor
        def _(pe):
            pe.wait_ge(acc_landed, 16)
            for half in range(2):
                mm = pe.matmul(m.ps[:, (4 + half) * BANK:(5 + half) * BANK], m.ones[:, :], acc[:, half * BANK:(half + 1) * BANK],
                               start=True, stop=True)
            mm.then_inc(gt_done, 1)
            for n in range(NOUT):
                panel_ready(pe, m, Q_OUT + n // 2, n % 2)
                for t in range(TT):
                    if n == 1 and t == 0:
                        pe.wait_ge(gt1_ready, 1)
                    if n >= 2 and t % 4 == 0:
                        pe.wait_ge(o_drained, 2 * n + t // 4 - 3)
                    b = 4 * (n % 2) * BANK + t * PW
                    for k in range(KT):
                        pe.wait_ge(y_lo, k + 1)
                        for g, (w, x) in enumerate(passes(m, n % 2, yhi, ylo)):
                            mm = pe.matmul(m.ps[:, b:b + PW], x[:, k, t * P:(t + 1) * P], kn(w[:, :])[:, k, :],
                                           start=(k == 0 and g == 0), stop=(k == KT - 1 and g == 2))
                    if t % 4 == 3:
                        mm.then_inc(o_done, 1)
                pe.wait_ge(o_done, 2 * n + 2)
                pe.sem_inc(m.w_used, 1)
            pe.wait_ge(o_drained, 2 * NOUT - 2)
            for j in range(2 * KT):
                mm = pe.matmul(m.ps[:, j * P:(j + 1) * P], acc[:, D + j * P:D + (j + 1) * P], m.ones[:, :], start=True, stop=True)
            mm.then_inc(c_done, 1)



def stage_norm(nc, m, io):
    with ExitStack() as ctx:
        alloc = lambda name, shape, dt=F32, **kw: ctx.enter_context(nc.sbuf_tensor(name, shape, dt, **kw))
        sem = m.sem
        hn, temp = alloc("hn", [P, TT, D]), alloc("norm_temp", [P, 2, S])
        h_stored, sq_done, var_ready, rms_ready, h_normed = sem("h_stored"), sem("sq2_done"), sem("var2_ready"), sem("rms2_ready"), sem("h_normed")
        h_turned, u_ready, uhi_ready, ulo_ready = sem("h_turned"), sem("u2_ready"), sem("u2hi_ready"), sem("u2lo_ready")
        block = ctx.enter_context(nc.Block("norm"))

        @block.sync
        def _(sp):
            sp.dma_start(io.h.rearrange("(t p) n -> p t n", p=P), m.y[:, :, :]).then_inc(h_stored, 16)
            sp.wait_ge(h_stored, 16)

        @block.gpsimd
        def _(pool):
            for a in range(2):
                c = slice(a * 4, a * 4 + 4)
                pool.wait_ge(sq_done, 4 * a + 4)
                pool.tensor_scalar(m.stat[:, c], m.stat[:, c], 1.0 / D, EPS, ALU.mult, ALU.add).then_inc(var_ready, 1)
                pool.wait_ge(var_ready, a + 1)
                pool.tensor_tensor(m.stat[:, TT + a * 4:TT + a * 4 + 4], m.stat[:, c], m.neghalf[:, 0:4], ALU.pow).then_inc(rms_ready, 1)

        @block.scalar
        def _(act):
            for t in range(TT):
                if t >= 2:
                    act.wait_ge(sq_done, t - 1)
                act.activation(temp[:, t % 2, :], m.y[:, t, :], ACT.Square, accum_out=m.stat[:, t:t + 1]).then_inc(sq_done, 1)
            split_hi(act, m, Q_FIN, 0, ffn_parts(0, 0))
            act.wait_ge(sq_done, TT)
            for k in range(KT):
                act.wait_ge(h_turned, k + 1)
                if k >= 2:
                    act.wait_ge(ulo_ready, k - 1)
                b = 2 * (k % 4) * BANK
                act.activation(temp[:, k % 2, :], m.ps[:, b:b + S], ACT.Identity,
                               scale=m.aff[:, k:k + 1], bias=m.aff[:, KT + k:KT + k + 1]).then_inc(u_ready, 1)

        @block.vector
        def _(dve):
            for t in range(TT):
                dve.wait_ge(rms_ready, t // 4 + 1)
                dve.tensor_scalar(hn[:, t, :], m.y[:, t, :], m.stat[:, TT + t:TT + t + 1], None, ALU.mult).then_inc(h_normed, 1)
            split_lo(dve, m, Q_FIN, 0)
            for k in range(KT):
                dve.wait_ge(u_ready, k + 1)
                dve.tensor_copy(m.u2hi[:, k, :], temp[:, k % 2, :]).then_inc(uhi_ready, 1)
                dve.wait_ge(uhi_ready, k + 1)
                dve.tensor_tensor(m.u2lo[:, k, :], temp[:, k % 2, :], m.u2hi[:, k, :], ALU.subtract).then_inc(ulo_ready, 1)

        @block.tensor
        def _(pe):
            for k in range(KT):
                if k >= 4:
                    pe.wait_ge(u_ready, k - 3)
                for t in range(TT):
                    if k == 0:
                        pe.wait_ge(h_normed, t + 1)
                    b = 2 * (k % 4) * BANK + t * P
                    mm = pe.transpose(m.ps[:, b:b + P], hn[:, t, k * P:(k + 1) * P], m.ident)
                mm.then_inc(h_turned, 1)



def stage_hidden(nc, m, io):
    with ExitStack() as ctx:
        sem = m.sem
        f_done, sig_ready, g_ready, f_drained = sem("f_done"), sem("sig_ready"), sem("g_ready"), sem("f_drained")
        block = ctx.enter_context(nc.Block("hidden"))
        pair = lambda s, a: m.ps[:, (4 * s + 2 * a) * BANK:(4 * s + 2 * a + 2) * BANK]
        tile = lambda n: m.hidden[:, bass.ds(n, 1), :].rearrange("p a n -> p (a n)")

        @block.sync
        def _(sp):
            with sp.Fori(1, FT // 2) as i:
                for s in range(2):
                    load_panel(sp, m, i + Q_FIN, s, io.ffn_panel(m, s, i * 2 + s))
            for s in range(2):
                load_panel(sp, m, Q_FOUT, s, [io.ffn_out_panel(m, s, s)])

        @block.scalar
        def _(act):
            def step(i, s, last=False):
                split_hi(act, m, i + (Q_FIN + s), 1 - s, None if last else ffn_parts(i + s, 1 - s))
                act.wait_ge(f_done, i * 4 + (2 * s + 1))
                act.activation(tile(i * 2 + s), pair(s, 0), ACT.Sigmoid).then_inc(sig_ready, 1)

            with act.Fori(0, FT // 2 - 1) as i:
                step(i, 0)
                step(i, 1)
            step(FT // 2 - 1, 0)
            step(FT // 2 - 1, 1, last=True)

        @block.vector
        def _(dve):
            dve.sem_inc(f_drained, 2)
            with dve.Fori(0, FT // 2) as i:
                for s in range(2):
                    split_lo(dve, m, i + (Q_FIN + s), 1 - s)
                    dve.wait_ge(sig_ready, i * 2 + (s + 1))
                    h = tile(i * 2 + s)
                    dve.tensor_tensor(h, pair(s, 0), h, ALU.mult).then_inc(g_ready, 1)
                    dve.wait_ge(g_ready, i * 2 + (s + 1))
                    dve.wait_ge(f_done, i * 4 + (2 * s + 2))
                    dve.tensor_tensor(h, pair(s, 1), h, ALU.mult).then_inc(f_drained, 1)

        @block.tensor
        def _(pe):
            with pe.Fori(0, FT // 2) as i:
                for s in range(2):
                    panel_ready(pe, m, i + Q_FIN, s)
                    pe.wait_ge(f_drained, i * 2 + (s + 1))
                    for a in range(2):
                        for k in range(KT):
                            for g, (w, x) in enumerate(passes(m, s, m.u2hi, m.u2lo)):
                                for half in range(2):
                                    mm = pe.matmul(pair(s, a)[:, half * BANK:(half + 1) * BANK], kn(w[:, :])[:, k, a * P:(a + 1) * P],
                                                   x[:, k, half * BANK:(half + 1) * BANK],
                                                   start=(k == 0 and g == 0), stop=(k == KT - 1 and g == 2))
                        mm.then_inc(f_done, 1)
                    pe.wait_ge(f_done, i * 4 + (2 * s + 2))
                    pe.sem_inc(m.w_used, 1)



def stage_final(nc, m, io):
    NP = FT // 2
    QT = TT // 2
    with ExitStack() as ctx:
        alloc = lambda name, shape, dt=F32, **kw: ctx.enter_context(nc.sbuf_tensor(name, shape, dt, **kw))
        sem = m.sem
        hhi = [alloc(f"hid_hi{i}", [P, 2, HALF], F32R) for i in range(2)]
        hlo = [alloc(f"hid_lo{i}", [P, 2, HALF], F32R) for i in range(2)]
        acc, gt2, gfin = alloc("gt2_acc", [P, D]), alloc("gt2", [P, D]), alloc("gfin", [P, D])
        h, tmp = alloc("h_half", [P, QT, D]), alloc("fin_tmp", [P, QT, D])
        acc_landed, gt2_landed, gfin_landed = sem("acc2_landed"), sem("b_gt2_landed"), sem("gfin_landed")
        hr_landed, hid_hi, hid_lo, out_stored = sem("hr_landed"), sem("hid_hi"), sem("hid_lo"), [sem("out_stored0"), sem("out_stored1")]
        gt_done, gt2_ready, p_done, d_drained, h2_ready = sem("gt2_done"), sem("gt2_ready"), sem("fo_done"), sem("d_drained"), sem("h2_ready")
        t_done = sem("fo_tile_done")
        sq_done, var_ready, rms_ready, out_ready = sem("sq3_done"), sem("var3_ready"), sem("rms3_ready"), sem("out_ready")
        block = ctx.enter_context(nc.Block("final"))
        rows = lambda t: m.ps[:, 2 * t * BANK:2 * (t + 1) * BANK]

        def over_panels(eng, step, drain=lambda hf: None, finish=lambda hf: None):
            step(0, 0, 0, 0, 0)
            step(1, 0, 1, 1, 0)
            with eng.Fori(1, NP // 2) as i:
                step(i * 2, i, 0, i * 2, 0)
                step(i * 2 + 1, i, 1, i * 2 + 1, 0)
            step(NP - 1, NP // 2, 0, NP - 1, 0)
            drain(0)
            step(NP, NP // 2, 1, 0, 1)
            finish(0)
            with eng.Fori(NP // 2 + 1, NP - 1) as i:
                step(i * 2, i, 0, i * 2 - NP, 1)
                step(i * 2 + 1, i, 1, i * 2 + (1 - NP), 1)
            step(FT - 2, NP - 1, 0, NP - 2, 1)
            step(FT - 1, NP - 1, 1, NP - 1, 1)
            drain(1)
            finish(1)

        @block.sync
        def _(sp):
            def step(n, q, s, p, hf):
                if not (isinstance(n, int) and n < 2):
                    load_panel(sp, m, q + Q_FOUT, s, [io.ffn_out_panel(m, s, p)])

            def store(hf):
                for t in range(QT):
                    sp.wait_ge(out_ready, QT * hf + t + 1)
                    r = (hf * QT + t) * P
                    sp.dma_start(io.out[r:r + P, :], tmp[:, t, :]).then_inc(out_stored[hf], 16)

            over_panels(sp, step, finish=store)
            for hf in range(2):
                sp.wait_ge(out_stored[hf], 16 * QT)

        @block.gpsimd
        def _(pool):
            pool.dma_start(acc[:, :], io.ada_acc[:, 3 * D:4 * D]).then_inc(acc_landed, 16)
            pool.dma_start(gt2[:, :], io.b_ada[:, 5 * D:6 * D].partition_broadcast(P)).then_inc(gt2_landed, 16)
            pool.dma_start(gfin[:, :], io.g_final.partition_broadcast(P)).then_inc(gfin_landed, 16)
            for hf in range(2):
                if hf:
                    pool.wait_ge(h2_ready, QT)
                pool.dma_start(h[:, :, :], io.h[hf * HALF:(hf + 1) * HALF, :].rearrange("(t p) n -> p t n", p=P)).then_inc(hr_landed, 16)
                for t in range(QT):
                    n = QT * hf + t
                    pool.wait_ge(sq_done, n + 1)
                    ss = m.stat[:, t:t + 1]
                    pool.tensor_scalar(ss, ss, 1.0 / D, EPS, ALU.mult, ALU.add).then_inc(var_ready, 1)
                    pool.wait_ge(var_ready, n + 1)
                    pool.tensor_tensor(m.stat[:, TT + t:TT + t + 1], ss, m.neghalf[:, 0:1], ALU.pow).then_inc(rms_ready, 1)

        @block.scalar
        def _(act):
            def step(n, q, s, p, hf):
                if not (isinstance(n, int) and n == 0):
                    split_hi(act, m, q + Q_FOUT, s)
                if not (isinstance(n, int) and n < 2):
                    act.wait_ge(m.w_used, n + 2 * Q_FOUT)
                sl = hf * HALF
                act.activation(hhi[s][:, :, :], m.hidden[:, bass.ds(p * 2, 2), sl:sl + HALF], ACT.Copy).then_inc(hid_hi, 1)

            def finish(hf):
                for t in range(QT):
                    act.wait_ge(h2_ready, QT * hf + t + 1)
                    if hf or t:
                        act.wait_ge(sq_done, QT * hf + t)
                    if hf:
                        act.wait_ge(rms_ready, t + 1)
                    act.activation(acc[:, :], tmp[:, t, :], ACT.Square, accum_out=m.stat[:, t:t + 1]).then_inc(sq_done, 1)

            over_panels(act, step, finish=finish)

        @block.vector
        def _(dve):
            dve.wait_ge(gt_done, 1)
            dve.wait_ge(gt2_landed, 16)
            dve.tensor_tensor(gt2[:, :], m.ps[:, 0:2 * BANK], gt2[:, :], ALU.add).then_inc(gt2_ready, 1)
            dve.wait_ge(gt2_ready, 1)
            dve.wait_ge(gfin_landed, 16)

            def step(n, q, s, p, hf):
                if not (isinstance(n, int) and n == 0):
                    split_lo(dve, m, q + Q_FOUT, s)
                dve.wait_ge(hid_hi, n + 1)
                if not (isinstance(n, int) and n < 2):
                    dve.wait_ge(m.w_used, n + 2 * Q_FOUT)
                sl = hf * HALF
                dve.tensor_tensor(hlo[s][:, :, :], m.hidden[:, bass.ds(p * 2, 2), sl:sl + HALF], hhi[s][:, :, :], ALU.subtract).then_inc(hid_lo, 1)

            def drain_tile(hf, t):
                dve.wait_ge(t_done, QT * hf + t + 1)
                dve.tensor_tensor(tmp[:, t, :], rows(t), gt2[:, :], ALU.mult).then_inc(d_drained, 1)

            def residual(hf, t):
                dve.wait_ge(d_drained, QT * hf + t + 1)
                dve.tensor_tensor(tmp[:, t, :], tmp[:, t, :], h[:, t, :], ALU.add).then_inc(h2_ready, 1)

            def scaled(hf, t):
                dve.wait_ge(rms_ready, QT * hf + t + 1)
                dve.scalar_tensor_tensor(out=tmp[:, t, :], in0=tmp[:, t, :], scalar=m.stat[:, TT + t:TT + t + 1], in1=gfin[:, :],
                                         op0=ALU.mult, op1=ALU.mult).then_inc(out_ready, 1)

            def drain(hf):
                if hf:
                    dve.wait_ge(out_stored[0], 16 * QT)
                    dve.wait_ge(hr_landed, 16 * 2)
                for t in range(QT):
                    drain_tile(hf, t)
                    if hf:
                        residual(hf, t)
                        if t:
                            scaled(hf, t - 1)

            def finish(hf):
                if hf:
                    scaled(hf, QT - 1)
                    return
                dve.wait_ge(hr_landed, 16)
                for t in range(QT):
                    residual(hf, t)
                for t in range(QT):
                    scaled(hf, t)

            over_panels(dve, step, drain, finish)

        @block.tensor
        def _(pe):
            pe.wait_ge(acc_landed, 16)
            for half in range(2):
                mm = pe.matmul(m.ps[:, half * BANK:(half + 1) * BANK], m.ones[:, :], acc[:, half * BANK:(half + 1) * BANK], start=True, stop=True)
            mm.then_inc(gt_done, 1)
            pe.wait_ge(gt2_ready, 1)

            def step(n, q, s, p, hf):
                first, last = isinstance(p, int) and p == 0, isinstance(p, int) and p == NP - 1
                panel_ready(pe, m, q + Q_FOUT, s)
                pe.wait_ge(hid_lo, n + 1)
                for t in range(QT):
                    if first and hf:
                        pe.wait_ge(d_drained, t + 1)
                    for k in range(2):
                        for g, (w, x) in enumerate(passes(m, s, hhi[s], hlo[s])):
                            for half in range(2):
                                mm = pe.matmul(rows(t)[:, half * BANK:(half + 1) * BANK], x[:, k, t * P:(t + 1) * P],
                                               kn(w[:, :], 2)[:, k, half * BANK:(half + 1) * BANK],
                                               start=first and k == 0 and g == 0, stop=last and k == 1 and g == 2)
                    if last:
                        mm.then_inc(t_done, 1)
                if last:
                    pe.wait_ge(t_done, QT * hf + QT)
                    pe.sem_inc(p_done, 1)
                else:
                    mm.then_inc(p_done, 1)
                pe.wait_ge(p_done, n + 1)
                pe.sem_inc(m.w_used, 1)

            over_panels(pe, step)


def program(nc, io, upto=9):
    with ExitStack() as ctx:
        m = Record()
        m.stage_sems = []

        def sem(name):
            m.stage_sems.append(nc.alloc_semaphore(name))
            return m.stage_sems[-1]

        def stage(function):
            m.stage_sems = []
            function(nc, m, io)
            nc.clear_and_free_semaphores(m.stage_sems)
            nc.all_engine_barrier()

        m.sem = sem
        alloc = lambda name, shape, dt=F32: ctx.enter_context(nc.sbuf_tensor(name, shape, dt))
        m.raw = alloc("raw", [P, 2, PANEL])
        m.whi = [alloc(f"whi{s}", [P, PANEL], F32R) for s in range(2)]
        m.wlo = [alloc(f"wlo{s}", [P, PANEL], F32R) for s in range(2)]
        m.raw_landed, m.w_hi, m.w_lo, m.w_used = [m.sem("raw_landed0"), m.sem("raw_landed1")], m.sem("w_hi"), m.sem("w_lo"), m.sem("w_used")
        m.parts_landed = [m.sem("parts_landed0"), m.sem("parts_landed1")]
        m.const = alloc("const", [P, NCONST])
        m.ident = m.const[:, K_ID:K_ID + P]
        m.rows, m.cols, m.ones = alloc("rows", [P, P]), alloc("cols", [P, P]), alloc("ones", [P, P])
        m.bif, m.csil = alloc("bif", [P, 2]), alloc("csil", [P, KT])
        m.stat, m.neghalf = alloc("stat", [P, 4 * TT]), alloc("neghalf", [P, 4 * TT])
        m.aff = alloc("aff", [P, 2 * KT])
        m.ps = ctx.enter_context(nc.psum_tensor("ps", [P, 8 * BANK], F32))
        with ExitStack() as early:
            tmp = lambda name, shape: early.enter_context(nc.sbuf_tensor(name, shape, F32))
            m.xs, m.ada_raw, m.ada_acc = tmp("xs", [P, TT, D]), tmp("ada_raw", [P, 4, ADA1]), tmp("ada_acc", [P, ADA1])
        late = ctx.enter_context(ExitStack())
        with ExitStack() as heads:
            tmp = lambda name, shape: heads.enter_context(nc.sbuf_tensor(name, shape, F32))
            m.qk = tmp("qk", [P, 2 * MH, S])
            with ExitStack() as lats:
                m.lat = lats.enter_context(nc.sbuf_tensor("lat", [P, 4, S], F32))
                with ExitStack() as inner:
                    tmp = lambda name, shape: inner.enter_context(nc.sbuf_tensor(name, shape, F32))
                    m.vaug, m.osig = tmp("vaug", [P, TT, MH, VA]), tmp("osig", [P, MH, S])
                    stage(stage_project)
                    if upto == 1:
                        return m
                    stage(stage_mlstm)
                if upto == 2:
                    return m
                with ExitStack() as inner:
                    alloc_attention(nc, m, inner)
                    stage(stage_latents)
                    if upto == 3:
                        return m
                    stage(stage_attention)
                if upto == 4:
                    return m
            m.y = late.enter_context(nc.sbuf_tensor("y", [P, KT, S], F32, side="right"))
            stage(stage_branches)
            if upto == 5:
                return m
        stage(stage_out)
        if upto == 6:
            return m
        with ExitStack() as inner:
            m.u2hi = inner.enter_context(nc.sbuf_tensor("u2hi", [P, KT, S], F32R))
            m.u2lo = inner.enter_context(nc.sbuf_tensor("u2lo", [P, KT, S], F32R))
            stage(stage_norm)
            late.close()
            m.hidden = ctx.enter_context(nc.sbuf_tensor("hidden", [P, FT, S], F32, side="right"))
            stage(stage_hidden)
        if upto == 7:
            return m
        stage(stage_final)
        return m


def build(nc, args, out, upto=9):
    io = Record()
    flat = lambda name, n: args[name].rearrange("a (r c) -> (a r) c", c=P)
    io.rows = [("c", flat("c", 0))] + [(n, flat(n, 0)) for n in ("b_ada", "g_mix", "g_ffn")] + [
        ("conv_w", args["conv_w"].rearrange("a j (r c) -> (a j r) c", c=P))] + [
        (n, flat(n, 0)) for n in ("conv_b", "g_mhead", "g_q_lat", "g_kv_lat")]
    io.const = args["constants"]
    io.b_igate, io.b_fgate = (args[n].rearrange("a (h o) -> (a h) o", o=1) for n in ("b_igate", "b_fgate"))
    (io.x, io.w_ada, io.w_in, io.w_uq, io.w_ukv, io.w_branch_m, io.w_branch_a, io.w_out, io.w_ffn_in, io.w_ffn_out) = (
        args[n].rearrange("a b c -> (a b) c")
        for n in ("x", "w_ada", "w_in", "w_uq", "w_ukv", "w_branch_m", "w_branch_a", "w_out", "w_ffn_in", "w_ffn_out"))
    io.gates = nc.dram_tensor("gates", [2 * KT, P, S], F32, kind="Internal").ap()

    def branch_panel(m, j, s):
        return [(kn(m.raw[:, s, :], MH), cols_of((io.w_branch_m, io.w_branch_a)[s], j * BANK, BANK))]

    io.branch_panel = branch_panel

    def ffn_panel(m, s, n):
        return [(kn(m.raw[:, s, :])[:, :, a * P:(a + 1) * P], cols_of(io.w_ffn_in, n * P + a * FF, P)) for a in range(2)]

    def ffn_out_panel(m, s, n):
        return kn(m.raw[:, s, :], 2), io.w_ffn_out[bass.ds(n * (2 * P), 2 * P), :].rearrange("(k p) c -> p k c", p=P)

    io.ffn_panel, io.ffn_out_panel = ffn_panel, ffn_out_panel
    io.ada_acc = nc.dram_tensor("ada_sums", [P, 4 * D], F32, kind="Internal").ap()
    io.h = nc.dram_tensor("h_mid", [S, D], F32, kind="Internal").ap()
    io.b_ada = args["b_ada"]
    io.positions, io.g_final = args["positions"], args["g_final"].rearrange("(o n) -> o n", o=1)
    io.out = out.rearrange("a b c -> (a b) c")
    return program(nc, io, upto)


_INS = ["x", "c", "positions", "w_ada", "b_ada", "g_mix", "w_in", "conv_w", "conv_b", "b_igate", "b_fgate", "g_mhead",
        "g_q_lat", "w_uq", "g_kv_lat", "w_ukv", "w_branch_m", "w_branch_a", "w_out", "g_ffn", "w_ffn_in", "w_ffn_out",
        "g_final"]


def kernel(**inputs):
    import numpy as _np
    import concourse.bacc as _bacc
    from concourse import mybir as _mybir
    from concourse.bass_utils import run_bass_kernel_spmd as _run

    nc = _bacc.Bacc("TRN2", target_bir_lowering=False, num_devices=1)
    given = {name: _np.ascontiguousarray(inputs[name]) for name in _INS}
    given["constants"] = constants()
    arrays = {f"in_{name}_dram": a for name, a in given.items()}
    args = {name: nc.dram_tensor(f"in_{name}_dram", a.shape, _mybir.dt.from_np(a.dtype), kind="ExternalInput").ap()
            for name, a in given.items()}
    out = nc.dram_tensor("out_0_dram", (1, S, D), F32, kind="ExternalOutput").ap()
    build(nc, args, out)
    r = _run(nc, [arrays], core_ids=[0])
    return r.results[0]["out_0_dram"]
```

```python
from contextlib import ExitStack

import numpy as np

import concourse.bass as bass
from concourse import mybir

F32, F32R, I32 = mybir.dt.float32, mybir.dt.float32r, mybir.dt.int32
ALU, ACT, AX = mybir.AluOpType, mybir.ActivationFunctionType, mybir.AxisListType

P = 128
BANK = 512
S = 1024
D = 1024
TT = S // P
KT = D // P
MH, MD = 4, 128
MW = MH * MD
CONV = 4
VA = MD + 2
AH, NOPE, ROPE, AV = 8, 64, 32, 64
AQK = NOPE + ROPE
QR, KVR = 256, 128
AW = AH * AV
FF = ((8 * D + 3 * 256 - 1) // (3 * 256)) * 256
FT = FF // P
EPS = 1e-6
NEG = -1e30
PW = 256
PANEL = KT * PW

C_V, C_O, C_I, C_F = 2 * MW, 3 * MW, 4 * MW, 4 * MW + MH
C_QL = C_F + MH
C_KVL = C_QL + QR
C_KR = C_KVL + KVR
C_GATE = C_KR + ROPE

ROWS = {}
for _name, _n in (("c", KT), ("b_ada", 6 * KT), ("g_mix", KT), ("g_ffn", KT), ("conv_w", CONV * 2 * MH),
                  ("conv_b", 2 * MH), ("g_mhead", MH), ("g_q_lat", QR // P), ("g_kv_lat", KVR // P)):
    ROWS[_name] = (sum(n for _, n in ROWS.values()), _n)
NROWS = sum(n for _, n in ROWS.values())

K_ID, K_QMASK, K_TMASK, K_FOLD, K_SEL = 0, P, 2 * P, 3 * P, 4 * P
K_COL = K_SEL + MH * P
NCONST = K_COL + 3 + 2 * MH


def constants():
    t = np.zeros((P, NCONST), np.float32)
    r = np.arange(P)
    t[:, K_ID:K_ID + P] = np.eye(P)
    t[:, K_QMASK:K_QMASK + P] = np.where(r[None, :] <= r[:, None], 0, NEG)
    t[:, K_TMASK:K_TMASK + P] = np.where(r[:, None] <= r[None, :], 0, NEG)
    t[:, K_FOLD:K_FOLD + P] = (r[:, None] >= NOPE) & (r[None, :] >= NOPE) & ((r[:, None] - r[None, :]) % ROPE == 0)
    for h in range(MH):
        t[[h, 32 + h], K_SEL + h * P:K_SEL + (h + 1) * P] = 1
    inv = np.float32(10000.0) ** (-np.arange(0, ROPE, 2, dtype=np.float32) / np.float32(ROPE))
    t[NOPE:, K_COL] = inv[r[NOPE:] % (ROPE // 2)]
    turns = np.zeros(P)
    turns[NOPE:NOPE + ROPE] = 0.25
    turns[NOPE + ROPE:NOPE + ROPE + ROPE // 2] = 0.5
    t[:, K_COL + 1] = turns
    t[:, K_COL + 2] = turns * 2 * np.pi
    t[:, K_COL + 3:K_COL + 3 + 2 * MH] = np.repeat([MD ** -0.5, 1.0], MH)
    return t


class Record:
    pass


class Count:

    def __init__(self, eng, sem):
        self.eng, self.sem, self.n, self.var, self.per = eng, sem, 0, None, 0

    def loop(self, var, per):
        self.start, self.var, self.per = self.n, var, per

    def end(self, iterations):
        assert self.n - self.start == self.per, (self.n - self.start, self.per)
        self.n, self.var = self.start + self.per * iterations, None

    def value(self):
        return self.n if self.var is None else self.var * self.per + self.n

    def then(self, ins):
        ins.then_inc(self.sem, 1)
        self.n += 1
        return ins

    def wait(self):
        self.eng.wait_ge(self.sem, self.value())


def col(m, name, n=0):
    return m.cols[:, bass.ds(ROWS[name][0] + n, 1)]



SPEC_PARTS = 5 * 16


def load_panel(sp, m, q, s, parts, first=False):
    if not first:
        sp.wait_ge(m.w_hi, q * 2 + (s - 1))
        sp.wait_ge(m.w_lo, q * 2 + (s - 1))
    for n, (dst, src) in enumerate(parts):
        sp.dma_start(dst, src).then_inc(m.parts_landed[s] if n else m.raw_landed[s], 16)


def split_hi(act, m, q, s, parts=None):
    act.wait_ge(m.raw_landed[s], q * 16 + 16)
    if parts is not None:
        act.wait_ge(m.parts_landed[s], parts)
    if not (s == 0 and isinstance(q, int) and q == 0):
        act.wait_ge(m.w_used, q * 2 + s)
    act.activation(m.whi[s][:, :], m.raw[:, s, :], ACT.Copy).then_inc(m.w_hi, 1)


def split_lo(dve, m, q, s):
    dve.wait_ge(m.w_hi, q * 2 + (s + 1))
    if not (s == 0 and isinstance(q, int) and q == 0):
        dve.wait_ge(m.w_used, q * 2 + s)
    dve.tensor_tensor(m.wlo[s][:, :], m.raw[:, s, :], m.whi[s][:, :], ALU.subtract).then_inc(m.w_lo, 1)


def ffn_parts(i, s):
    return i * 16 + (16 + SPEC_PARTS * s)


def panel_ready(pe, m, q, s):
    pe.wait_ge(m.w_hi, q * 2 + (s + 1))
    pe.wait_ge(m.w_lo, q * 2 + (s + 1))


def kn(ap, k=KT):
    return ap.rearrange("p (k n) -> p k n", k=k)


def cols_of(w, c0, n=PW):
    return w[:, bass.ds(c0, n)].rearrange("(k p) c -> p k c", p=P)


def passes(m, s, xhi, xlo):
    return (m.whi[s], xhi), (m.whi[s], xlo), (m.wlo[s], xhi)



NQK, NV, NO, NL, NG = 4, 2, 2, 2, 8
ADA1 = 2 * D
NZ = NQK + NV + NO + NL + NG
ACC = P
PIECES = 4 * D // ACC // NG


def stage_project(nc, m, io):
    with ExitStack() as ctx:
        alloc = lambda name, shape, dt=F32: ctx.enter_context(nc.sbuf_tensor(name, shape, dt))
        uhi, ulo = alloc("uhi", [P, KT, S], F32R), alloc("ulo", [P, KT, S], F32R)
        conv = alloc("conv", [P, 2, S + CONV])
        temp = conv[:, :, CONV:CONV + S]
        acc_raw = temp[:, 1, :].rearrange("p (a k n) -> p a k n", a=2, k=KT // 2)
        acc_sum = alloc("acc_sum", [P, 2, ACC])
        acc_landed, acc_stored = ([m.sem(f"{n}{i}") for i in range(2)] for n in ("accr_landed", "acc_stored"))
        acc_step = m.sem("acc_step")
        csig = alloc("csig", [P, KT])
        sem = m.sem
        c_landed, ident_landed, c_turned = sem("c_landed"), sem("ident_landed"), sem("c_turned")
        rows_landed, const_landed, ones_ready = sem("rows_landed"), sem("const_landed"), sem("ones_ready")
        ada_landed, ada_used = [sem(f"ada_landed{i}") for i in range(4)], sem("ada_used")
        x_landed = [sem(f"x_landed{i}") for i in range(4)]
        rows_zeroed, cols_turned, cols_ready, c_sig = sem("rows_zeroed"), sem("cols_turned"), sem("cols_ready"), sem("c_sig")
        sq_done, rms_ready, x_normed = sem("sq_done"), sem("rms_ready"), sem("x_normed")
        ada_summed, ada_in_ps, ada1_ready = sem("ada_summed"), sem("ada_in_ps"), sem("ada1_ready")
        x_turned, u_ready, uhi_ready, ulo_ready = sem("x_turned"), sem("u_ready"), sem("uhi_ready"), sem("ulo_ready")
        tile_done, tile_drained = sem("z_tile_done"), sem("z_tile_drained")
        conv_acc, conv_sig, conv_out = sem("conv_acc"), sem("conv_sig"), sem("conv_out")
        gate_stored = sem("gate_stored")
        dve_own, pool_own, pool_first = sem("dve_own1"), sem("pool_own1"), sem("pool_first")
        w_in = io.w_in
        GQ = (NZ - NG) // 2

        block = ctx.enter_context(nc.Block("project"))

        @block.sync
        def _(sp):
            sp.wait_ge(rows_zeroed, 1)
            sp.dma_start(m.const[:, :], io.const).then_inc(ident_landed, 16)
            sp.dma_start(m.rows[0:KT, :], io.rows[0][1]).then_inc(c_landed, 16)
            sp.wait_ge(x_landed[2], 16)
            for k in range(KT):
                if k == 4:
                    for name, src in io.rows[1:]:
                        r, n = ROWS[name]
                        sp.dma_start(m.rows[r:r + n, :], src).then_inc(rows_landed, 16)
                    sp.dma_start(m.bif[32:32 + MH, 0:1], io.b_igate).then_inc(const_landed, 16)
                    sp.dma_start(m.bif[0:MH, 0:1], io.b_fgate).then_inc(const_landed, 16)
                if k >= 4:
                    sp.wait_ge(ada_used, k - 3)
                sp.dma_start(m.ada_raw[:, k % 4, :], io.w_ada[k * P:(k + 1) * P, 0:ADA1]).then_inc(ada_landed[k % 4], 16)
            panels = [[(kn(m.raw[:, n % 2, :]), cols_of(w_in, c))] for n, c in
                      enumerate([PW * i for i in range(NQK)] + [C_V, C_V + PW, C_O, C_O + PW, C_QL])]
            r, half = kn(m.raw[:, 1, :]), ROPE // 2
            panels.append([(r[:, :, a:a + n], cols_of(w_in, c, n)) for a, c, n in (
                (0, C_KVL, KVR), (P, C_F, MH), (P + 32, C_I, MH), (P + NOPE, C_KR, ROPE),
                (P + NOPE + ROPE, C_KR + half, half), (P + NOPE + ROPE + half, C_KR, half))])
            for n, parts in enumerate(panels):
                load_panel(sp, m, n // 2, n % 2, parts, first=n < 2)

            def gate_panel(q, s, c):
                load_panel(sp, m, q, s, [(kn(m.raw[:, s, :]), cols_of(w_in, c + (C_GATE + s * PW)))])

            def pieces(i, s):
                for n in range(PIECES * s, PIECES * (s + 1)):
                    for h in range(2):
                        sp.wait_ge(acc_step, i * (2 * PIECES * KT) + (KT * n + KT // 2 * (h + 1)))
                        sp.dma_start(acc_raw[:, h, :, :], io.w_ada[h * S // 2:(h + 1) * S // 2, bass.ds(i * (2 * PIECES * ACC) + (ADA1 + n * ACC), ACC)].rearrange(
                            "(k p) n -> p k n", p=P)).then_inc(acc_landed[h], 16)

            for s in range(2):
                gate_panel(GQ, s, 0)
            sp.wait_ge(conv_out, 2 * NQK)
            with sp.Fori(0, NG // 2 - 1) as i:
                for s in range(2):
                    gate_panel(i + (GQ + 1), s, i * (2 * PW) + 2 * PW)
                    pieces(i, s)
            for s in range(2):
                load_panel(sp, m, NZ // 2, s, io.branch_panel(m, 0, s))
                pieces(NG // 2 - 1, s)

        @block.gpsimd
        def _(pool):
            own = Count(pool, pool_own)
            pool.memset(m.rows[:, :], 0.0).then_inc(rows_zeroed, 1)
            pool.memset(m.ones[:, :], 1.0).then_inc(ones_ready, 1)
            own.then(pool.memset(m.neghalf[:, :], -0.5))
            pool.memset(conv[:, 0, 0:CONV], 0.0).then_inc(pool_first, 1)
            pool.wait_ge(sq_done, TT)
            own.then(pool.tensor_scalar(m.stat[:, 0:TT], m.stat[:, 0:TT], 1.0 / D, EPS, ALU.mult, ALU.add))
            own.wait()
            pool.tensor_tensor(m.stat[:, TT:2 * TT], m.stat[:, 0:TT], m.neghalf[:, 0:TT], ALU.pow).then_inc(rms_ready, 1)
            pool.wait_ge(tile_drained, 4)
            own.then(pool.memset(m.vaug[:, :, :, MD:VA], 1.0))

            with pool.Fori(0, NG // 2) as i:
                for n in range(2 * PIECES):
                    pool.wait_ge(acc_step, i * (2 * PIECES * KT) + KT * (n + 2))
                    pool.dma_start(io.ada_acc[:, bass.ds(i * (2 * PIECES * ACC) + n * ACC, ACC)], acc_sum[:, n % 2, :]).then_inc(acc_stored[n % 2], 16)
            for s in range(2):
                pool.wait_ge(acc_stored[s], 16 * PIECES * NG // 2)

        @block.scalar
        def _(act):
            act.wait_ge(c_landed, 16)
            act.wait_ge(ident_landed, 16)
            for i in range(4):
                act.dma_start(m.xs[:, 2 * i:2 * i + 2, :], io.x[i * 2 * P:(i + 1) * 2 * P, :].rearrange("(t p) n -> p t n", p=P)).then_inc(x_landed[i], 16)
            act.wait_ge(c_turned, 1)
            act.activation(csig[:, :], m.ps[:, 3 * BANK:3 * BANK + KT], ACT.Sigmoid).then_inc(c_sig, 1)
            for t in range(TT):
                act.wait_ge(x_landed[t // 2], 16)
                if t >= 2:
                    act.wait_ge(sq_done, t - 1)
                act.activation(uhi[:, t % 2, :], m.xs[:, t, :], ACT.Square, accum_out=m.stat[:, t:t + 1]).then_inc(sq_done, 1)
            act.wait_ge(rms_ready, 1)
            for t in range(TT):
                act.activation(m.xs[:, t, :], m.xs[:, t, :], ACT.Copy, scale=m.stat[:, TT + t:TT + t + 1]).then_inc(x_normed, 1)
            split_hi(act, m, 0, 0)
            act.wait_ge(ada1_ready, 1)
            for k in range(KT):
                act.wait_ge(x_turned, k + 1)
                if k >= 2:
                    act.wait_ge(ulo_ready, k - 1)
                b = (4 + 2 * (k % 2)) * BANK
                act.activation(temp[:, k % 2, :], m.ps[:, b:b + S], ACT.Identity,
                               scale=m.aff[:, k:k + 1], bias=m.aff[:, KT + k:KT + k + 1]).then_inc(u_ready, 1)
            act.wait_ge(u_ready, KT)
            act.sem_inc(tile_drained, 2)
            act.wait_ge(ulo_ready, KT)
            act.wait_ge(pool_first, 1)

            def banks(n):
                return m.ps[:, 2 * n * BANK:2 * (n + 1) * BANK]

            with act.Fori(0, NQK // 2) as i:
                for s in range(2):
                    split_hi(act, m, i + s, 1 - s)
                    for t in range(2):
                        n = 2 * s + t
                        act.wait_ge(tile_done, i * 4 + (n + 1))
                        act.wait_ge(conv_acc, i * 4 + (n + 1))
                        act.activation(conv[:, 0, CONV - 1:CONV - 1 + S], banks(n), ACT.Copy).then_inc(tile_drained, 1)
                        act.wait_ge(conv_acc, i * 4 + (n + 2))
                        act.activation(temp[:, 1, :], m.qk[:, bass.ds(i * 4 + n, 1), :].rearrange("p a n -> p (a n)"),
                                       ACT.Sigmoid).then_inc(conv_sig, 1)
            for n in range(NQK, NZ - NG):
                split_hi(act, m, (n + 1) // 2, (n + 1) % 2, SPEC_PARTS if n + 1 == NZ - NG - 1 else None)
                for t in range(2):
                    act.wait_ge(tile_done, 2 * n + t + 1)
                    src, func = banks(2 * (n % 2) + t), ACT.Copy
                    if n < NQK + NV:
                        h = 2 * (n - NQK)
                        src = src.rearrange("p (t h e) -> p t h e", t=TT // 2, h=2)
                        dst = m.vaug[:, TT // 2 * t:TT // 2 * (t + 1), h:h + 2, 0:MD]
                    elif n < NQK + NV + NO:
                        dst, func = m.osig[:, 2 * (n - NQK - NV) + t, :], ACT.Sigmoid
                    else:
                        dst = m.lat[:, 2 * (n - NQK - NV - NO) + t, :]
                    act.activation(dst, src, func).then_inc(tile_drained, 1)
            act.wait_ge(conv_out, 2 * NQK)
            with act.Fori(0, NG // 2) as i:
                for s in range(2):
                    split_hi(act, m, i + (GQ + s), 1 - s)
                    for t in range(2):
                        n = 2 * s + t
                        act.wait_ge(tile_done, i * 4 + (4 * GQ + n + 1))
                        if n:
                            act.wait_ge(gate_stored, i * 64 + 16 * n)
                        act.activation(temp[:, 0, :], banks(n), ACT.Sigmoid).then_inc(tile_drained, 1)
                        act.wait_ge(tile_drained, i * 4 + (4 * GQ + n + 1 + 4))
                        act.dma_start(io.gates[bass.ds(i * 4 + n, 1), :, :].rearrange("a p n -> p (a n)"), temp[:, 0, :]).then_inc(gate_stored, 16)
                act.wait_ge(gate_stored, i * 64 + 64)

        @block.vector
        def _(dve):
            own = Count(dve, dve_own)
            dve.wait_ge(c_sig, 1)
            own.then(dve.tensor_tensor(m.csil[:, :], m.ps[:, 3 * BANK:3 * BANK + KT], csig[:, :], ALU.mult))

            for k in range(KT):
                dve.wait_ge(ada_landed[k % 4], 16 * (k // 4 + 1))
                own.wait()
                own.then(dve.tensor_scalar(m.ada_acc[:, :], m.ada_raw[:, 0, :], m.csil[:, 0:1], None, ALU.mult) if k == 0 else
                         dve.scalar_tensor_tensor(out=m.ada_acc[:, :], in0=m.ada_raw[:, k % 4, :], scalar=m.csil[:, k:k + 1],
                                                  in1=m.ada_acc[:, :], op0=ALU.mult, op1=ALU.add))
                own.wait()
                dve.sem_inc(ada_used, 1)
            dve.sem_inc(ada_summed, 1)
            dve.wait_ge(cols_turned, 1)
            dve.tensor_copy(m.cols[:, :], m.ps[:, 2 * BANK:2 * BANK + P]).then_inc(cols_ready, 1)
            dve.wait_ge(cols_ready, 1)
            split_lo(dve, m, 0, 0)
            dve.wait_ge(ada_in_ps, 1)
            adac = m.ps[:, 0:2 * KT * P].rearrange("p (j n) -> p j n", n=P)[:, :, 0]
            r = ROWS["b_ada"][0]
            own.then(dve.tensor_tensor(m.aff[:, KT:2 * KT], adac[:, 0:KT], m.cols[:, r:r + KT], ALU.add))
            own.then(dve.tensor_tensor(m.aff[:, 0:KT], adac[:, KT:2 * KT], m.cols[:, r + KT:r + 2 * KT], ALU.add))
            own.wait()
            dve.sem_inc(tile_drained, 2)
            r = ROWS["g_mix"][0]
            dve.scalar_tensor_tensor(out=m.aff[:, 0:KT], in0=m.aff[:, 0:KT], scalar=1.0, in1=m.cols[:, r:r + KT],
                                     op0=ALU.add, op1=ALU.mult).then_inc(ada1_ready, 1)
            for k in range(KT):
                dve.wait_ge(u_ready, k + 1)
                dve.tensor_copy(uhi[:, k, :], temp[:, k % 2, :]).then_inc(uhi_ready, 1)
                dve.wait_ge(uhi_ready, k + 1)
                dve.tensor_tensor(ulo[:, k, :], temp[:, k % 2, :], uhi[:, k, :], ALU.subtract).then_inc(ulo_ready, 1)
            dve.sem_inc(conv_acc, 1)
            with dve.Fori(0, NQK // 2) as i:
                own.loop(i, 2 * 2 * CONV - 4)
                for s in range(2):
                    split_lo(dve, m, i + s, 1 - s)
                    for t in range(2):
                        n = 2 * s + t
                        acc = m.qk[:, bass.ds(i * 4 + n, 1), :].rearrange("p a n -> p (a n)")
                        dve.wait_ge(tile_drained, i * 4 + (n + 1 + 4))
                        own.then(dve.tensor_scalar(acc, conv[:, 0, 0:S], col(m, "conv_w", i * 4 + n), col(m, "conv_b", i * 4 + n),
                                                   ALU.mult, ALU.add))
                        for j in range(1, CONV):
                            own.wait()
                            ins = dve.scalar_tensor_tensor(out=acc, in0=conv[:, 0, j:j + S], scalar=col(m, "conv_w", i * 4 + (j * 2 * MH + n)),
                                                           in1=acc, op0=ALU.mult, op1=ALU.add)
                            if j < CONV - 1:
                                own.then(ins)
                            else:
                                ins.then_inc(conv_acc, 1)
                        dve.wait_ge(conv_sig, i * 4 + (n + 1))
                        dve.scalar_tensor_tensor(out=acc, in0=acc, scalar=m.const[:, bass.ds(i * 4 + (K_COL + 3 + n), 1)],
                                                 in1=temp[:, 1, :], op0=ALU.mult, op1=ALU.mult).then_inc(conv_out, 1)
                own.end(NQK // 2)
            for n in range(NQK, NZ - NG):
                split_lo(dve, m, (n + 1) // 2, (n + 1) % 2)
            dve.sem_inc(acc_step, KT)
            with dve.Fori(0, NG // 2) as i:
                for s in range(2):
                    split_lo(dve, m, i + (GQ + s), 1 - s)
                    for n in range(PIECES * s, PIECES * (s + 1)):
                        if n >= 2:
                            dve.wait_ge(acc_stored[n % 2], i * (16 * PIECES) + 16 * (n // 2))
                        for k in range(KT):
                            if k % (KT // 2) == 0:
                                dve.wait_ge(acc_landed[2 * k // KT], i * (32 * PIECES) + 16 * (n + 1))
                            dve.wait_ge(acc_step, i * (2 * PIECES * KT) + (KT * (n + 1) + k))
                            raw, out = acc_raw[:, 2 * k // KT, k % (KT // 2), :], acc_sum[:, n % 2, :]
                            (dve.tensor_scalar(out, raw, m.csil[:, 0:1], None, ALU.mult) if k == 0 else
                             dve.scalar_tensor_tensor(out=out, in0=raw, scalar=m.csil[:, k:k + 1], in1=out, op0=ALU.mult, op1=ALU.add)
                             ).then_inc(acc_step, 1)
                for n in range(2):
                    dve.wait_ge(acc_stored[n], i * (16 * PIECES) + 16 * PIECES)

        @block.tensor
        def _(pe):
            pe.sem_inc(m.w_used, 1)
            pe.wait_ge(ident_landed, 16)
            pe.wait_ge(c_landed, 16)
            pe.transpose(m.ps[:, 3 * BANK:3 * BANK + KT], m.rows[0:KT, :], m.ident[0:KT, 0:KT]).then_inc(c_turned, 1)
            pe.wait_ge(rows_landed, 16 * (len(io.rows) - 1))
            pe.wait_ge(const_landed, 32)
            pe.transpose(m.ps[:, 2 * BANK:2 * BANK + P], m.rows[:, :], m.ident).then_inc(cols_turned, 1)

            def turn(k):
                if k >= 2:
                    pe.wait_ge(u_ready, k - 1)
                for t in range(TT):
                    if k == 0:
                        pe.wait_ge(x_normed, t + 1)
                    b = (4 + 2 * (k % 2)) * BANK + t * P
                    mm = pe.transpose(m.ps[:, b:b + P], m.xs[:, t, k * P:(k + 1) * P], m.ident)
                mm.then_inc(x_turned, 1)

            pe.wait_ge(ones_ready, 1)
            pe.wait_ge(cols_ready, 1)
            for j in range(2 * KT):
                mm = pe.matmul(m.ps[:, j * P:(j + 1) * P], m.ada_acc[:, j * P:(j + 1) * P], m.ones[:, :], start=True, stop=True)
            mm.then_inc(ada_in_ps, 1)
            for k in range(KT):
                turn(k)

            def feature_major(q):
                for s in range(2):
                    panel_ready(pe, m, q, s)
                    for t in range(2):
                        pe.wait_ge(tile_drained, q * 4 + (2 * s + t + 1))
                        for k in range(KT):
                            pe.wait_ge(ulo_ready, k + 1)
                            for g, (w, x) in enumerate(passes(m, s, uhi, ulo)):
                                for half in range(2):
                                    b = (4 * s + 2 * t + half) * BANK
                                    mm = pe.matmul(m.ps[:, b:b + BANK], kn(w[:, :])[:, k, t * P:(t + 1) * P],
                                                   x[:, k, half * BANK:(half + 1) * BANK],
                                                   start=(k == 0 and g == 0), stop=(k == KT - 1 and g == 2))
                        mm.then_inc(tile_done, 1)
                    pe.wait_ge(tile_done, q * 4 + (2 * s + 2))
                    pe.sem_inc(m.w_used, 1)

            with pe.Fori(0, NQK // 2) as i:
                feature_major(i)
            for n in range(NQK, NQK + NV):
                panel_ready(pe, m, n // 2, n % 2)
                for t in range(TT):
                    if t % 4 == 0:
                        pe.wait_ge(tile_drained, 2 * n + t // 4 + 1)
                    b = 4 * (n % 2) * BANK + t * PW
                    for k in range(KT):
                        for g, (w, x) in enumerate(passes(m, n % 2, uhi, ulo)):
                            mm = pe.matmul(m.ps[:, b:b + PW], x[:, k, t * P:(t + 1) * P], kn(w[:, :])[:, k, :],
                                           start=(k == 0 and g == 0), stop=(k == KT - 1 and g == 2))
                    if t % 4 == 3:
                        mm.then_inc(tile_done, 1)
                pe.wait_ge(tile_done, 2 * n + 2)
                pe.sem_inc(m.w_used, 1)
            with pe.Fori(0, (NZ - NQK - NV) // 2) as i:
                feature_major(i + (NQK + NV) // 2)



def stage_mlstm(nc, m, io):
    NC = TT
    with ExitStack() as ctx:
        alloc = lambda name, shape, dt=F32: ctx.enter_context(nc.sbuf_tensor(name, shape, dt))
        sem = m.sem
        g = alloc("gate_rows", [P, 4, S])
        x_, sp_, lf, cm = (g[0:MH, n, :] for n in range(4))
        a_, b_ = x_, sp_
        cmr, sel2 = alloc("cm_parts", [P, S], F32R), alloc("selectors", [P, MH * P], F32R)
        cmr_zeroed, cmr_hi, cmr_ready = m.sem("cmr_zeroed"), m.sem("cmr_hi"), m.sem("cmr_ready")
        turn = alloc("turn_rows", [P, S])
        mprev, mdec = alloc("mprev", [P, NC + 1]), alloc("mdec", [P, NC])
        acol = alloc("acol", [P, NC, MH])
        ecol = alloc("ecol", [P, NC, 3, MH])
        cmb = alloc("cmb", [P, MH, S])
        decay = alloc("decay", [P, MH, NC])
        state = alloc("state", [P, MH, VA])
        qkc = [alloc(f"qkc{i}", [P, 2 * MH, P]) for i in range(2)]
        kw = [alloc(f"kw{i}", [P, MH, P]) for i in range(2)]
        sw = [alloc(f"sw{i}", [P, MH, P]) for i in range(2)]
        arg, dmat = alloc("arg", [P, MH, P]), alloc("dmat", [P, MH, P])
        inter, num = alloc("inter", [P, MH, VA]), alloc("num", [P, MH, VA])
        sq, hs = alloc("sq", [P, P]), alloc("hs", [P, MH, P])
        den, ss, rt = alloc("den", [P, MH]), alloc("ss", [P, MH]), alloc("rt", [P, 4, MH])

        zeroed, x_ready, l_ready, lf_ready, cm_ready, turn_ready, turned = (
            sem("l_zeroed"), sem("lx_ready"), sem("l_ready"), sem("lf_ready"), sem("cm_ready"), sem("turn_ready"), sem("turned"))
        act_own, dve_own, cmb_ps, cols_done = sem("act_own2"), sem("dve_own2"), sem("cmb_ps"), sem("l_cols_done")
        kc_ready, kt_done, kw_ready, s_done, arg_ready, d_ready, sw_ready = (
            sem("kc_ready"), sem("kt_done"), sem("kw_ready"), sem("s_done"), sem("arg_ready"), sem("d_ready"), sem("sw_ready"))
        upd_done, inter_done, intra_done, state_ready, inter_ready, num_ready = (
            sem("upd_done"), sem("inter_done"), sem("intra_done"), sem("state_ready"), sem("inter_ready"), sem("num_ready"))
        ss_ready, var_ready, pow_ready, hs_ready, ht_done, hm_ready, pool_own = (
            sem("ss_ready"), sem("var_ready"), sem("pow_ready"), sem("hs_ready"), sem("ht_done"), sem("hm_ready"), sem("pool_own2"))

        B = lambda n, w=BANK: m.ps[:, n * BANK:n * BANK + w]
        heads = lambda ap: ap.rearrange("p (h n) -> p h n", h=MH)
        two = lambda n: m.ps[:, n * BANK:(n + 2) * BANK].rearrange("p (b n) -> p b n", b=2)[:, :, 0:2 * VA]
        slot = lambda n, h: m.ps[:, (n + h // 2) * BANK + (h % 2) * VA:(n + h // 2) * BANK + (h % 2 + 1) * VA]
        chunk = lambda ap, c: ap[:, :, bass.ds(c * P, P)]
        LOOPS = (NC - 3) // 2
        is_ = lambda c, n: isinstance(c, int) and c == n

        block = ctx.enter_context(nc.Block("mlstm"))

        def schedule(eng, step, own=None, per=0):
            step(0, 0)
            with eng.Fori(0, LOOPS) as i:
                if own:
                    own.loop(i, 2 * per)
                for k in (1, 2):
                    step(i * 2 + k, k % 2)
                if own:
                    own.end(LOOPS)
            for c in range(2 * LOOPS + 1, NC):
                step(c, c % 2)

        @block.gpsimd
        def _(pool):
            own = Count(pool, pool_own)
            pool.memset(cmr[0:32 + MH, :].bitcast(F32), 0.0).then_inc(cmr_zeroed, 1)
            own.then(pool.memset(turn[:, :], 0.0))
            own.then(pool.memset(mprev[:, :], 0.0))
            own.then(pool.memset(state[:, :, :], 0.0))
            own.wait()
            pool.sem_inc(zeroed, 1)

            def step(c, s):
                pool.wait_ge(var_ready, c + 1)
                pool.tensor_tensor(rt[:, 2, :], rt[:, 1, :], m.neghalf[:, 0:MH], ALU.pow).then_inc(pow_ready, 1)

            schedule(pool, step)

        @block.scalar
        def _(act):
            own = Count(act, act_own)
            act.wait_ge(x_ready, 1)
            own.then(act.activation(sp_, x_, ACT.Abs))
            own.wait()
            own.then(act.activation(sp_, sp_, ACT.Exp, scale=-1.0))
            own.wait()
            act.activation(sp_, sp_, ACT.Ln, bias=1.0).then_inc(l_ready, 1)
            act.activation(sel2[0:32 + MH, :], m.const[0:32 + MH, K_SEL:K_SEL + MH * P], ACT.Copy).then_inc(cmr_ready, 1)
            act.wait_ge(cm_ready, 1)
            act.wait_ge(cmr_zeroed, 1)
            act.activation(cmr[0:MH, :], cm, ACT.Copy).then_inc(cmr_hi, 1)
            act.wait_ge(cmb_ps, 1)
            act.activation(cmb[:, 0:2, :].rearrange("p h n -> p (h n)"), m.ps[:, 0:2 * S], ACT.Copy).then_inc(cols_done, 1)
            act.wait_ge(cmb_ps, 2)
            act.activation(cmb[:, 2:4, :].rearrange("p h n -> p (h n)"), m.ps[:, 2 * S:4 * S], ACT.Copy).then_inc(cols_done, 1)
            act.wait_ge(turned, 1)
            t = m.ps[:, 0:S].rearrange("p (c n) -> p c n", c=NC)
            act.activation(acol[:, :, :], t[:, :, 0:MH], ACT.Copy).then_inc(cols_done, 1)
            for n in range(3):
                act.activation(ecol[:, :, n, :], t[:, :, 32 * (n + 1):32 * (n + 1) + MH], ACT.Exp).then_inc(cols_done, 1)
            act.activation(decay[:, :, :], m.ps[:, 2 * BANK:2 * BANK + MH * NC].rearrange("p (h c) -> p h c", h=MH), ACT.Exp).then_inc(cols_done, 1)
            act.wait_ge(cols_done, 7)

            def copy(c, s):
                if not (isinstance(c, int) and c < 2):
                    act.wait_ge(s_done, c - 1)
                    act.wait_ge(kt_done, c - 1)
                    act.wait_ge(inter_done, c - 1)
                act.activation(qkc[s][:, :, :], chunk(m.qk[:, :, :], c), ACT.Copy).then_inc(kc_ready, 1)

            def weights(c, s):
                act.wait_ge(kt_done, c + 1)
                if not (isinstance(c, int) and c < 2):
                    act.wait_ge(upd_done, c - 1)
                for h in range(MH):
                    last = act.activation(kw[s][:, h, :], heads(B(0))[:, h, :], ACT.Copy,
                                          scale=ecol[:, bass.ds(c, 1), 2, h:h + 1].rearrange("p a n -> p (a n)"))
                last.then_inc(kw_ready, 1)
                act.wait_ge(arg_ready, c + 1)
                if not is_(c, 0):
                    act.wait_ge(sw_ready, c)
                act.activation(dmat[:, :, :], arg[:, :, :], ACT.Exp).then_inc(d_ready, 1)

            def step(c, s):
                if not is_(c, NC - 1):
                    weights(c + 1, 1 - s)
                act.wait_ge(inter_done, c + 1)
                if not is_(c, 0):
                    act.wait_ge(num_ready, c)
                for h in range(MH):
                    last = act.activation(inter[:, h, :], slot(4, h), ACT.Copy,
                                          scale=ecol[:, bass.ds(c, 1), 0, h:h + 1].rearrange("p a n -> p (a n)"))
                last.then_inc(inter_ready, 1)
                if not (isinstance(c, int) and c >= NC - 2):
                    copy(c + 2, s)
                act.wait_ge(num_ready, c + 1)
                if not is_(c, 0):
                    act.wait_ge(var_ready, c)
                for h in range(MH):
                    if h or not is_(c, 0):
                        act.wait_ge(ss_ready, c * MH + h)
                    act.activation(sq[:, :], num[:, h, 0:MD], ACT.Square, accum_out=ss[:, h:h + 1]).then_inc(ss_ready, 1)

            copy(0, 0)
            copy(1, 1)
            weights(0, 0)
            schedule(act, step)

        @block.vector
        def _(dve):
            own = Count(dve, dve_own)
            dve.wait_ge(zeroed, 1)
            dve.tensor_scalar(x_, m.lat[0:MH, 3, :], m.bif[0:MH, 0:1], None, ALU.add).then_inc(x_ready, 1)
            own.then(dve.tensor_scalar(cm, m.lat[32:32 + MH, 3, :], m.bif[32:32 + MH, 0:1], None, ALU.add))
            dve.wait_ge(x_ready, 1)
            own.then(dve.tensor_scalar(lf, x_, 0.0, None, ALU.min))
            own.wait()
            dve.wait_ge(l_ready, 1)
            own.then(dve.tensor_tensor(lf, lf, sp_, ALU.subtract))
            own.wait()
            for c in range(NC):
                r = slice(c * P, (c + 1) * P)
                own.then(dve.tensor_tensor_scan(b_[:, r], m.ones[0:MH, :], lf[:, r], 0.0, ALU.mult, ALU.add))
            own.wait()
            own.then(dve.tensor_tensor(a_, cm, b_, ALU.subtract))
            own.wait()
            for c in range(NC):
                r, e = slice(c * P, (c + 1) * P), slice((c + 1) * P - 1, (c + 1) * P)
                own.then(dve.tensor_tensor_scan(cm[:, r], a_[:, r], a_[:, r], mprev[0:MH, c:c + 1], ALU.max, ALU.max))
                own.wait()
                own.then(dve.tensor_tensor(mprev[0:MH, c + 1:c + 2], b_[:, e], cm[:, e], ALU.add))
                own.wait()
            dve.sem_inc(cm_ready, 1)
            own.then(dve.tensor_copy(turn[0:MH, :], a_))
            dve.wait_ge(cmr_hi, 1)
            dve.tensor_tensor(cmr[32:32 + MH, :], cm, cmr[0:MH, :], ALU.subtract).then_inc(cmr_ready, 1)
            cend = cm.rearrange("p (c n) -> p c n", c=NC)[:, :, P - 1:P]
            mp = mprev[0:MH, 0:NC].rearrange("p (c o) -> p c o", o=1)
            c3 = lambda ap: ap.rearrange("p (c n) -> p c n", c=NC)
            own.then(dve.tensor_tensor(c3(turn[32:32 + MH, :]), mp.to_broadcast([MH, NC, P]), c3(cm), ALU.subtract))
            own.then(dve.scalar_tensor_tensor(out=turn[64:64 + MH, :], in0=b_, scalar=-1.0, in1=cm, op0=ALU.mult, op1=ALU.subtract))
            own.then(dve.tensor_tensor(c3(turn[96:96 + MH, :]), c3(a_), cend.to_broadcast([MH, NC, P]), ALU.subtract))
            own.then(dve.tensor_tensor(mdec[0:MH, :].rearrange("p (c o) -> p c o", o=1), mp, cend, ALU.subtract))
            own.wait()
            dve.sem_inc(turn_ready, 1)
            dve.wait_ge(cols_done, 7)

            def exponents(c):
                if not is_(c, 0):
                    dve.wait_ge(d_ready, c)
                for h in range(MH):
                    last = dve.scalar_tensor_tensor(out=arg[:, h, :], in0=m.const[:, K_TMASK:K_TMASK + P],
                                                    scalar=acol[:, bass.ds(c, 1), h:h + 1].rearrange("p a n -> p (a n)"),
                                                    in1=cmb[:, h, bass.ds(c * P, P)], op0=ALU.add, op1=ALU.subtract)
                last.then_inc(arg_ready, 1)

            def weights(c, s):
                dve.wait_ge(s_done, c + 1)
                dve.wait_ge(d_ready, c + 1)
                if not (isinstance(c, int) and c < 2):
                    dve.wait_ge(intra_done, c - 1)
                dve.tensor_tensor(sw[s][:, :, :], heads(B(1)), dmat[:, :, :], ALU.mult).then_inc(sw_ready, 1)

            def out(c):
                dve.wait_ge(ht_done, c + 1)
                for h in range(MH):
                    last = dve.scalar_tensor_tensor(out=m.qk[:, h, bass.ds(c * P, P)], in0=heads(B(0))[:, h, :], scalar=col(m, "g_mhead", h),
                                                    in1=m.osig[:, h, bass.ds(c * P, P)], op0=ALU.mult, op1=ALU.mult)
                last.then_inc(hm_ready, 1)

            def step(c, s):
                if not is_(c, NC - 1):
                    weights(c + 1, 1 - s)
                dve.wait_ge(upd_done, c + 1)
                dve.wait_ge(inter_done, c + 1)
                for h in range(MH):
                    last = dve.scalar_tensor_tensor(out=state[:, h, :], in0=state[:, h, :], scalar=decay[:, h, bass.ds(c, 1)],
                                                    in1=slot(6, h), op0=ALU.mult, op1=ALU.add)
                last.then_inc(state_ready, 1)
                dve.wait_ge(intra_done, c + 1)
                dve.wait_ge(inter_ready, c + 1)
                if not is_(c, 0):
                    dve.wait_ge(hs_ready, c)
                    dve.wait_ge(ss_ready, c * MH)
                dve.tensor_tensor(num[:, :, :].rearrange("p (b h) n -> p b (h n)", b=2), two(2),
                                  inter[:, :, :].rearrange("p (b h) n -> p b (h n)", b=2), ALU.add).then_inc(num_ready, 1)
                if not is_(c, 0):
                    out(c - 1)
                dve.wait_ge(num_ready, c + 1)
                d = num[:, :, MD]
                own.then(dve.scalar_tensor_tensor(out=den[:, :], in0=d, scalar=-1.0, in1=d, op0=ALU.mult, op1=ALU.max))
                own.wait()
                own.then(dve.tensor_tensor(den[:, :], den[:, :], ecol[:, bass.ds(c, 1), 1, :].rearrange("p a n -> p (a n)"), ALU.max))
                own.wait()
                own.then(dve.reciprocal(rt[:, 0, :], den[:, :]))
                own.wait()
                own.then(dve.tensor_tensor(rt[:, 3, :], rt[:, 0, :], rt[:, 0, :], ALU.mult))
                own.wait()
                dve.wait_ge(ss_ready, c * MH + MH)
                own.then(dve.tensor_tensor(rt[:, 1, :], ss[:, :], rt[:, 3, :], ALU.mult))
                own.wait()
                dve.tensor_scalar(rt[:, 1, :], rt[:, 1, :], 1.0 / MD, EPS, ALU.mult, ALU.add).then_inc(var_ready, 1)
                if not (isinstance(c, int) and c >= NC - 2):
                    exponents(c + 2)
                dve.wait_ge(pow_ready, c + 1)
                own.then(dve.tensor_tensor(rt[:, 3, :], rt[:, 0, :], rt[:, 2, :], ALU.mult))
                own.wait()
                if not is_(c, 0):
                    dve.wait_ge(ht_done, c)
                for h in range(MH):
                    last = dve.tensor_scalar(hs[:, h, :], num[:, h, 0:MD], rt[:, 3, h:h + 1], None, ALU.mult)
                last.then_inc(hs_ready, 1)

            exponents(0)
            weights(0, 0)
            exponents(1)
            schedule(dve, step, own, 6)
            out(NC - 1)

        @block.tensor
        def _(pe):
            sel = lambda h: m.const[0:MH, K_SEL + h * P:K_SEL + (h + 1) * P]
            pe.sem_inc(hm_ready, 1)
            pe.wait_ge(cmr_ready, 2)
            for h in range(MH):
                for half in range(2):
                    mm = pe.matmul(B(2 * h + half), sel2[0:32 + MH, h * P:(h + 1) * P], cmr[0:32 + MH, half * BANK:(half + 1) * BANK],
                                   start=True, stop=True)
                if h % 2:
                    mm.then_inc(cmb_ps, 1)
            pe.wait_ge(turn_ready, 1)
            pe.wait_ge(cols_done, 2)
            for c in range(NC):
                pe.transpose(m.ps[:, c * P:(c + 1) * P], turn[:, c * P:(c + 1) * P], m.ident)
            for h in range(MH):
                mm = pe.matmul(m.ps[:, 2 * BANK + h * NC:2 * BANK + (h + 1) * NC], sel(h), mdec[0:MH, :], start=True, stop=True)
            mm.then_inc(turned, 1)
            pe.wait_ge(cols_done, 7)

            def front(c, s):
                pe.wait_ge(kc_ready, c + 1)
                if not is_(c, 0):
                    pe.wait_ge(sw_ready, c)
                for h in range(MH):
                    mm = pe.matmul(heads(B(1))[:, h, :], qkc[s][:, MH + h, :], qkc[s][:, h, :], start=True, stop=True)
                mm.then_inc(s_done, 1)
                if not is_(c, 0):
                    pe.wait_ge(kw_ready, c)
                if not (isinstance(c, int) and c < 2):
                    pe.wait_ge(hm_ready, c - 1)
                for h in range(MH):
                    mm = pe.transpose(heads(B(0))[:, h, :], qkc[s][:, MH + h, :], m.ident)
                mm.then_inc(kt_done, 1)

            def tail(c):
                pe.wait_ge(hs_ready, c + 1)
                if isinstance(c, int):
                    pe.wait_ge(kw_ready, min(c + 3, NC))
                else:
                    pe.wait_ge(kw_ready, c + 3)
                if is_(c, NC - 1):
                    pe.wait_ge(hm_ready, c + 1)
                for h in range(MH):
                    mm = pe.transpose(heads(B(0))[:, h, :], hs[:, h, :], m.ident)
                mm.then_inc(ht_done, 1)

            def step(c, s):
                if not is_(c, NC - 1):
                    front(c + 1, 1 - s)
                pe.wait_ge(kw_ready, c + 1)
                if not is_(c, 0):
                    pe.wait_ge(state_ready, c)
                v = lambda h: m.vaug[:, bass.ds(c, 1), h, :].rearrange("p a n -> p (a n)")
                for h in range(MH):
                    mm = pe.matmul(slot(6, h), kw[s][:, h, :], v(h), start=True, stop=True)
                mm.then_inc(upd_done, 1)
                if not is_(c, 0):
                    pe.wait_ge(inter_ready, c)
                for h in range(MH):
                    mm = pe.matmul(slot(4, h), qkc[s][:, h, :], state[:, h, :], start=True, stop=True)
                mm.then_inc(inter_done, 1)
                pe.wait_ge(sw_ready, c + 1)
                if not is_(c, 0):
                    pe.wait_ge(num_ready, c)
                for h in range(MH):
                    mm = pe.matmul(slot(2, h), sw[s][:, h, :], v(h), start=True, stop=True)
                mm.then_inc(intra_done, 1)
                if not is_(c, 0):
                    tail(c - 1)

            front(0, 0)
            schedule(pe, step)
            tail(NC - 1)



SCALE = AQK ** -0.5
TURN = (6.28125, 1.93500518798828125e-3, 3.0192172958656e-7)
MAGIC = 1.5 * 2.0 ** 23
GROUPS = [0]
for _qb in range(TT):
    GROUPS.append(GROUPS[-1] + (_qb + 4) // 4)
NGRP, NPAIR = GROUPS[-1], TT // 2


def alloc_attention(nc, m, ctx):
    alloc = lambda name, shape, dt=F32: ctx.enter_context(nc.sbuf_tensor(name, shape, dt))
    m.cqhi, m.cqlo = alloc("cqhi", [P, 2, S], F32R), alloc("cqlo", [P, 2, S], F32R)
    m.ckhi, m.cklo = alloc("ckhi", [P, S], F32R), alloc("cklo", [P, S], F32R)
    m.wuq = alloc("wuq", [P, 2, AH, P])
    m.wkhi, m.wklo = alloc("wkhi", [P, AH * P], F32R), alloc("wklo", [P, AH * P], F32R)
    m.rot = alloc("rot", [P, S])
    m.sq = [alloc(f"stq{i}", [P, 2, P], F32R) for i in range(2)]
    m.sk = [alloc(f"stk{i}", [P, P], F32R) for i in range(2)]
    m.qf = alloc("qf", [P, S])
    m.q = [w[:, 0:S] for w in (m.whi[1], m.wlo[1])]
    m.k = [w[:, S:2 * S] for w in (m.whi[1], m.wlo[1])]
    m.vall = m.lat[:, :, :].rearrange("p a n -> p (a n)").rearrange("p (t n) -> p t n", t=TT)
    m.oa = m.qk[:, MH:2 * MH, :]


def stage_latents(nc, m, io):
    with ExitStack() as ctx:
        alloc = lambda name, shape, dt=F32: ctx.enter_context(nc.sbuf_tensor(name, shape, dt))
        sem = m.sem
        pos_i, pos = alloc("pos_i", [P, S], I32), alloc("pos", [P, S])
        ang, turns, sq = alloc("ang", [P, S]), alloc("turns", [P, S]), alloc("lat_sq", [P, 3, S])
        wkv, krt, diag = alloc("wkv", [P, AH * P]), alloc("krt", [P, S]), alloc("lat_diag", [P, 2 * TT, P])
        pos_landed, wuq_landed, wkv_landed = sem("pos_landed"), sem("wuq_landed"), sem("wkv_landed")
        sq_ready, sum_done, var_ready, rinv_ready = sem("lat_sq_ready"), sem("lat_sum_done"), sem("lat_var_ready"), sem("lat_rinv_ready")
        diag_ready, row_done, pos_ready = sem("lat_diag_ready"), sem("lat_row_done"), sem("pos_ready")
        lat_ready, lhi_ready, llo_ready = sem("lat_ready"), sem("lhi_ready"), sem("llo_ready")
        wk_hi, wk_lo, ang_ready, rot_ready, krt_ready, kr_done, krhi_ready = (
            sem("wk_hi"), sem("wk_lo"), sem("ang_ready"), sem("rot_ready"), sem("krt_ready"), sem("kr_done"), sem("krhi_ready"))
        v_done, v_ready, dve_own, pool_own = sem("v_done"), sem("v_ready"), sem("dve_own3"), sem("pool_own3")
        lo = slice(NOPE, P)
        block = ctx.enter_context(nc.Block("latents"))
        row = lambda n: m.ps[:, (4 + 2 * n) * BANK:(6 + 2 * n) * BANK]
        w0_ready, w0_lo, proj_done, qf_ready, qk_hi = sem("w0_ready"), sem("w0_lo"), sem("proj0_done"), sem("qf0_ready"), sem("qk0_hi")
        lats = [(m.lat[:, 2, :], ("g_kv_lat", 0), 0, m.ckhi[:, :], m.cklo[:, :]),
                (m.lat[:, 0, :], ("g_q_lat", 0), 1, m.cqhi[:, 0, :], m.cqlo[:, 0, :]),
                (m.lat[:, 1, :], ("g_q_lat", 1), 1, m.cqhi[:, 1, :], m.cqlo[:, 1, :])]

        def vbank(t):
            return (2 + t % 2) * BANK

        @block.sync
        def _(sp):
            sp.dma_start(pos_i[lo, :], io.positions.partition_broadcast(P - NOPE)).then_inc(pos_landed, 16)
            sp.dma_start(wkv[:, :], io.w_ukv).then_inc(wkv_landed, 16)
            for k in range(2):
                sp.dma_start(m.wuq[:, k, :, 0:AQK], io.w_uq[k * P:(k + 1) * P, :].rearrange("p (h c) -> p h c", h=AH)).then_inc(wuq_landed, 16)

        @block.gpsimd
        def _(pool):
            pool.memset(m.rot[0:NOPE, :], 1.0).then_inc(pool_own, 1)
            pool.wait_ge(var_ready, 2)
            for n in range(2):
                c = slice(n * TT, (n + 1) * TT)
                pool.tensor_tensor(m.stat[:, 2 * TT:][:, c], m.stat[:, c], m.neghalf[:, 0:TT], ALU.pow).then_inc(rinv_ready, 1)
            half = ROPE // 2
            pool.wait_ge(wuq_landed, 32)
            for a, b in ((NOPE, NOPE + half), (NOPE + half, NOPE)):
                for k in range(2):
                    pool.tensor_copy(m.wuq[:, k, :, a + ROPE:a + ROPE + half], m.wuq[:, k, :, b:b + half]).then_inc(pool_own, 1)

        @block.scalar
        def _(act):
            for n in range(3):
                act.activation(sq[:, n, :], lats[n][0], ACT.Square).then_inc(sq_ready, 1)
            act.wait_ge(pos_landed, 16)
            act.activation(pos[lo, :], pos_i[lo, :], ACT.Copy).then_inc(pos_ready, 1)
            act.wait_ge(wkv_landed, 16)
            act.activation(m.wkhi[:, :], wkv[:, :], ACT.Copy).then_inc(wk_hi, 1)
            act.wait_ge(wk_lo, 1)
            for i, w in enumerate((m.wkhi, m.wklo)):
                act.activation(m.sk[i][:, :], w[:, 0:P], ACT.Copy).then_inc(w0_ready, 1)
            for n in range(2 * TT):
                act.wait_ge(rinv_ready, n // TT + 1)
                act.activation(diag[:, n, :], m.ident, ACT.Copy, scale=m.stat[:, 2 * TT + n:2 * TT + n + 1]).then_inc(diag_ready, 1)
            act.wait_ge(ang_ready, 1)
            act.activation(m.rot[lo, :], ang[lo, :], ACT.Sin).then_inc(rot_ready, 1)

            def high(n):
                act.wait_ge(lat_ready, n + 1)
                act.activation(lats[n][3], lats[n][0], ACT.Copy).then_inc(lhi_ready, 1)

            high(0)
            act.wait_ge(pool_own, 5)
            act.activation(m.sq[0][:, :, :], m.wuq[:, :, 0, :], ACT.Copy).then_inc(w0_ready, 1)
            high(1)
            high(2)
            act.wait_ge(kr_done, 1)
            act.activation(m.k[0][lo, :], m.ps[lo, 0:2 * BANK], ACT.Copy).then_inc(krhi_ready, 1)
            act.wait_ge(proj_done, 1)
            act.activation(m.k[0][0:NOPE, :], m.ps[0:NOPE, 4 * BANK:6 * BANK], ACT.Copy).then_inc(qk_hi, 1)
            act.wait_ge(krt_ready, 1)
            act.wait_ge(llo_ready, 3)
            for t in range(TT):
                if t == 2:
                    act.wait_ge(qf_ready, 1)
                    act.activation(m.q[0], m.qf[:, :], ACT.Copy).then_inc(qk_hi, 1)
                act.wait_ge(v_done, t + 1)
                act.activation(m.vall[:, t, :], m.ps[:, vbank(t):vbank(t) + BANK], ACT.Copy).then_inc(v_ready, 1)

        @block.vector
        def _(dve):
            own = Count(dve, dve_own)

            def step(ins):
                own.then(ins)
                own.wait()

            c = lambda n: m.const[lo, K_COL + n:K_COL + n + 1]

            def angles():
                yield dve.tensor_scalar(ang[lo, :], pos[lo, :], c(0), None, ALU.mult)
                yield dve.tensor_scalar(turns[lo, :], ang[lo, :], 1 / (2 * np.pi), c(1), ALU.mult, ALU.add)
                yield dve.tensor_scalar(turns[lo, :], turns[lo, :], MAGIC, None, ALU.add)
                yield dve.tensor_scalar(turns[lo, :], turns[lo, :], MAGIC, None, ALU.subtract)
                for part in TURN:
                    yield dve.scalar_tensor_tensor(out=ang[lo, :], in0=turns[lo, :], scalar=-part, in1=ang[lo, :], op0=ALU.mult, op1=ALU.add)
                yield dve.tensor_scalar(ang[lo, :], ang[lo, :], c(2), None, ALU.add)

            dve.wait_ge(pos_ready, 1)
            left = angles()
            for _ in range(2):
                step(next(left))

            def variance(n, width):
                dve.wait_ge(sum_done, n + 1)
                sums = m.ps[:, 2 * n * BANK:2 * (n + 1) * BANK].rearrange("p (t n) -> p t n", n=P)[:, :, 0]
                dve.tensor_scalar(m.stat[:, n * TT:(n + 1) * TT], sums, 1.0 / width, EPS, ALU.mult, ALU.add).then_inc(var_ready, 1)

            variance(0, KVR)
            step(next(left))
            dve.wait_ge(wk_hi, 1)
            dve.tensor_tensor(m.wklo[:, :], wkv[:, :], m.wkhi[:, :], ALU.subtract).then_inc(wk_lo, 1)
            step(next(left))
            variance(1, QR)
            for ins in left:
                step(ins)
            dve.tensor_scalar(ang[lo, :], ang[lo, :], 3.1415925, -3.1415925, ALU.min, ALU.max).then_inc(ang_ready, 1)

            def normed(n):
                src, g, r, _, _ = lats[n]
                dve.wait_ge(row_done, r + 1)
                dve.scalar_tensor_tensor(out=src, in0=src, scalar=col(m, *g), in1=row(r), op0=ALU.mult, op1=ALU.mult).then_inc(lat_ready, 1)

            def low(n):
                src, _, _, hi, low_ = lats[n]
                dve.wait_ge(lhi_ready, n + 1)
                dve.tensor_tensor(low_, src, hi, ALU.subtract).then_inc(llo_ready, 1)

            normed(0)
            dve.wait_ge(rot_ready, 1)
            dve.tensor_tensor(krt[lo, :], m.lat[lo, 3, :], m.rot[lo, :], ALU.mult).then_inc(krt_ready, 1)
            low(0)
            normed(1)
            dve.wait_ge(w0_ready, 3)
            dve.tensor_tensor(m.sq[1][:, :, :], m.wuq[:, :, 0, :], m.sq[0][:, :, :], ALU.subtract).then_inc(w0_lo, 1)
            normed(2)
            low(1)
            low(2)
            dve.wait_ge(krhi_ready, 1)
            dve.tensor_tensor(m.k[1][lo, :], m.ps[lo, 0:2 * BANK], m.k[0][lo, :], ALU.subtract).then_inc(dve_own, 1)
            dve.wait_ge(qk_hi, 1)
            dve.tensor_tensor(m.k[1][0:NOPE, :], m.ps[0:NOPE, 4 * BANK:6 * BANK], m.k[0][0:NOPE, :], ALU.subtract).then_inc(dve_own, 1)
            dve.wait_ge(proj_done, 2)
            dve.tensor_tensor(m.qf[:, :], m.ps[:, 6 * BANK:8 * BANK], m.rot[:, :], ALU.mult).then_inc(qf_ready, 1)
            dve.wait_ge(qk_hi, 2)
            dve.tensor_tensor(m.q[1], m.qf[:, :], m.q[0], ALU.subtract).then_inc(dve_own, 1)

        @block.tensor
        def _(pe):
            for n, ks in ((0, (0,)), (1, (1, 2))):
                pe.wait_ge(sq_ready, ks[-1] + 1)
                for t in range(TT):
                    for k in ks:
                        mm = pe.matmul(m.ps[:, 2 * n * BANK + t * P:2 * n * BANK + (t + 1) * P], sq[:, k, t * P:(t + 1) * P],
                                       m.ones[:, :], start=k == ks[0], stop=k == ks[-1])
                mm.then_inc(sum_done, 1)
            for n in range(2):
                for t in range(TT):
                    pe.wait_ge(diag_ready, n * TT + t + 1)
                    mm = pe.matmul(row(n)[:, t * P:(t + 1) * P], m.ones[:, :], diag[:, n * TT + t, :], start=True, stop=True)
                mm.then_inc(row_done, 1)
            pe.wait_ge(krt_ready, 1)
            pe.wait_ge(var_ready, 1)
            for half in range(2):
                mm = pe.matmul(m.ps[:, half * BANK:(half + 1) * BANK], m.const[lo, K_FOLD:K_FOLD + P],
                               krt[lo, half * BANK:(half + 1) * BANK], start=True, stop=True)
            mm.then_inc(kr_done, 1)
            pe.wait_ge(llo_ready, 1)
            pe.wait_ge(w0_ready, 2)
            for g, (w, x) in enumerate(((m.sk[0], m.ckhi), (m.sk[0], m.cklo), (m.sk[1], m.ckhi))):
                for half in range(2):
                    mm = pe.matmul(m.ps[:, (4 + half) * BANK:(5 + half) * BANK], w[:, :], x[:, half * BANK:(half + 1) * BANK], start=g == 0, stop=g == 2)
            mm.then_inc(proj_done, 1)
            v = lambda w: w[:, :].rearrange("p (h n) -> p h n", h=AH)[:, :, NOPE:P]
            pe.wait_ge(var_ready, 2)
            for t in range(TT):
                if t == 2:
                    pe.wait_ge(llo_ready, 3)
                    pe.wait_ge(w0_lo, 1)
                    for k in range(2):
                        for g, (w, x) in enumerate(((m.sq[0], m.cqhi), (m.sq[0], m.cqlo), (m.sq[1], m.cqhi))):
                            for half in range(2):
                                mm = pe.matmul(m.ps[:, (6 + half) * BANK:(7 + half) * BANK], w[:, k, :], x[:, k, half * BANK:(half + 1) * BANK],
                                               start=(k == 0 and g == 0), stop=(k == 1 and g == 2))
                    mm.then_inc(proj_done, 1)
                if t >= 2:
                    pe.wait_ge(v_ready, t - 1)
                for g, (x, w) in enumerate(((m.ckhi, m.wkhi), (m.ckhi, m.wklo), (m.cklo, m.wkhi))):
                    mm = pe.matmul(m.ps[:, vbank(t):vbank(t) + BANK], x[:, t * P:(t + 1) * P], v(w),
                                   start=g == 0, stop=g == 2)
                mm.then_inc(v_done, 1)


def stage_attention(nc, m, io):
    with ExitStack() as ctx:
        alloc = lambda name, shape, dt=F32: ctx.enter_context(nc.sbuf_tensor(name, shape, dt))
        sem = m.sem
        sq, sk, qf = m.sq, m.sk, m.qf
        v = [alloc(f"vh{i}", [P, (TT + 1) * AV], F32R) for i in range(2)]
        p = [alloc(f"prob{i}", [P, (TT // 2 + 1 + i) * P]) for i in range(4)]
        pt = [[alloc(f"probt{g}{i}", [P, TT - 2 + 2 * g, 2 * P], F32R) for i in range(2)] for g in range(2)]
        diag = alloc("diag", [P, 4, P])
        share = [alloc(f"share{i}", [AV, 2 * P]) for i in range(2)]
        mx, nb, rs, rr = (alloc(n, [P, TT]) for n in ("mx", "nb", "rs", "rr"))
        init = sem("att_init")
        sq_hi, sq_lo, sk_ready, projq, projk = sem("sq_hi"), sem("sq_lo"), sem("sk_ready"), sem("projq"), sem("projk")
        qf_ready, q_hi, q_lo, k_hi, k_lo, v_hi, v_lo = (sem("qf_ready"), sem("q_hi"), sem("q_lo"), sem("k_hi"), sem("k_lo"), sem("vh_hi"), sem("vh_lo"))
        sc_done, masked, max_ready, nb_ready, e_ready, rr_ready, diag_ready = (
            sem("sc_done"), sem("masked"), sem("max_ready"), sem("nb_ready"), sem("e_ready"), sem("rr_ready"), sem("diag_ready"))
        share_ready = sem("share_ready")
        t_done, th_ready, tl_ready, pv_done, oa_ready = sem("t_done"), sem("th_ready"), sem("tl_ready"), sem("pv_done"), sem("oa_ready")
        block = ctx.enter_context(nc.Block("attention"))
        B = lambda n, w=BANK: m.ps[:, n * BANK:n * BANK + w]

        def first_bank(qb):
            return (0, 2, 1, 3)[qb] if qb < 4 else 2 * (qb % 2)

        def scores_of(qb):
            n = (qb + 1) * P
            b = first_bank(qb)
            if n <= BANK:
                return B(b, n)
            return m.ps[:, b * BANK:(b + 2) * BANK].rearrange("p (a n) -> p a n", a=2)[:, :, 0:n // 2]

        def diagonal(qb):
            n = (qb + 1) * P
            end = first_bank(qb) * BANK + (n if n <= BANK else BANK + n // 2)
            return m.ps[:, end - P:end]

        def prob(qb):
            n = (qb + 1) * P
            ap = p[qb % 4][:, 0:n]
            return ap if n <= BANK else ap.rearrange("p (a n) -> p a n", a=2)

        def groups(qb):
            return [(GROUPS[qb] + n, 4 * n, min(4, qb + 1 - 4 * n)) for n in range((qb + 4) // 4)]

        def turned(gi, nb_):
            return B(4 + gi % 2, nb_ * P).rearrange("p (j n) -> p j n", j=nb_)

        def sums(g):
            return m.ps[0:AV, (6 + g % 2) * BANK:(7 + g % 2) * BANK]

        def pt_part(i, qb, j0, n):
            first = 2 * (qb // 2) + 2 - j0 - n
            return pt[(qb // 2) % 2][i][:, first:first + n, (qb % 2) * P:(qb % 2 + 1) * P]

        ORDER = dict(
            pe="S0 S1 S2 X3 S3 T0 T1 S4 S5 T2 V0 T3 S6 T4 V1 S7 T5 Q0 T6 K0 V2 T7",
            act="S0 S1 X3 S2 T0 T1 W0 S3 T2 S4 V0 T3 S5 T4 S6 V1 T5 S7 Q0 T6 K0 V2 T7",
            dve="S0 S1 S2 H0 H1 S3 H2 X3 W0 T0 T1 S4 H3 T2 H4 V0 S5 T3 S6 T4 V1 S7 T5 H5 Q0 H6 H7 R0 T6 K0 T7 V2")

        def run(eng, order, start, parts):
            start()
            parts["X"] = parts["V"]

            def head(h, pair, odd):
                first, last = isinstance(h, int) and h == 0, isinstance(h, int) and h == AH - 1
                for o in ORDER[order].split():
                    if not (first and o[0] == "X" or last and o[0] in "WQRK"):
                        at = (h, pair, odd) if o[0] != "X" else (h - 1, pair if odd else pair - 1, 1 - odd)
                        parts[o[0]](*at, int(o[1]))

            head(0, 0, 0)
            with eng.Fori(0, (AH - 2) // 2) as i:
                head(i * 2 + 1, i, 1)
                head(i * 2 + 2, i + 1, 0)
            head(AH - 1, AH // 2 - 1, 1)
            parts["X"](AH - 1, AH // 2 - 1, 1, NPAIR - 1)

        @block.gpsimd
        def _(pool):
            for i in range(2):
                pool.memset(v[i][:, TT * AV:].bitcast(F32), 0.0).then_inc(init, 1)
                for g in range(2):
                    pool.memset(pt[g][i][:, 0, 0:P].bitcast(F32), 0.0).then_inc(init, 1)

        @block.scalar
        def _(act):
            def weights(h):
                act.activation(sq[0][:, :, :], m.wuq[:, :, bass.ds(h, 1), :].rearrange("p k a n -> p k (a n)"), ACT.Copy).then_inc(sq_hi, 1)
                for i, w in enumerate((m.wkhi, m.wklo)):
                    act.activation(sk[i][:, :], w[:, bass.ds(h * P, P)], ACT.Copy).then_inc(sk_ready, 1)

            def next_weights(h, pair, odd, _):
                act.wait_ge(projk, h + 1)
                weights(h + 1)

            def queries(h):
                act.wait_ge(qf_ready, h + 1)
                act.activation(m.q[0], qf[:, :], ACT.Copy).then_inc(q_hi, 1)

            def keys(h):
                act.wait_ge(projk, h + 1)
                act.activation(m.k[0][0:NOPE, :], m.ps[0:NOPE, 2 * BANK:4 * BANK], ACT.Copy).then_inc(k_hi, 1)

            def values(h):
                act.activation(v[0][:, 0:TT * AV].rearrange("p (t n) -> p t n", t=TT), m.vall[:, :, bass.ds(h * AV, AV)], ACT.Copy).then_inc(v_hi, 1)

            def exps(h, pair, odd, qb):
                act.wait_ge(nb_ready, h * TT + (qb + 1))
                act.wait_ge(t_done, h * NGRP + (GROUPS[qb - 3] + NGRP if qb >= 4 else GROUPS[qb + 5]))
                act.activation(prob(qb), scores_of(qb), ACT.Exp, bias=nb[:, qb:qb + 1], scale=SCALE,
                               accum_out=rs[:, qb:qb + 1]).then_inc(e_ready, 1)

            def hi(h, pair, odd, qb):
                if qb % 2 == 0:
                    act.wait_ge(pv_done, h * NPAIR + (qb // 2 - 1 + NPAIR))
                for gi, j0, n in groups(qb):
                    act.wait_ge(t_done, h * NGRP + (gi + 1 + NGRP))
                    act.activation(pt_part(0, qb, j0, n), turned(gi, n), ACT.Copy).then_inc(th_ready, 1)

            def out(h, pair, odd, g):
                act.wait_ge(pv_done, h * NPAIR + (g + 1 + NPAIR))
                act.wait_ge(oa_ready, h * NPAIR + (g - 1 + NPAIR))
                act.activation(share[g % 2][:, :], sums(g)[:, 2 * P:4 * P], ACT.Copy).then_inc(share_ready, 1)
                if g == NPAIR - 1 and not (isinstance(h, int) and h == AH - 1):
                    values(h + 1)

            def q_next(h, pair, odd, _):
                act.wait_ge(sc_done, h * TT + TT)
                queries(h + 1)

            def k_next(h, pair, odd, _):
                act.wait_ge(sc_done, h * TT + TT)
                keys(h + 1)

            act.wait_ge(init, 6)
            act.sem_inc(th_ready, NGRP)
            for ready, n in ((sq_hi, 1), (sk_ready, 2), (k_hi, 1), (q_hi, 1)):
                act.sem_inc(ready, n)
            run(act, "act", lambda: values(0), {"S": exps, "T": hi, "V": out, "W": next_weights, "Q": q_next, "K": k_next})

        @block.vector
        def _(dve):
            def weights(h):
                dve.wait_ge(sq_hi, h + 1)
                dve.tensor_tensor(sq[1][:, :, :], m.wuq[:, :, bass.ds(h, 1), :].rearrange("p k a n -> p k (a n)"), sq[0][:, :, :],
                                  ALU.subtract).then_inc(sq_lo, 1)

            def queries(h):
                dve.wait_ge(projq, h + 1)
                dve.tensor_tensor(qf[:, :], m.ps[:, 0:2 * BANK], m.rot[:, :], ALU.mult).then_inc(qf_ready, 1)

            def queries_lo(h):
                dve.wait_ge(q_hi, h + 1)
                dve.tensor_tensor(m.q[1], qf[:, :], m.q[0], ALU.subtract).then_inc(q_lo, 1)

            def keys(h):
                dve.wait_ge(k_hi, h + 1)
                dve.tensor_tensor(m.k[1][0:NOPE, :], m.ps[0:NOPE, 2 * BANK:4 * BANK], m.k[0][0:NOPE, :], ALU.subtract).then_inc(k_lo, 1)

            def values(h):
                dve.wait_ge(v_hi, h + 1)
                dve.tensor_tensor(v[1][:, 0:TT * AV].rearrange("p (t n) -> p t n", t=TT), m.vall[:, :, bass.ds(h * AV, AV)],
                                  v[0][:, 0:TT * AV].rearrange("p (t n) -> p t n", t=TT), ALU.subtract).then_inc(v_lo, 1)

            def maxima(h, pair, odd, qb):
                n = h * TT + (qb + 1)
                dve.wait_ge(sc_done, n)
                dve.tensor_tensor(diagonal(qb), diagonal(qb), m.const[:, K_QMASK:K_QMASK + P], ALU.add).then_inc(masked, 1)
                dve.wait_ge(masked, n)
                dve.tensor_reduce(mx[:, qb:qb + 1], scores_of(qb), AX.X if qb < 4 else AX.XY, ALU.max).then_inc(max_ready, 1)
                dve.wait_ge(max_ready, n)
                dve.tensor_scalar(nb[:, qb:qb + 1], mx[:, qb:qb + 1], -SCALE, None, ALU.mult).then_inc(nb_ready, 1)

            def shares(h, pair, odd, qb):
                dve.wait_ge(e_ready, h * TT + (qb + 1))
                dve.reciprocal(rr[:, qb:qb + 1], rs[:, qb:qb + 1]).then_inc(rr_ready, 1)
                dve.wait_ge(pv_done, h * NPAIR + (qb // 2 - 1 + NPAIR))
                dve.wait_ge(rr_ready, h * TT + (qb + 1))
                dve.tensor_scalar(diag[:, qb % 4, :], m.ident, rr[:, qb:qb + 1], None, ALU.mult).then_inc(diag_ready, 1)

            def lo(h, pair, odd, qb):
                for gi, j0, n in groups(qb):
                    dve.wait_ge(th_ready, h * NGRP + (gi + 1 + NGRP))
                    dve.tensor_tensor(pt_part(1, qb, j0, n), turned(gi, n), pt_part(0, qb, j0, n), ALU.subtract).then_inc(tl_ready, 1)

            def next_weights(h, pair, odd, _):
                dve.wait_ge(projq, h + 1)
                weights(h + 1)

            def out(h, pair, odd, g):
                dve.wait_ge(share_ready, h * NPAIR + (g + 1))
                dst = m.oa[odd * AV:(odd + 1) * AV, bass.ds(pair, 1), g * 2 * P:(g + 1) * 2 * P].rearrange("p a n -> p (a n)")
                dve.tensor_tensor(dst, sums(g)[:, 0:2 * P], share[g % 2][:, :], ALU.mult).then_inc(oa_ready, 1)
                if g == NPAIR - 1 and not (isinstance(h, int) and h == AH - 1):
                    values(h + 1)

            dve.sem_inc(tl_ready, NGRP)
            dve.sem_inc(oa_ready, NPAIR)
            for ready in (sq_lo, qf_ready, q_lo, k_lo):
                dve.sem_inc(ready, 1)
            run(dve, "dve", lambda: values(0),
                {"S": maxima, "H": shares, "T": lo, "V": out,
                 "W": next_weights, "Q": lambda h, *_: queries(h + 1), "R": lambda h, *_: queries_lo(h + 1), "K": lambda h, *_: keys(h + 1)})

        @block.tensor
        def _(pe):
            def proj_q(h):
                pe.wait_ge(sq_lo, h + 1)
                for k in range(2):
                    for g, (w, x) in enumerate(((sq[0], m.cqhi), (sq[0], m.cqlo), (sq[1], m.cqhi))):
                        for half in range(2):
                            mm = pe.matmul(B(half), w[:, k, :], x[:, k, half * BANK:(half + 1) * BANK],
                                           start=(k == 0 and g == 0), stop=(k == 1 and g == 2))
                mm.then_inc(projq, 1)

            def proj_k(h):
                pe.wait_ge(sk_ready, h * 2 + 2)
                for g, (w, x) in enumerate(((sk[0], m.ckhi), (sk[0], m.cklo), (sk[1], m.ckhi))):
                    for half in range(2):
                        mm = pe.matmul(B(2 + half), w[:, :], x[:, half * BANK:(half + 1) * BANK], start=g == 0, stop=g == 2)
                mm.then_inc(projk, 1)

            def scores(h, pair, odd, qb):
                if qb < 4:
                    pe.wait_ge(q_lo, h + 1)
                    pe.wait_ge(k_lo, h + 1)
                else:
                    pe.wait_ge(e_ready, h * TT + (qb - 1))
                n = max((qb + 1) * P, 2 * P)
                pieces = [(0, n)] if n <= BANK else [(0, n // 2), (n // 2, n // 2)]
                for g, (a, b) in enumerate(((0, 0), (0, 1), (1, 0))):
                    for j, (c0, w) in enumerate(pieces):
                        mm = pe.matmul(B(first_bank(qb) + j, w), m.q[a][:, qb * P:(qb + 1) * P], m.k[b][:, c0:c0 + w],
                                       start=g == 0, stop=g == 2)
                mm.then_inc(sc_done, 1)

            def turn(h, pair, odd, qb):
                pe.wait_ge(e_ready, h * TT + (qb + 1))
                for gi, j0, n in groups(qb):
                    pe.wait_ge(tl_ready, h * NGRP + (gi - 1 + NGRP))
                    for j in range(n):
                        mm = pe.transpose(B(4 + gi % 2)[:, (n - 1 - j) * P:(n - j) * P], p[qb % 4][:, (j0 + j) * P:(j0 + j + 1) * P], m.ident)
                    mm.then_inc(t_done, 1)

            def values(h, pair, odd, g):
                pe.wait_ge(tl_ready, h * NGRP + (GROUPS[2 * g + 2] + NGRP))
                pe.wait_ge(v_lo, h + 1)
                pe.wait_ge(oa_ready, h * NPAIR + (g - 1 + NPAIR))
                nj = 2 * g + 2
                for j in range(nj):
                    for n, (a, b) in enumerate(((0, 0), (0, 1), (1, 0))):
                        mm = pe.matmul(B(6 + g % 2, 2 * P), v[a][:, j * AV:j * AV + P], pt[g % 2][b][:, nj - 1 - j, :],
                                       start=(j == 0 and n == 0), stop=(j == nj - 1 and n == 2))
                pe.wait_ge(diag_ready, h * TT + (2 * g + 2))
                for j in range(2):
                    mm = pe.matmul(sums(g)[:, (2 + j) * P:(3 + j) * P], m.ones[:, 0:AV], diag[:, (2 * g + j) % 4, :], start=True, stop=True)
                mm.then_inc(pv_done, 1)

            def q_next(h, pair, odd, _):
                pe.wait_ge(e_ready, h * TT + (TT - 1))
                proj_q(h + 1)

            def k_next(h, pair, odd, _):
                pe.wait_ge(e_ready, h * TT + TT)
                proj_k(h + 1)

            pe.sem_inc(t_done, NGRP)
            pe.sem_inc(pv_done, NPAIR)
            pe.sem_inc(projq, 1)
            pe.sem_inc(projk, 1)
            run(pe, "pe", lambda: None,
                {"S": scores, "T": turn, "V": values, "Q": q_next, "K": k_next})



Q_BRANCH = NZ // 2
Q_OUT = Q_BRANCH + 2
NOUT = D // PW
Q_FIN = Q_OUT + NOUT // 2
Q_FOUT = Q_FIN + FT // 2
HALF = S // 2
FA = FT - KT


def stage_branches(nc, m, io):
    with ExitStack() as ctx:
        alloc = lambda name, shape, dt=F32, **kw: ctx.enter_context(nc.sbuf_tensor(name, shape, dt, **kw))
        sem = m.sem
        bhi, blo = alloc("bhi", [P, 2 * MH, S], F32R), alloc("blo", [P, 2 * MH, S], F32R)
        gate = alloc("gate", [P, 2, 2, S], side="right")
        b_hi, b_lo = sem("b_hi"), sem("b_lo")
        gate_landed = [[sem(f"gate_landed{s}{i}") for i in range(2)] for s in range(2)]
        b_done, b_drained, y_ready = sem("b_done"), sem("b_drained"), sem("y_ready")
        block = ctx.enter_context(nc.Block("branches"))
        pair = lambda t, s: m.ps[:, (4 * (t % 2) + 2 * s) * BANK:(4 * (t % 2) + 2 * s + 2) * BANK]

        @block.sync
        def _(sp):
            for s in range(2):
                load_panel(sp, m, Q_BRANCH + 1, s, io.branch_panel(m, 1, s))
            for s in range(2):
                load_panel(sp, m, Q_OUT, s, [(kn(m.raw[:, s, :]), cols_of(io.w_out, s * PW))])

        @block.gpsimd
        def _(pool):
            with pool.Fori(0, 2) as j:
                for t in range(4):
                    pool.wait_ge(y_ready, j * 4 + (t + 1))
                    for s in range(2):
                        pool.dma_start(gate[:, s, t % 2, :], io.gates[bass.ds(j * 4 + (s * KT + t), 1), :, :].rearrange(
                            "a p n -> p (a n)")).then_inc(gate_landed[s][t % 2], 16)

        @block.scalar
        def _(act):
            for k in range(2 * MH):
                act.activation(bhi[:, k, :], m.qk[:, k, :], ACT.Copy).then_inc(b_hi, 1)
                if k == MH - 1:
                    split_hi(act, m, Q_BRANCH, 1)
            for n in range(3):
                split_hi(act, m, Q_BRANCH + 1 + n // 2, n % 2)

        @block.vector
        def _(dve):
            dve.sem_inc(b_drained, 4)
            dve.sem_inc(y_ready, 2)
            for k in range(2 * MH):
                dve.wait_ge(b_hi, k + 1)
                dve.tensor_tensor(blo[:, k, :], m.qk[:, k, :], bhi[:, k, :], ALU.subtract).then_inc(b_lo, 1)
                if k == MH - 1:
                    split_lo(dve, m, Q_BRANCH, 1)

            def merged(j, t):
                for s in range(2):
                    dve.wait_ge(b_done, j * 8 + (2 * t + s + 1))
                    dve.wait_ge(gate_landed[s][t % 2], j * 32 + 16 * (t // 2 + 1))
                    g = gate[:, s, t % 2, :]
                    dve.tensor_tensor(g, pair(t, s), g, ALU.mult).then_inc(b_drained, 1)
                dve.wait_ge(b_drained, j * 8 + (2 * t + 2 + 4))
                dve.tensor_tensor(m.y[:, bass.ds(j * 4 + t, 1), :].rearrange("p a n -> p (a n)"), gate[:, 0, t % 2, :],
                                  gate[:, 1, t % 2, :], ALU.add).then_inc(y_ready, 1)

            for j in range(2):
                for t in range(3):
                    merged(j, t)
                split_lo(dve, m, Q_BRANCH + 1 + j, 0)
                merged(j, 3)
                if j == 0:
                    split_lo(dve, m, Q_BRANCH + 1, 1)

        @block.tensor
        def _(pe):
            with pe.Fori(0, 2) as j:
                for t in range(4):
                    for s in range(2):
                        if t == 0:
                            panel_ready(pe, m, j + Q_BRANCH, s)
                        pe.wait_ge(b_drained, j * 8 + (2 * t + s + 1))
                        for k in range(MH):
                            if t == 0:
                                pe.wait_ge(b_lo, MH * s + k + 1)
                            for g, (w, x) in enumerate(passes(m, s, bhi, blo)):
                                for half in range(2):
                                    mm = pe.matmul(pair(t, s)[:, half * BANK:(half + 1) * BANK], kn(w[:, :], MH)[:, k, t * P:(t + 1) * P],
                                                   x[:, MH * s + k, half * BANK:(half + 1) * BANK],
                                                   start=(k == 0 and g == 0), stop=(k == MH - 1 and g == 2))
                        mm.then_inc(b_done, 1)
                        if t == 3:
                            pe.wait_ge(b_done, j * 8 + (2 * t + s + 1))
                            pe.sem_inc(m.w_used, 1)



def stage_out(nc, m, io):
    with ExitStack() as ctx:
        alloc = lambda name, shape, dt=F32, **kw: ctx.enter_context(nc.sbuf_tensor(name, shape, dt, **kw))
        sem = m.sem
        yhi, ylo = alloc("yhi", [P, KT, S], F32R), alloc("ylo", [P, KT, S], F32R)
        acc, gt1, tmp = alloc("ada_acc2", [P, 4 * D]), alloc("gt1", [P, D]), alloc("out_tmp", [P, 4, PW])
        gt2 = alloc("gt2_row", [P, D])
        sq_done, gt2_stored = m.sem("sq2_done"), m.sem("gt2_stored")
        acc_landed, gt1_landed, xr_landed = sem("acc_landed"), sem("b_gt1_landed"), [sem(f"xr_landed{i}") for i in range(4)]
        y_hi, y_lo, gt_done, gt1_ready, c_done = sem("y_hi"), sem("y_lo"), sem("gt1_done"), sem("gt1_ready"), sem("c2_done")
        o_done, o_drained, h_ready, dve_own = sem("o_done"), sem("o_drained"), sem("h_ready"), sem("dve_own5")
        gt2_landed, var_ready, rms_ready = sem("b_gt2_landed"), sem("var2_ready"), sem("rms2_ready")
        block = ctx.enter_context(nc.Block("out"))
        quad = lambda n, a: m.ps[:, (4 * (n % 2) + 2 * a) * BANK:(4 * (n % 2) + 2 * a + 2) * BANK]

        @block.sync
        def _(sp):
            for s in range(2):
                load_panel(sp, m, Q_OUT + 1, s, [(kn(m.raw[:, s, :]), cols_of(io.w_out, (2 + s) * PW))])
            for s in range(2):
                load_panel(sp, m, Q_FIN, s, io.ffn_panel(m, s, s))

        @block.gpsimd
        def _(pool):
            pool.dma_start(acc[:, :], io.ada_acc).then_inc(acc_landed, 16)
            pool.dma_start(gt1[:, :], io.b_ada[:, 2 * D:3 * D].partition_broadcast(P)).then_inc(gt1_landed, 16)
            pool.dma_start(gt2[0:1, :], io.b_ada[:, 5 * D:6 * D]).then_inc(gt2_landed, 16)
            for i in range(4):
                pool.wait_ge(y_lo, 2 * i + 2)
                pool.dma_start(m.y[:, 2 * i:2 * i + 2, :], io.x[i * 2 * P:(i + 1) * 2 * P, :].rearrange("(t p) n -> p t n", p=P)).then_inc(xr_landed[i], 16)
            for a in range(2):
                c = slice(a * 4, a * 4 + 4)
                pool.wait_ge(sq_done, 4 * a + 4)
                pool.tensor_scalar(m.stat[:, c], m.stat[:, c], 1.0 / D, EPS, ALU.mult, ALU.add).then_inc(var_ready, 1)
                pool.wait_ge(var_ready, a + 1)
                pool.tensor_tensor(m.stat[:, TT + a * 4:TT + a * 4 + 4], m.stat[:, c], m.neghalf[:, 0:4], ALU.pow).then_inc(rms_ready, 1)

        @block.scalar
        def _(act):
            for k in range(KT):
                act.activation(yhi[:, k, :], m.y[:, k, :], ACT.Copy).then_inc(y_hi, 1)
            for n in range(1, NOUT):
                split_hi(act, m, Q_OUT + n // 2, n % 2)
            act.wait_ge(gt1_ready, 2)
            for t in range(TT):
                act.wait_ge(h_ready, t // 4 + 1)
                if t:
                    act.wait_ge(sq_done, t)
                act.activation(acc[:, 0:D], m.y[:, t, :], ACT.Square, accum_out=m.stat[:, t:t + 1]).then_inc(sq_done, 1)
            act.wait_ge(gt1_ready, 2)
            act.dma_start(io.gt2, gt2[0:1, :]).then_inc(gt2_stored, 16)
            act.wait_ge(gt2_stored, 16)

        @block.vector
        def _(dve):
            own = Count(dve, dve_own)
            for k in range(KT):
                dve.wait_ge(y_hi, k + 1)
                dve.tensor_tensor(ylo[:, k, :], m.y[:, k, :], yhi[:, k, :], ALU.subtract).then_inc(y_lo, 1)
            split_lo(dve, m, Q_OUT, 1)
            dve.wait_ge(gt_done, 1)
            dve.wait_ge(gt1_landed, 16)
            dve.wait_ge(gt2_landed, 16)
            dve.tensor_tensor(gt1[:, :], m.ps[:, 4 * BANK:6 * BANK], gt1[:, :], ALU.add).then_inc(gt1_ready, 1)
            dve.tensor_tensor(gt2[0:1, :], m.ps[0:1, 6 * BANK:8 * BANK], gt2[0:1, :], ALU.add).then_inc(gt1_ready, 1)
            for i in range(4):
                dve.wait_ge(xr_landed[i], 16)
            for n in range(NOUT):
                if 1 < n + 1 < NOUT:
                    split_lo(dve, m, Q_OUT + (n + 1) // 2, (n + 1) % 2)
                dve.wait_ge(gt1_ready, 1)
                g = gt1[:, n * PW:(n + 1) * PW].rearrange("p (o n) -> p o n", o=1).to_broadcast([P, 4, PW])
                for a in range(2):
                    dve.wait_ge(o_done, 2 * n + a + 1)
                    own.wait()
                    dve.tensor_tensor(tmp[:, :, :], quad(n, a).rearrange("p (t n) -> p t n", t=4), g, ALU.mult).then_inc(o_drained, 1)
                    dve.wait_ge(o_drained, 2 * n + a + 1)
                    h = m.y[:, 4 * a:4 * a + 4, n * PW:(n + 1) * PW]
                    own.then(dve.tensor_tensor(h, h, tmp[:, :, :], ALU.add))
                    if n == NOUT - 1:
                        own.wait()
                        dve.sem_inc(h_ready, 1)
            dve.wait_ge(c_done, 1)
            adac = m.ps[:, 0:2 * KT * P].rearrange("p (j n) -> p j n", n=P)[:, :, 0]
            r = ROWS["b_ada"][0] + 3 * KT
            own.then(dve.tensor_tensor(m.aff[:, KT:2 * KT], adac[:, 0:KT], m.cols[:, r:r + KT], ALU.add))
            own.then(dve.tensor_tensor(m.aff[:, 0:KT], adac[:, KT:2 * KT], m.cols[:, r + KT:r + 2 * KT], ALU.add))
            own.wait()
            r = ROWS["g_ffn"][0]
            own.then(dve.scalar_tensor_tensor(out=m.aff[:, 0:KT], in0=m.aff[:, 0:KT], scalar=1.0, in1=m.cols[:, r:r + KT],
                                              op0=ALU.add, op1=ALU.mult))

        @block.tensor
        def _(pe):
            for n in range(NOUT):
                panel_ready(pe, m, Q_OUT + n // 2, n % 2)
                for t in range(TT):
                    if n == 0 and t == 4:
                        pe.wait_ge(acc_landed, 16)
                        for half in range(4):
                            c = (half // 2) * 3 * D + (half % 2) * BANK
                            mm = pe.matmul(m.ps[:, (4 + half) * BANK:(5 + half) * BANK], m.ones[:, :], acc[:, c:c + BANK], start=True, stop=True)
                        mm.then_inc(gt_done, 1)
                    if n == 1 and t % 4 == 0:
                        pe.wait_ge(gt1_ready, 2)
                    if n >= 2 and t % 4 == 0:
                        pe.wait_ge(o_drained, 2 * n + t // 4 - 3)
                    b = 4 * (n % 2) * BANK + t * PW
                    for k in range(KT):
                        pe.wait_ge(y_lo, k + 1)
                        for g, (w, x) in enumerate(passes(m, n % 2, yhi, ylo)):
                            mm = pe.matmul(m.ps[:, b:b + PW], x[:, k, t * P:(t + 1) * P], kn(w[:, :])[:, k, :],
                                           start=(k == 0 and g == 0), stop=(k == KT - 1 and g == 2))
                    if t % 4 == 3:
                        mm.then_inc(o_done, 1)
                pe.wait_ge(o_done, 2 * n + 2)
                pe.sem_inc(m.w_used, 1)
            pe.wait_ge(o_drained, 2 * NOUT - 2)
            for j in range(2 * KT):
                mm = pe.matmul(m.ps[:, j * P:(j + 1) * P], acc[:, D + j * P:D + (j + 1) * P], m.ones[:, :], start=True, stop=True)
            mm.then_inc(c_done, 1)



def stage_hidden(nc, m, io):
    with ExitStack() as ctx:
        sem = m.sem
        h, hn, temp = m.y, m.hidden[:, FA - TT:FA, :], m.hidden[:, 2:4, :]
        h_stored, h_normed = sem("h_stored"), sem("h_normed")
        h_turned, u_ready, uhi_ready, ulo_ready = sem("h_turned"), sem("u2_ready"), sem("u2hi_ready"), sem("u2lo_ready")
        f_done, sig_ready, g_ready, f_drained = sem("f_done"), sem("sig_ready"), sem("g_ready"), sem("f_drained")
        block = ctx.enter_context(nc.Block("hidden"))
        pair = lambda s, a: m.ps[:, (4 * s + 2 * a) * BANK:(4 * s + 2 * a + 2) * BANK]
        tile = lambda where, n: where[:, bass.ds(n, 1), :].rearrange("p a n -> p (a n)")
        turned = lambda k: (4 + 2 * (k % 2)) * BANK

        @block.sync
        def _(sp):
            sp.dma_start(io.h.rearrange("(t p) n -> p t n", p=P), h[:, :, :]).then_inc(h_stored, 16)
            with sp.Fori(1, FT // 2) as i:
                for s in range(2):
                    load_panel(sp, m, i + Q_FIN, s, io.ffn_panel(m, s, i * 2 + s))
            for s in range(2):
                load_panel(sp, m, Q_FOUT, s, [io.ffn_out_panel(m, s, s)])

        @block.scalar
        def _(act):
            split_hi(act, m, Q_FIN, 0, ffn_parts(0, 0))
            for k in range(KT):
                act.wait_ge(h_turned, k + 1)
                if k >= 2:
                    act.wait_ge(ulo_ready, k - 1)
                act.activation(temp[:, k % 2, :], m.ps[:, turned(k):turned(k) + S], ACT.Identity,
                               scale=m.aff[:, k:k + 1], bias=m.aff[:, KT + k:KT + k + 1]).then_inc(u_ready, 1)
            act.wait_ge(ulo_ready, KT)
            act.wait_ge(h_stored, 16)

            def step(i, s, where, n0, last=False):
                split_hi(act, m, i + (Q_FIN + s), 1 - s, None if last else ffn_parts(i + s, 1 - s))
                act.wait_ge(f_done, i * 4 + (2 * s + 1))
                act.activation(tile(where, i * 2 + (s - n0)), pair(s, 0), ACT.Sigmoid).then_inc(sig_ready, 1)

            with act.Fori(0, FA // 2) as i:
                step(i, 0, m.hidden, 0)
                step(i, 1, m.hidden, 0)
            with act.Fori(FA // 2, FT // 2 - 1) as i:
                step(i, 0, m.y, FA)
                step(i, 1, m.y, FA)
            step(FT // 2 - 1, 0, m.y, FA)
            step(FT // 2 - 1, 1, m.y, FA, last=True)

        @block.vector
        def _(dve):
            for t in range(TT):
                dve.tensor_scalar(hn[:, t, :], h[:, t, :], m.stat[:, TT + t:TT + t + 1], None, ALU.mult).then_inc(h_normed, 1)
            split_lo(dve, m, Q_FIN, 0)
            for k in range(KT):
                dve.wait_ge(u_ready, k + 1)
                dve.tensor_copy(m.u2hi[:, k, :], temp[:, k % 2, :]).then_inc(uhi_ready, 1)
                dve.wait_ge(uhi_ready, k + 1)
                dve.tensor_tensor(m.u2lo[:, k, :], temp[:, k % 2, :], m.u2hi[:, k, :], ALU.subtract).then_inc(ulo_ready, 1)
            dve.sem_inc(f_drained, 1)
            dve.wait_ge(u_ready, KT)
            dve.sem_inc(f_drained, 1)

            def step(i, s, where, n0):
                split_lo(dve, m, i + (Q_FIN + s), 1 - s)
                dve.wait_ge(sig_ready, i * 2 + (s + 1))
                out = tile(where, i * 2 + (s - n0))
                dve.tensor_tensor(out, pair(s, 0), out, ALU.mult).then_inc(g_ready, 1)
                dve.wait_ge(g_ready, i * 2 + (s + 1))
                dve.wait_ge(f_done, i * 4 + (2 * s + 2))
                dve.tensor_tensor(out, pair(s, 1), out, ALU.mult).then_inc(f_drained, 1)

            with dve.Fori(0, FA // 2) as i:
                step(i, 0, m.hidden, 0)
                step(i, 1, m.hidden, 0)
            with dve.Fori(FA // 2, FT // 2) as i:
                step(i, 0, m.y, FA)
                step(i, 1, m.y, FA)

        @block.tensor
        def _(pe):
            def turn(k):
                if k >= 2:
                    pe.wait_ge(u_ready, k - 1)
                for t in range(TT):
                    if k == 0:
                        pe.wait_ge(h_normed, t + 1)
                    mm = pe.transpose(m.ps[:, turned(k) + t * P:turned(k) + (t + 1) * P], hn[:, t, k * P:(k + 1) * P], m.ident)
                mm.then_inc(h_turned, 1)

            def product(s, a, k):
                for g, (w, x) in enumerate(passes(m, s, m.u2hi, m.u2lo)):
                    for half in range(2):
                        mm = pe.matmul(pair(s, a)[:, half * BANK:(half + 1) * BANK], kn(w[:, :])[:, k, a * P:(a + 1) * P],
                                       x[:, k, half * BANK:(half + 1) * BANK],
                                       start=(k == 0 and g == 0), stop=(k == KT - 1 and g == 2))
                return mm

            turn(0)
            turn(1)
            turn(2)
            panel_ready(pe, m, Q_FIN, 0)
            for k in range(KT):
                if k + 3 < KT:
                    turn(k + 3)
                pe.wait_ge(ulo_ready, k + 1)
                mm = product(0, 0, k)
            mm.then_inc(f_done, 1)
            for k in range(KT):
                mm = product(0, 1, k)
            mm.then_inc(f_done, 1)
            pe.wait_ge(f_done, 2)
            pe.sem_inc(m.w_used, 1)

            def step(i, s):
                panel_ready(pe, m, i + Q_FIN, s)
                pe.wait_ge(f_drained, i * 2 + (s + 1))
                for a in range(2):
                    for k in range(KT):
                        mm = product(s, a, k)
                    mm.then_inc(f_done, 1)
                pe.wait_ge(f_done, i * 4 + (2 * s + 2))
                pe.sem_inc(m.w_used, 1)

            step(0, 1)
            with pe.Fori(1, FT // 2) as i:
                step(i, 0)
                step(i, 1)



def stage_final(nc, m, io):
    NP = FT // 2
    QT = TT // 2
    with ExitStack() as ctx:
        alloc = lambda name, shape, dt=F32, **kw: ctx.enter_context(nc.sbuf_tensor(name, shape, dt, **kw))
        sem = m.sem
        hhi = [alloc(f"hid_hi{i}", [P, 2, HALF], F32R) for i in range(2)]
        hlo = [alloc(f"hid_lo{i}", [P, 2, HALF], F32R) for i in range(2)]
        squares, gt2, gfin = alloc("squares", [P, D]), alloc("gt2", [P, D]), alloc("gfin", [P, D])
        h, tmp = alloc("h_half", [P, QT, D]), alloc("fin_tmp", [P, QT, D])
        gt2_landed, gfin_landed = sem("gt2_landed"), sem("gfin_landed")
        hr_landed, hid_hi, hid_lo, out_stored = sem("hr_landed"), sem("hid_hi"), sem("hid_lo"), [sem("out_stored0"), sem("out_stored1")]
        p_done, d_drained, h2_ready = sem("fo_done"), sem("d_drained"), sem("h2_ready")
        t_done = sem("fo_tile_done")
        sq_done, var_ready, rms_ready, out_ready = sem("sq3_done"), sem("var3_ready"), sem("rms3_ready"), sem("out_ready")
        block = ctx.enter_context(nc.Block("final"))
        rows = lambda t: m.ps[:, 2 * t * BANK:2 * (t + 1) * BANK]

        def tiles(p, hf):
            where = m.hidden
            if isinstance(p, int) and p >= FA // 2:
                where, p = m.y, p - FA // 2
            return where[:, bass.ds(p * 2, 2), hf * HALF:(hf + 1) * HALF]

        def over_panels(eng, step, middle=(None, None, None), finish=None):
            for n in range(2):
                step(n, n // 2, n % 2, n, 0)
            with eng.Fori(1, 3) as i:
                for s in range(2):
                    step(i * 2 + s, i, s, i * 2 + s, 0)
            for n in range(6, NP):
                step(n, n // 2, n % 2, n, 0)
            for n in range(3):
                step(NP + n, (NP + n) // 2, (NP + n) % 2, n, 1)
                if middle[n]:
                    middle[n]()
            with eng.Fori(7, 9) as i:
                for s in range(2):
                    step(i * 2 + s, i, s, i * 2 + (s - NP), 1)
            for n in range(18, FT):
                step(n, n // 2, n % 2, n - NP, 1)
            if finish:
                finish()

        @block.sync
        def _(sp):
            def step(n, q, s, p, hf):
                if not (isinstance(n, int) and n < 2):
                    load_panel(sp, m, q + Q_FOUT, s, [io.ffn_out_panel(m, s, p)])

            def store(hf):
                for t in range(QT):
                    sp.wait_ge(out_ready, QT * hf + t + 1)
                    r = (hf * QT + t) * P
                    sp.dma_start(io.out[r:r + P, :], tmp[:, t, :]).then_inc(out_stored[hf], 16)

            over_panels(sp, step, (None, None, lambda: store(0)), lambda: store(1))
            for hf in range(2):
                sp.wait_ge(out_stored[hf], 16 * QT)

        @block.gpsimd
        def _(pool):
            pool.dma_start(gt2[:, :], io.gt2.partition_broadcast(P)).then_inc(gt2_landed, 16)
            pool.dma_start(gfin[:, :], io.g_final.partition_broadcast(P)).then_inc(gfin_landed, 16)
            for hf in range(2):
                if hf:
                    pool.wait_ge(h2_ready, QT)
                pool.dma_start(h[:, :, :], io.h[hf * HALF:(hf + 1) * HALF, :].rearrange("(t p) n -> p t n", p=P)).then_inc(hr_landed, 16)
                for t in range(QT):
                    n = QT * hf + t
                    pool.wait_ge(sq_done, n + 1)
                    ss = m.stat[:, t:t + 1]
                    pool.tensor_scalar(ss, ss, 1.0 / D, EPS, ALU.mult, ALU.add).then_inc(var_ready, 1)
                    pool.wait_ge(var_ready, n + 1)
                    pool.tensor_tensor(m.stat[:, TT + t:TT + t + 1], ss, m.neghalf[:, 0:1], ALU.pow).then_inc(rms_ready, 1)

        @block.scalar
        def _(act):
            def step(n, q, s, p, hf):
                if not (isinstance(n, int) and n == 0):
                    split_hi(act, m, q + Q_FOUT, s)
                if not (isinstance(n, int) and n < 2):
                    act.wait_ge(m.w_used, n + 2 * Q_FOUT)
                act.activation(hhi[s][:, :, :], tiles(p, hf), ACT.Copy).then_inc(hid_hi, 1)

            def finish(hf):
                for t in range(QT):
                    act.wait_ge(h2_ready, QT * hf + t + 1)
                    if hf or t:
                        act.wait_ge(sq_done, QT * hf + t)
                    if hf:
                        act.wait_ge(rms_ready, t + 1)
                    act.activation(squares[:, :], tmp[:, t, :], ACT.Square, accum_out=m.stat[:, t:t + 1]).then_inc(sq_done, 1)

            over_panels(act, step, (None, lambda: finish(0), None), lambda: finish(1))

        @block.vector
        def _(dve):
            def step(n, q, s, p, hf):
                if not (isinstance(n, int) and n == 0):
                    split_lo(dve, m, q + Q_FOUT, s)
                dve.wait_ge(hid_hi, n + 1)
                if not (isinstance(n, int) and n < 2):
                    dve.wait_ge(m.w_used, n + 2 * Q_FOUT)
                dve.tensor_tensor(hlo[s][:, :, :], tiles(p, hf), hhi[s][:, :, :], ALU.subtract).then_inc(hid_lo, 1)

            def drain_tile(hf, t):
                dve.wait_ge(t_done, QT * hf + t + 1)
                dve.tensor_tensor(tmp[:, t, :], rows(t), gt2[:, :], ALU.mult).then_inc(d_drained, 1)

            def residual(hf, t):
                dve.wait_ge(d_drained, QT * hf + t + 1)
                dve.tensor_tensor(tmp[:, t, :], tmp[:, t, :], h[:, t, :], ALU.add).then_inc(h2_ready, 1)

            def scaled(hf, t):
                dve.wait_ge(rms_ready, QT * hf + t + 1)
                dve.scalar_tensor_tensor(out=tmp[:, t, :], in0=tmp[:, t, :], scalar=m.stat[:, TT + t:TT + t + 1], in1=gfin[:, :],
                                         op0=ALU.mult, op1=ALU.mult).then_inc(out_ready, 1)

            def drain(hf):
                if hf == 0:
                    dve.wait_ge(gt2_landed, 16)
                    dve.wait_ge(gfin_landed, 16)
                if hf:
                    dve.wait_ge(out_stored[0], 16 * QT)
                    dve.wait_ge(hr_landed, 16 * 2)
                for t in range(QT):
                    drain_tile(hf, t)
                    if hf:
                        residual(hf, t)
                        if t:
                            scaled(hf, t - 1)

            def residuals():
                drain(0)
                dve.wait_ge(hr_landed, 16)
                for t in range(QT):
                    residual(0, t)

            def outputs():
                for t in range(QT):
                    scaled(0, t)

            def finish():
                drain(1)
                scaled(1, QT - 1)

            over_panels(dve, step, (residuals, outputs, None), finish)

        @block.tensor
        def _(pe):
            def step(n, q, s, p, hf):
                first, last = isinstance(p, int) and p == 0, isinstance(p, int) and p == NP - 1
                panel_ready(pe, m, q + Q_FOUT, s)
                pe.wait_ge(hid_lo, n + 1)
                for t in range(QT):
                    if first and hf:
                        pe.wait_ge(d_drained, t + 1)
                    for k in range(2):
                        for g, (w, x) in enumerate(passes(m, s, hhi[s], hlo[s])):
                            for half in range(2):
                                mm = pe.matmul(rows(t)[:, half * BANK:(half + 1) * BANK], x[:, k, t * P:(t + 1) * P],
                                               kn(w[:, :], 2)[:, k, half * BANK:(half + 1) * BANK],
                                               start=first and k == 0 and g == 0, stop=last and k == 1 and g == 2)
                    if last:
                        mm.then_inc(t_done, 1)
                if last:
                    pe.wait_ge(t_done, QT * hf + QT)
                    pe.sem_inc(p_done, 1)
                else:
                    mm.then_inc(p_done, 1)
                pe.wait_ge(p_done, n + 1)
                pe.sem_inc(m.w_used, 1)

            over_panels(pe, step)


def program(nc, io, upto=9):
    with ExitStack() as ctx:
        m = Record()
        m.stage_sems = []

        def sem(name):
            m.stage_sems.append(nc.alloc_semaphore(name))
            return m.stage_sems[-1]

        def stage(function):
            m.stage_sems = []
            function(nc, m, io)
            nc.clear_and_free_semaphores(m.stage_sems)
            nc.all_engine_barrier()

        m.sem = sem
        alloc = lambda name, shape, dt=F32: ctx.enter_context(nc.sbuf_tensor(name, shape, dt))
        m.raw = alloc("raw", [P, 2, PANEL])
        m.whi = [alloc(f"whi{s}", [P, PANEL], F32R) for s in range(2)]
        m.wlo = [alloc(f"wlo{s}", [P, PANEL], F32R) for s in range(2)]
        m.raw_landed, m.w_hi, m.w_lo, m.w_used = [m.sem("raw_landed0"), m.sem("raw_landed1")], m.sem("w_hi"), m.sem("w_lo"), m.sem("w_used")
        m.parts_landed = [m.sem("parts_landed0"), m.sem("parts_landed1")]
        m.const = alloc("const", [P, NCONST])
        m.ident = m.const[:, K_ID:K_ID + P]
        m.rows, m.cols, m.ones = alloc("rows", [P, P]), alloc("cols", [P, P]), alloc("ones", [P, P])
        m.bif, m.csil = alloc("bif", [P, 2]), alloc("csil", [P, KT])
        m.stat, m.neghalf = alloc("stat", [P, 4 * TT]), alloc("neghalf", [P, 4 * TT])
        m.aff = alloc("aff", [P, 2 * KT])
        m.ps = ctx.enter_context(nc.psum_tensor("ps", [P, 8 * BANK], F32))
        with ExitStack() as early:
            tmp = lambda name, shape: early.enter_context(nc.sbuf_tensor(name, shape, F32))
            m.xs, m.ada_raw, m.ada_acc = tmp("xs", [P, TT, D]), tmp("ada_raw", [P, 4, ADA1]), tmp("ada_acc", [P, ADA1])
        with ExitStack() as heads:
            tmp = lambda name, shape: heads.enter_context(nc.sbuf_tensor(name, shape, F32))
            m.qk = tmp("qk", [P, 2 * MH, S])
            with ExitStack() as lats:
                m.lat = lats.enter_context(nc.sbuf_tensor("lat", [P, 4, S], F32))
                with ExitStack() as inner:
                    tmp = lambda name, shape: inner.enter_context(nc.sbuf_tensor(name, shape, F32))
                    m.vaug, m.osig = tmp("vaug", [P, TT, MH, VA]), tmp("osig", [P, MH, S])
                    stage(stage_project)
                    if upto == 1:
                        return m
                    stage(stage_mlstm)
                if upto == 2:
                    return m
                with ExitStack() as inner:
                    alloc_attention(nc, m, inner)
                    stage(stage_latents)
                    if upto == 3:
                        return m
                    stage(stage_attention)
                if upto == 4:
                    return m
            m.y = ctx.enter_context(nc.sbuf_tensor("y", [P, KT, S], F32, side="right"))
            stage(stage_branches)
            if upto == 5:
                return m
        stage(stage_out)
        if upto == 6:
            return m
        m.hidden = ctx.enter_context(nc.sbuf_tensor("hidden", [P, FA, S], F32, side="right"))
        with ExitStack() as inner:
            m.u2hi = inner.enter_context(nc.sbuf_tensor("u2hi", [P, KT, S], F32R))
            m.u2lo = inner.enter_context(nc.sbuf_tensor("u2lo", [P, KT, S], F32R))
            stage(stage_hidden)
        if upto == 7:
            return m
        stage(stage_final)
        return m


def build(nc, args, out, upto=9):
    io = Record()
    flat = lambda name, n: args[name].rearrange("a (r c) -> (a r) c", c=P)
    io.rows = [("c", flat("c", 0))] + [(n, flat(n, 0)) for n in ("b_ada", "g_mix", "g_ffn")] + [
        ("conv_w", args["conv_w"].rearrange("a j (r c) -> (a j r) c", c=P))] + [
        (n, flat(n, 0)) for n in ("conv_b", "g_mhead", "g_q_lat", "g_kv_lat")]
    io.const = args["constants"]
    io.b_igate, io.b_fgate = (args[n].rearrange("a (h o) -> (a h) o", o=1) for n in ("b_igate", "b_fgate"))
    (io.x, io.w_ada, io.w_in, io.w_uq, io.w_ukv, io.w_branch_m, io.w_branch_a, io.w_out, io.w_ffn_in, io.w_ffn_out) = (
        args[n].rearrange("a b c -> (a b) c")
        for n in ("x", "w_ada", "w_in", "w_uq", "w_ukv", "w_branch_m", "w_branch_a", "w_out", "w_ffn_in", "w_ffn_out"))
    io.gates = nc.dram_tensor("gates", [2 * KT, P, S], F32, kind="Internal").ap()

    def branch_panel(m, j, s):
        return [(kn(m.raw[:, s, :], MH), cols_of((io.w_branch_m, io.w_branch_a)[s], j * BANK, BANK))]

    io.branch_panel = branch_panel

    def ffn_panel(m, s, n):
        return [(kn(m.raw[:, s, :])[:, :, a * P:(a + 1) * P], cols_of(io.w_ffn_in, n * P + a * FF, P)) for a in range(2)]

    def ffn_out_panel(m, s, n):
        return kn(m.raw[:, s, :], 2), io.w_ffn_out[bass.ds(n * (2 * P), 2 * P), :].rearrange("(k p) c -> p k c", p=P)

    io.ffn_panel, io.ffn_out_panel = ffn_panel, ffn_out_panel
    io.ada_acc = nc.dram_tensor("ada_sums", [P, 4 * D], F32, kind="Internal").ap()
    io.gt2 = nc.dram_tensor("gt2_sums", [1, D], F32, kind="Internal").ap()
    io.h = nc.dram_tensor("h_mid", [S, D], F32, kind="Internal").ap()
    io.b_ada = args["b_ada"]
    io.positions, io.g_final = args["positions"], args["g_final"].rearrange("(o n) -> o n", o=1)
    io.out = out.rearrange("a b c -> (a b) c")
    return program(nc, io, upto)


_INS = ["x", "c", "positions", "w_ada", "b_ada", "g_mix", "w_in", "conv_w", "conv_b", "b_igate", "b_fgate", "g_mhead",
        "g_q_lat", "w_uq", "g_kv_lat", "w_ukv", "w_branch_m", "w_branch_a", "w_out", "g_ffn", "w_ffn_in", "w_ffn_out",
        "g_final"]


def kernel(**inputs):
    import numpy as _np
    import concourse.bacc as _bacc
    from concourse import mybir as _mybir
    from concourse.bass_utils import run_bass_kernel_spmd as _run

    nc = _bacc.Bacc("TRN2", target_bir_lowering=False, num_devices=1)
    given = {name: _np.ascontiguousarray(inputs[name]) for name in _INS}
    given["constants"] = constants()
    arrays = {f"in_{name}_dram": a for name, a in given.items()}
    args = {name: nc.dram_tensor(f"in_{name}_dram", a.shape, _mybir.dt.from_np(a.dtype), kind="ExternalInput").ap()
            for name, a in given.items()}
    out = nc.dram_tensor("out_0_dram", (1, S, D), F32, kind="ExternalOutput").ap()
    build(nc, args, out)
    r = _run(nc, [arrays], core_ids=[0])
    return r.results[0]["out_0_dram"]
```
